# Optimizing a Trainium2 kernel written in Bass

```python
import math
import jax, jax.numpy as jnp
from jax import lax
import numpy as np

D_MODEL = 1024
BATCH = 1
SEQ = 256
DEPTH = 2

EPS = 1e-6
A_HEADS = 4
A_DK = 128
A_DV = 128
A_CONV = 4
A_CHUNK = 64
A_W = A_HEADS * A_DK
B_HEADS = 4
B_DK = 128
B_DV = 128
B_CHUNK = 64
B_W = B_HEADS * B_DK
C_PAIRS = ((128, 1), (512, 4), (2048, 16))
C_GROUPS = 3
C_HEADS = 4
C_DH = 128
C_BLOCK = 128
C_W = C_HEADS * C_DH
REL_BUCKETS = 32
REL_MAX_DIST = 2048
D_FF = 2816
N_EXPERTS = 8
TOP_K = 2
D_FF_EXPERT = 3584
IN_SPLITS = (3 * A_W, A_HEADS, A_HEADS, A_HEADS * A_DV,
             B_W, B_W, B_HEADS * B_DV, B_HEADS * B_DV,
             3 * C_GROUPS * C_W,
             3 * D_MODEL)
D_IN = 3 * A_W + 2 * A_HEADS + A_HEADS * A_DV + 2 * B_W + 2 * B_HEADS * B_DV + 3 * C_GROUPS * C_W + 3 * D_MODEL

kernel_name = "hybrid_deltanet_hgrn2_dilated_moe"

def rms_norm(x, g):
    xf = x.astype(jnp.float32)
    y = xf * lax.rsqrt(jnp.mean(xf * xf, axis=-1, keepdims=True) + EPS)
    return (y * g.astype(jnp.float32)).astype(x.dtype)

def l2norm(x):
    return x * lax.rsqrt(jnp.sum(x * x, axis=-1, keepdims=True) + EPS)

def causal_conv(x, w):
    K, C = w.shape
    return lax.conv_general_dilated(x, w[:, None, :].astype(x.dtype), window_strides=(1,),
                                    padding=((K - 1, 0),), dimension_numbers=('NWC', 'WIO', 'NWC'),
                                    feature_group_count=C)

def to_chunks(t, C):
    B_, T = t.shape[:2]
    t = t.reshape(B_, T // C, C, *t.shape[2:])
    return jnp.moveaxis(t, 3, 1)

def gated_deltanet(qkv, beta_logit, alpha_logit, gate, conv_w, a_log, dt_bias, norm_g):
    f32 = jnp.float32
    B_, T, _ = qkv.shape
    C = A_CHUNK
    qkv = jax.nn.silu(causal_conv(qkv, conv_w)).astype(f32)
    q, k, v = jnp.split(qkv, 3, axis=-1)
    q = l2norm(q.reshape(B_, T, A_HEADS, A_DK)) * (A_DK ** -0.5)
    k = l2norm(k.reshape(B_, T, A_HEADS, A_DK))
    v = v.reshape(B_, T, A_HEADS, A_DV)
    beta = jax.nn.sigmoid(beta_logit.astype(f32))
    g = -jnp.exp(a_log.astype(f32)) * jax.nn.softplus(alpha_logit.astype(f32) + dt_bias.astype(f32))
    qc, kc, vc = to_chunks(q, C), to_chunks(k, C), to_chunks(v, C)
    bc = to_chunks(beta, C)
    gc = jnp.cumsum(to_chunks(g, C), axis=-1)
    incl = jnp.tril(jnp.ones((C, C), bool))
    strict = jnp.tril(jnp.ones((C, C), bool), -1)
    decay = jnp.exp(jnp.where(incl, gc[..., :, None] - gc[..., None, :], -jnp.inf))
    kb = kc * bc[..., None]
    m = jnp.einsum('bhnid,bhnjd->bhnij', kb, kc) * jnp.where(strict, decay, 0.0)
    tmat = m + jnp.eye(C, dtype=f32)
    rhs = jnp.concatenate([vc * bc[..., None], kb * jnp.exp(gc)[..., None]], axis=-1)
    sol = lax.linalg.triangular_solve(tmat, rhs, left_side=True, lower=True, unit_diagonal=True)
    u, w = sol[..., :A_DV], sol[..., A_DV:]
    attn = jnp.einsum('bhnid,bhnjd->bhnij', qc, kc) * decay
    qg = qc * jnp.exp(gc)[..., None]
    kg = kc * jnp.exp(gc[..., -1:] - gc)[..., None]
    gl = jnp.exp(gc[..., -1])
    xs = tuple(jnp.moveaxis(t, 2, 0) for t in (qg, kg, u, w, attn, gl))

    def step(S, inp):
        qg_n, kg_n, u_n, w_n, attn_n, gl_n = inp
        v_new = u_n - jnp.einsum('bhcd,bhde->bhce', w_n, S)
        o = jnp.einsum('bhcd,bhde->bhce', qg_n, S) + jnp.einsum('bhij,bhje->bhie', attn_n, v_new)
        S = S * gl_n[..., None, None] + jnp.einsum('bhcd,bhce->bhde', kg_n, v_new)
        return S, o

    S0 = jnp.zeros((B_, A_HEADS, A_DK, A_DV), f32)
    _, o = lax.scan(step, S0, xs)
    o = o.transpose(1, 0, 3, 2, 4).reshape(B_, T, A_HEADS, A_DV)
    o = rms_norm(o, norm_g) * jax.nn.silu(gate.astype(f32).reshape(B_, T, A_HEADS, A_DV))
    return o.reshape(B_, T, A_HEADS * A_DV)

def hgrn2(q, f_logit, i_in, gate, lb, norm_g):
    f32 = jnp.float32
    B_, T, _ = q.shape
    C = B_CHUNK
    q = jax.nn.silu(q.astype(f32))
    f = lb.astype(f32) + (1.0 - lb.astype(f32)) * jax.nn.sigmoid(f_logit.astype(f32))
    k = 1.0 - f
    g = jnp.log(f)
    qc = to_chunks(q.reshape(B_, T, B_HEADS, B_DK), C)
    kc = to_chunks(k.reshape(B_, T, B_HEADS, B_DK), C)
    vc = to_chunks(i_in.astype(f32).reshape(B_, T, B_HEADS, B_DV), C)
    gc = jnp.cumsum(to_chunks(g.reshape(B_, T, B_HEADS, B_DK), C), axis=3)
    incl = jnp.tril(jnp.ones((C, C), bool))
    qg = qc * jnp.exp(gc)
    kg = kc * jnp.exp(gc[..., -1:, :] - gc)
    gl = jnp.exp(gc[..., -1, :])
    xs = tuple(jnp.moveaxis(t, 2, 0) for t in (qc, kc, vc, gc, qg, kg, gl))

    def step(S, inp):
        q_n, k_n, v_n, g_n, qg_n, kg_n, gl_n = inp
        rel = jnp.exp(jnp.where(incl[:, :, None], g_n[:, :, :, None, :] - g_n[:, :, None, :, :], -jnp.inf))
        attn = jnp.einsum('bhijd,bhjd->bhij', q_n[:, :, :, None, :] * rel, k_n)
        o = jnp.einsum('bhid,bhde->bhie', qg_n, S) + jnp.einsum('bhij,bhje->bhie', attn, v_n)
        S = S * gl_n[..., None] + jnp.einsum('bhjd,bhje->bhde', kg_n, v_n)
        return S, o

    S0 = jnp.zeros((B_, B_HEADS, B_DK, B_DV), f32)
    _, o = lax.scan(step, S0, xs)
    o = o.transpose(1, 0, 3, 2, 4).reshape(B_, T, B_HEADS, B_DV)
    o = rms_norm(o, norm_g) * jax.nn.sigmoid(gate.astype(f32).reshape(B_, T, B_HEADS, B_DV))
    return o.reshape(B_, T, B_HEADS * B_DV)

def t5_bucket(n):
    max_exact = REL_BUCKETS // 2
    nf = jnp.maximum(n, 1).astype(jnp.float32)
    large = max_exact + (jnp.log(nf / max_exact) / math.log(REL_MAX_DIST / max_exact)
                         * (REL_BUCKETS - max_exact)).astype(jnp.int32)
    large = jnp.minimum(large, REL_BUCKETS - 1)
    return jnp.where(n < max_exact, n, large)

def dilated_group(q, k, v, table, window, dil):
    f32 = jnp.float32
    B_, T, H, D = q.shape
    span = window // dil
    L = T // dil
    nb = -(-L // C_BLOCK)
    Lp = nb * C_BLOCK

    def strided(t):
        t = t.reshape(B_, L, dil, H, D).transpose(0, 2, 3, 1, 4)
        t = jnp.pad(t, ((0, 0), (0, 0), (0, 0), (0, Lp - L), (0, 0)))
        return t.reshape(B_, dil, H, nb, C_BLOCK, D)

    def with_prev(t):
        prev = jnp.pad(t, ((0, 0), (0, 0), (0, 0), (1, 0), (0, 0), (0, 0)))[:, :, :, :-1]
        return jnp.concatenate([prev, t], axis=4)

    qb = strided(q)
    kb = with_prev(strided(k))
    vb = with_prev(strided(v))
    qi = jnp.arange(C_BLOCK)[:, None]
    kj = jnp.arange(2 * C_BLOCK)[None, :]
    dist = qi + C_BLOCK - kj
    blk = jnp.arange(nb)[:, None, None]
    valid = (dist >= 0) & (dist <= span) & (blk * C_BLOCK + kj - C_BLOCK >= 0)
    bias = table[t5_bucket(jnp.maximum(dist, 0) * dil)].transpose(2, 0, 1).astype(f32)
    s = jnp.einsum('brhnqd,brhnkd->brhnqk', qb, kb).astype(f32) * (D ** -0.5) + bias[:, None]
    s = jnp.where(valid, s, -jnp.inf)
    mx = jnp.max(s, axis=-1, keepdims=True)
    p = jnp.exp(s - mx)
    den = jnp.sum(p, axis=-1, keepdims=True)
    o = jnp.einsum('brhnqk,brhnkd->brhnqd', p, vb.astype(f32)) / den
    lse = (mx + jnp.log(den))[..., 0]

    def back(t):
        t = t.reshape(B_, dil, H, Lp, *t.shape[5:])[:, :, :, :L]
        t = jnp.moveaxis(t, 3, 1)
        return t.reshape(B_, T, H, *t.shape[4:])

    return back(o), back(lse)

def dilated_attention(qkv, q_gain, k_gain, rel_table):
    B_, T, _ = qkv.shape
    qkv = qkv.reshape(B_, T, 3, C_GROUPS, C_HEADS, C_DH)
    q = rms_norm(qkv[:, :, 0], q_gain[:, None, :])
    k = rms_norm(qkv[:, :, 1], k_gain[:, None, :])
    v = qkv[:, :, 2]
    outs, lses = [], []
    for gi, (window, dil) in enumerate(C_PAIRS):
        o, lse = dilated_group(q[:, :, gi], k[:, :, gi], v[:, :, gi],
                               rel_table[:, gi * C_HEADS:(gi + 1) * C_HEADS], window, dil)
        outs.append(o)
        lses.append(lse)
    wts = jax.nn.softmax(jnp.stack(lses, 0), axis=0)
    o = jnp.sum(wts[..., None] * jnp.stack(outs, 0), axis=0)
    return o.reshape(B_, T, C_W)

def swiglu(h, w1, w3, w2):
    return (jax.nn.silu(h @ w1) * (h @ w3)) @ w2

def moe_swiglu(h, w_router, w1, w3, w2):
    logits = (h @ w_router).astype(jnp.float32)
    top_val, top_idx = lax.top_k(logits, TOP_K)
    probs = jax.nn.softmax(top_val, axis=-1)
    combine = jnp.sum(jax.nn.one_hot(top_idx, N_EXPERTS, dtype=jnp.float32) * probs[..., None], axis=-2)
    combine = combine.astype(h.dtype)
    out = jnp.zeros_like(h)
    for e in range(N_EXPERTS):
        out = out + combine[..., e:e + 1] * swiglu(h, w1[e], w3[e], w2[e])
    return out

def setup_inputs(seed: int = 0) -> dict:
    key = jax.random.key(seed)
    ks = jax.random.split(key, 26)
    f32 = jnp.float32
    n_dense = (DEPTH + 1) // 2
    n_moe = DEPTH // 2

    def nrm(k, shape, fan_in):
        return jax.random.normal(k, shape, f32) * (fan_in ** -0.5)

    def gain(k, shape):
        return 1.0 + 0.02 * jax.random.normal(k, shape, f32)

    dt = jnp.exp(jax.random.uniform(ks[5], (DEPTH, A_HEADS), f32, math.log(0.001), math.log(0.1)))
    return {
        "x": jax.random.normal(ks[0], (BATCH, SEQ, D_MODEL), f32),
        "w_in": nrm(ks[1], (DEPTH, D_MODEL, D_IN), D_MODEL),
        "norm_mix": gain(ks[2], (DEPTH, D_MODEL)),
        "conv_a": nrm(ks[3], (DEPTH, A_CONV, 3 * A_W), A_CONV),
        "a_log": jnp.log(jax.random.uniform(ks[4], (DEPTH, A_HEADS), f32, 1.0, 16.0)),
        "dt_bias": dt + jnp.log(-jnp.expm1(-dt)),
        "gnorm_a": gain(ks[6], (DEPTH, A_DV)),
        "lb_logits": jax.random.normal(ks[7], (DEPTH, B_W), f32),
        "gnorm_b": gain(ks[8], (DEPTH, B_DV)),
        "qnorm_c": gain(ks[9], (DEPTH, C_GROUPS, C_DH)),
        "knorm_c": gain(ks[10], (DEPTH, C_GROUPS, C_DH)),
        "rel_bias": 0.2 * jax.random.normal(ks[11], (REL_BUCKETS, C_GROUPS * C_HEADS), f32),
        "w_br_a": nrm(ks[12], (DEPTH, A_HEADS * A_DV, D_MODEL), A_HEADS * A_DV),
        "w_br_b": nrm(ks[13], (DEPTH, B_HEADS * B_DV, D_MODEL), B_HEADS * B_DV),
        "w_br_c": nrm(ks[14], (DEPTH, C_W, D_MODEL), C_W),
        "w_out": nrm(ks[15], (DEPTH, D_MODEL, D_MODEL), D_MODEL),
        "norm_ffn": gain(ks[16], (DEPTH, D_MODEL)),
        "ffn_w1": nrm(ks[17], (n_dense, D_MODEL, D_FF), D_MODEL),
        "ffn_w3": nrm(ks[18], (n_dense, D_MODEL, D_FF), D_MODEL),
        "ffn_w2": nrm(ks[19], (n_dense, D_FF, D_MODEL), D_FF),
        "router": nrm(ks[20], (n_moe, D_MODEL, N_EXPERTS), D_MODEL),
        "moe_w1": nrm(ks[21], (n_moe, N_EXPERTS, D_MODEL, D_FF_EXPERT), D_MODEL),
        "moe_w3": nrm(ks[22], (n_moe, N_EXPERTS, D_MODEL, D_FF_EXPERT), D_MODEL),
        "moe_w2": nrm(ks[23], (n_moe, N_EXPERTS, D_FF_EXPERT, D_MODEL), D_FF_EXPERT),
    }

def reference(x, w_in, norm_mix, conv_a, a_log, dt_bias, gnorm_a, lb_logits, gnorm_b,
              qnorm_c, knorm_c, rel_bias, w_br_a, w_br_b, w_br_c, w_out, norm_ffn,
              ffn_w1, ffn_w3, ffn_w2, router, moe_w1, moe_w3, moe_w2):
    B_, T, _ = x.shape
    p_lb = jax.nn.softmax(lb_logits.astype(jnp.float32), axis=0)
    lower_bounds = jnp.cumsum(p_lb, axis=0) - p_lb[0:1]
    offsets = np.cumsum(IN_SPLITS)[:-1].tolist()
    for layer in range(DEPTH):
        h = rms_norm(x, norm_mix[layer])
        proj = h @ w_in[layer]
        (a_qkv, a_beta, a_alpha, a_gate, b_q, b_f, b_i, b_gate, c_qkv, br_gate) = jnp.split(proj, offsets, axis=-1)
        o_a = gated_deltanet(a_qkv, a_beta, a_alpha, a_gate, conv_a[layer], a_log[layer],
                             dt_bias[layer], gnorm_a[layer]).astype(x.dtype)
        o_b = hgrn2(b_q, b_f, b_i, b_gate, lower_bounds[layer], gnorm_b[layer]).astype(x.dtype)
        o_c = dilated_attention(c_qkv, qnorm_c[layer], knorm_c[layer], rel_bias).astype(x.dtype)
        gates = jax.nn.sigmoid(br_gate.reshape(B_, T, 3, D_MODEL))
        mix = (gates[:, :, 0] * (o_a @ w_br_a[layer])
               + gates[:, :, 1] * (o_b @ w_br_b[layer])
               + gates[:, :, 2] * (o_c @ w_br_c[layer]))
        x = x + mix @ w_out[layer]
        h = rms_norm(x, norm_ffn[layer])
        if layer % 2 == 0:
            li = layer // 2
            x = x + swiglu(h, ffn_w1[li], ffn_w3[li], ffn_w2[li])
        else:
            li = layer // 2
            x = x + moe_swiglu(h, router[li], moe_w1[li], moe_w3[li], moe_w2[li])
    return x


_drawn_inputs = setup_inputs


def setup_inputs(seed=0):
    import zlib

    import numpy as np

    out = dict(_drawn_inputs(seed))
    spreads = {}
    factors = {'gnorm_b': 3.368, 'qnorm_c': 8.0, 'knorm_c': 8.0, 'gnorm_a': 3.386, 'rel_bias': 3.654}
    for name, (base, spread) in spreads.items():
        noise = np.random.default_rng([zlib.crc32(name.encode()), seed]).standard_normal(out[name].shape)
        drawn = base * np.exp(spread * noise) if base else spread * noise
        out[name] = __import__('jax').numpy.asarray(drawn.astype(out[name].dtype))
    for name, factor in factors.items():
        out[name] = (out[name] * factor).astype(out[name].dtype)
    return out
```

```python
import math
from contextlib import ExitStack, contextmanager

import concourse.bass as bass
import numpy as np
from concourse import mybir

F32 = mybir.dt.float32
F32R = mybir.dt.float32r
I32 = mybir.dt.int32
ALU = mybir.AluOpType
ACT = mybir.ActivationFunctionType
AX = mybir.AxisListType

P = 128
T = 256
TT = T // P
D = 1024
KT = D // P
DEPTH = 2
EPS = 1e-6
H = 4
W = H * P
TAPS = 4
CT = 3 * H
GROUPS = 3
DILATION = (1, 4, 16)
SPAN = 128
BUCKETS, MAX_DIST = 32, 2048
E = 8
FF, FFE = 2816, 3584
SUB = 256
UE = 2048

C_QKV = 0
C_AB = 3 * W
C_AGATE = C_AB + 2 * H
C_BQ = C_AGATE + W
C_CQKV = C_BQ + 4 * W
C_BR = C_CQKV + 9 * W
NEG = -1e30

RAW = 6
SPLIT = 2
U_A, U_AG, U_B, U_C, U_BR, U_OUT, U_FF = 0, 6, 8, 16, 34, 52, 56
PAIRS = FF // (2 * SUB)
U_DENSE = 3 * (FF // SUB)
LAYER_U = (0, U_FF + U_DENSE)
U_END = LAYER_U[1] + U_FF
EXPERT_PAIRS = FFE // (2 * SUB)
STEPS_DENSE = FF // SUB
N_ROW_LOADS = 6
EXPERT_R = EXPERT_PAIRS
G_N = 31

K_ID, K_LE, K_GT, K_M0, K_MT, K_FLIP, K_N = 0, 1, 2, 3, 4, 11, 12
LEVELS = 7
R_CONV, R_LB, R_GA, R_GB, R_QN, R_KN, R_N = 0, 96, 104, 106, 108, 114, 120
DIST = 384


def shape_constants():
    i, j = np.arange(P)[:, None], np.arange(P)[None, :]
    tiles = [i == j, i <= j, i > j, (i // 2 == j // 2) & (i > j)]
    for n in range(LEVELS):
        s = 1 << n
        tiles.append((i // (2 * s) == j // (2 * s)) & (j % (2 * s) >= s) & (i % (2 * s) < s))
    tiles.append(i + j == P - 1)
    masks = np.stack([t.astype(np.float32) for t in tiles], 1)
    buckets = np.zeros((BUCKETS + 1, GROUPS, DIST), np.float32)
    exact = BUCKETS // 2
    for g, dil in enumerate(DILATION):
        for z in range(DIST):
            dist = T - 1 - z
            if dist < 0 or dist % dil or dist // dil > SPAN:
                buckets[BUCKETS, g, z] = NEG
                continue
            b = dist
            if dist >= exact:
                big = np.log(np.float32(dist) / np.float32(exact)) / np.float32(math.log(MAX_DIST / exact))
                b = min(exact + int(np.float32(big) * np.float32(BUCKETS - exact)), BUCKETS - 1)
            buckets[b, g, z] = 1.0
    return masks, buckets


class Signal:

    def __init__(self, ctx, nc, name, per_layer=1, ahead=0):
        self.sem = ctx.enter_context(nc.semaphore(name))
        self.per_layer, self.ahead = per_layer, ahead

    def at(self, layer, k=0):
        return self.ahead + layer * self.per_layer + k + 1

    def count(self, n):
        return n + self.ahead


class Program:

    def __init__(self, own):
        self.own = own
        self.n, self.turn = 0, None
        self.u, self.rounds = 0, None

    def step(self):
        self.n += 1
        return self.n if self.turn is None else self.n + self.turn

    def unit(self, k=0, each=1):
        n = (self.u + k) * each
        return n if self.rounds is None else n + self.rounds * (6 * each)

    @contextmanager
    def loop(self, eng, trips, steps, rounds=1):
        with eng.Fori(0, trips) as i:
            n, u, turn, r = self.n, self.u, self.turn, self.rounds
            self.turn = i * steps if turn is None else turn + i * steps
            self.rounds = i * rounds if r is None else r + i * rounds
            yield i
            assert self.n - n == steps, f"{self.n - n} steps in a turn, not {steps}"
            assert self.u - u == 6 * rounds, f"{self.u - u} units in a turn"
            self.turn, self.rounds = turn, r
        self.n, self.u = n + trips * steps, u + trips * 6 * rounds


def build(ctx, nc, dram):
    cursor = nc.sbuf_base + (-nc.sbuf_base) % 64

    def sb(name, shape, dtype=F32, at=None):
        nonlocal cursor
        size = int(np.prod(shape[1:])) * 4
        size += (-size) % 64
        if at is None:
            at, cursor = cursor, cursor + size
        assert at + size <= nc.sbuf_usable_end, (name, at + size - nc.sbuf_usable_end)
        return nc.alloc_sbuf_tensor_at(name, shape, dtype, offset=at)

    raw = [sb(f"raw{s}", [P, UE]) for s in range(RAW)]
    hi = [sb(f"hi{s}", [P, UE], F32R) for s in range(SPLIT)]
    lo = [sb(f"lo{s}", [P, UE], F32R) for s in range(SPLIT)]
    x = sb("x", [P, TT, D])
    ones_t = sb("ones_t", [P, P])
    actT_hi = sb("actT_hi", [P, KT, T], F32R)
    actT_lo = sb("actT_lo", [P, KT, T], F32R)
    consts = sb("consts", [P, K_N, P])
    bias = sb("bias", [P, GROUPS * H, T])
    small = sb("small", [P, R_N])
    ab = sb("ab", [P, 3, KT, 8])
    ab_hi = sb("ab_hi", [P, 3, KT, 8], F32R)
    ab_lo = sb("ab_lo", [P, 3, KT, 8], F32R)
    a_par = sb("a_par", [P, 2, DEPTH, H])
    a_rate = sb("a_rate", [P, DEPTH, H])
    lb = sb("lb", [P, 8, H])
    tiny = sb("tiny", [P, 8])
    stat = sb("stat", [P, 16])
    ident, le, gt = consts[:, K_ID, :], consts[:, K_LE, :], consts[:, K_GT, :]
    eps_t, one_t, lnq_t, zero_t = (tiny[:, n:n + 1] for n in range(4))

    u0 = cursor
    a_in = sb("a_in", [P, CT, 3 + T])
    u1 = cursor
    a_act = sb("a_act", [P, CT, T])
    b_q = sb("b_q", [P, H, T])
    b_f = sb("b_f", [P, H, T])
    oT = sb("oT", [P, 3, H, T])
    c0 = cursor
    cursor = c0 + 36 * 1024
    a_s = sb("a_s", [P, 20, TT * H])
    a_gate = sb("a_gate", [P, TT, W], at=u0)
    b_i = sb("b_i", [P, TT, W], at=u0 + 4096)
    b_gate = sb("b_gate", [P, TT, W], at=u0 + 8192)
    gain = sb("gain", [P, D], at=u1)
    b_gc = sb("b_gc", [P, H, T], at=u1)
    b_qe = sb("b_qe", [P, H, T], at=u1 + 4096)
    b_ke = sb("b_ke", [P, H, T], at=u1 + 8192)
    hn = sb("hn", [P, TT, D], at=c0)
    S8 = [P, TT, H, P]
    k_nat, v_nat, attn, t_m, t_n, t_x, t_y, t_w, t_v = (
        sb(name, S8, at=c0 + 4096 * n)
        for n, name in enumerate(("k_nat", "v_nat", "attn", "t_m", "t_n", "t_x", "t_y", "t_w", "t_v")))
    b_attn = sb("b_attn", [P, 3, H, P], at=c0)
    b_e = sb("b_e", [P, H, T], at=c0 + 6144)
    b_o = sb("b_o", [P, TT, W], at=c0 + 10240)
    b_o2 = sb("b_o2", [P, TT, W], at=c0 + 14336)
    b_k = sb("b_k", [P, H, T], at=c0 + 18432)
    c_qT = sb("c_qT", [P, GROUPS * H, T], at=c0)
    c_kT = sb("c_kT", [P, GROUPS * H, T], at=c0 + 12288)
    c_v = sb("c_v", [P, TT, GROUPS, W], at=c0 + 24576)
    c_sq = sb("c_sq", [P, TT, W], at=u0)
    c_n = sb("c_n", [P, TT, W], at=u0 + 4096)
    c_s = sb("c_s", [P, GROUPS * T], at=u0 + 8192)
    c_p = sb("c_p", [P, GROUPS * T], at=u0 + 11264)
    c_pT = sb("c_pT", [P, 2 * GROUPS * P], at=u0 + 14336)
    c_o = sb("c_o", [P, TT, W], at=u0 + 17408)
    g_sig = sb("g_sig", [P, TT, W], at=c0)
    g_prod = sb("g_prod", [P, TT, W], at=c0 + 4096)
    mix = sb("mix", [P, TT, D], at=c0 + 8192)
    o_hi = sb("o_hi", [P, H, T], F32R, at=c0 + 16384)
    o_lo = sb("o_lo", [P, H, T], F32R, at=c0 + 20480)
    rows = sb("rows", [P, P], at=u0)
    picks = sb("picks", [BUCKETS + 1, GROUPS, DIST], at=u0 + 512)
    table = sb("table", [BUCKETS + 1, GROUPS * H], at=u0 + 512 + 4608)
    by_dist = sb("by_dist", [H, GROUPS, DIST], at=u1 + 12288)
    hankel = sb("hankel", [P, GROUPS * H, T], at=u1 + 12288 + 8192)

    cursor = u0
    fn = sb("fn", [P, TT, D])
    f_gain = sb("f_gain", [P, D])
    f_s = [sb(f"f_s{s}", [P, 512]) for s in range(2)]
    f_g = [sb(f"f_g{s}", [P, 512]) for s in range(2)]
    fT_hi = [sb(f"fT_hi{s}", [P, 2, T], F32R) for s in range(2)]
    fT_lo = [sb(f"fT_lo{s}", [P, 2, T], F32R) for s in range(2)]
    zero = sb("zero", [P, 512], F32R)
    zero_f = sb("zero_f", [P, 512])
    r_t = sb("r_t", [P, 20, TT * E])
    r_flag = sb("r_flag", [P, 2], I32)
    slots = sb("slots", [P, 2 * P])
    slots_i = sb("slots_i", [P, 2 * P], I32)
    fn_hi = sb("fn_hi", [P, TT, D], F32R)
    fn_lo = sb("fn_lo", [P, TT, D], F32R)
    pick = sb("pick", [P, TT, P])
    pick_r = sb("pick_r", [P, TT, P], F32R)
    pickT = sb("pickT", [P, TT, P], F32R)
    e_hi = sb("e_hi", [P, KT, P], F32R)
    e_lo = sb("e_lo", [P, KT, P], F32R)
    y_hi = sb("y_hi", [P, D], F32R)
    y_lo = sb("y_lo", [P, D], F32R)

    PS = ctx.enter_context(nc.psum_tensor("PS", [P, 8, 512], F32))
    hankel_dram = nc.dram_tensor("hankel_dram", (GROUPS * H, DIST), F32, kind="Internal").ap()

    def signal(name, per_layer=1, ahead=0):
        return Signal(ctx, nc, name, per_layer, ahead)

    raw_full = [signal(f"raw_full{s}") for s in range(RAW)]
    hi_made = signal("hi_made")
    lo_made = signal("lo_made")
    unit_used = signal("unit_used")
    act_step = signal("act_step")
    dve_step = signal("dve_step")
    x_here = signal("x_here")
    consts_here = signal("consts_here")
    rows_here = signal("rows_here")
    table_here = signal("table_here")
    ab_here = signal("ab_here")
    par_here = signal("par_here")
    rows_T = signal("rows_T")
    rows_kept = signal("rows_kept")
    by_dist_done = signal("by_dist_done")
    by_dist_kept = signal("by_dist_kept")
    by_dist_out = signal("by_dist_out")
    hankel_here = signal("hankel_here")
    bias_done = signal("bias_done")
    bias_kept = signal("bias_kept")
    ab_split = signal("ab_split")
    lb_m = signal("lb_m")
    lb_e = signal("lb_e")
    a_rate_e = signal("a_rate_e")
    tiny_made = signal("tiny_made")
    gain_here = signal("gain_here")
    norm_r = signal("norm_r", 2)
    norm_made = signal("norm_made", 4)
    turned = signal("turned", 12)
    actT_hi_made = signal("actT_hi_made", 12)
    actT_lo_made = signal("actT_lo_made", 12)
    x_made = signal("x_made", 3)
    a_raw = signal("a_raw", 6)
    pad_made = signal("pad_made")
    a_conv = signal("a_conv", 3)
    a_tanh = signal("a_tanh", 3)
    a_silu = signal("a_silu", 3)
    ab_done = signal("ab_done")
    ab_read = signal("ab_read")
    a_e1 = signal("a_e1")
    a_e2 = signal("a_e2")
    a_g = signal("a_g")
    a_cum = signal("a_cum")
    a_cum_e = signal("a_cum_e")
    gate_tanh = signal("gate_tanh", 3)
    gate_made = signal("gate_made", 4)
    a_fwd = signal("a_fwd", 6)
    a_sq = signal("a_sq", 4)
    a_v = signal("a_v", 2)
    a_ss = signal("a_ss")
    a_r = signal("a_r")
    a_qn = signal("a_qn", 2)
    a_kn = signal("a_kn", 2)
    a_back = signal("a_back", 4)
    a_T = signal("a_T", 4)
    a_seg = signal("a_seg", 2)
    a_dec = signal("a_dec", 4)
    a_exp = signal("a_exp", 4)
    a_kk = signal("a_kk", 4)
    a_M = signal("a_M", 2)
    a_attn = signal("a_attn", 2)
    a_N = signal("a_N", 2)
    a_Nc = signal("a_Nc", 2)
    a_X = signal("a_X", 11)
    a_Y = signal("a_Y", 13)
    a_No = signal("a_No", 6)
    a_P = signal("a_P", 12)
    a_Pc = signal("a_Pc", 12)
    a_XP = signal("a_XP", 10)
    a_YP = signal("a_YP", 12)
    a_r0 = signal("a_r0")
    a_kg = signal("a_kg")
    a_vn = signal("a_vn", 2)
    a_vc = signal("a_vc", 2)
    a_S = signal("a_S")
    a_Sc = signal("a_Sc")
    a_kS = signal("a_kS")
    a_qS = signal("a_qS")
    a_r1 = signal("a_r1")
    a_o = signal("a_o", 2)
    a_oc = signal("a_oc", 2)
    o_sq = signal("o_sq", 2)
    o_ss = signal("o_ss", 2)
    o_r = signal("o_r", 2)
    o_made = signal("o_made", 3)
    o_T = signal("o_T", 6)
    oT_made = signal("oT_made", 3)
    bf_read = signal("bf_read")
    bf_s = signal("bf_s")
    b_clamp = signal("b_clamp")
    b_g = signal("b_g")
    b_diff = signal("b_diff", 8)
    b_exp = signal("b_exp", 8)
    b_qk = signal("b_qk", 9)
    b_att = signal("b_att", 9)
    b_masked = signal("b_masked", 9)
    b_od = signal("b_od")
    b_oc = signal("b_oc")
    c_sqd = signal("c_sqd", 6)
    c_ss = signal("c_ss", 6, ahead=1)
    c_r = signal("c_r", 6)
    c_nm = signal("c_nm", 6, ahead=1)
    c_Td = signal("c_Td", 6, ahead=1)
    c_Te = signal("c_Te", 6, ahead=1)
    c_vc = signal("c_vc", 3, ahead=1)
    c_sd = signal("c_sd", 8)
    c_sm = signal("c_sm", 8)
    c_mx = signal("c_mx", 8)
    c_e = signal("c_e", 8)
    c_Pd = signal("c_Pd", 8)
    c_PTc = signal("c_PTc", 8)
    c_od = signal("c_od", 8)
    c_oc = signal("c_oc", 8)
    o_hi_made = signal("o_hi_made", 3)
    o_lo_made = signal("o_lo_made", 3)
    g_tanh = signal("g_tanh", 6, ahead=1)
    g_prod_made = signal("g_prod_made", 6, ahead=1)
    mix_made = signal("mix_made", 6, ahead=1)
    f_zero = signal("f_zero")
    f_silu = signal("f_silu")
    f_gm = signal("f_gm", 1, ahead=2)
    f_gT = signal("f_gT", 1, ahead=1)
    f_hi = signal("f_hi")
    f_lo = signal("f_lo", 1, ahead=1)
    r_done = signal("r_done")
    r_read = signal("r_read")
    r_e = signal("r_e")
    r_sel = signal("r_sel")
    r_cnt = signal("r_cnt")
    r_flag_made = signal("r_flag_made")
    slots_here = signal("slots_here")
    fn_hi_made = signal("fn_hi_made")
    fn_lo_made = signal("fn_lo_made")
    pick0 = signal("pick0")
    pick_made = signal("pick_made")
    pickT_done = signal("pickT_done", 1, ahead=1)
    pickT_made = signal("pickT_made")
    e_done = signal("e_done", 1, ahead=1)
    e_hi_made = signal("e_hi_made")
    e_lo_made = signal("e_lo_made", 1, ahead=1)
    y_hi_made = signal("y_hi_made")
    y_lo_made = signal("y_lo_made", 1, ahead=1)
    s_done = signal("s_done")
    s_read = signal("s_read", 1, ahead=1)
    x_last = signal("x_last")
    out_here = signal("out_here")

    def unit_view(t, k):
        return t[:, :].rearrange("p (k n) -> p k n", k=k)

    def wide(ap, n):
        return ap.unsqueeze(2).broadcast_to([P, ap.shape[1], n])

    def over(ap, m):
        return ap.unsqueeze(1).broadcast_to([P, m, ap.shape[1]])

    ones = ones_t[:, :]

    def second_turn(eng, prog):
        eng.wait_ge(r_flag_made.sem, 1)
        return eng.value_load(r_flag[0:1, 0:1], min_val=0, max_val=1)

    block = ctx.enter_context(nc.Block())

    @block.tensor
    def _(pe):
        prog = Program(None)
        for sig in (c_Td, e_done, pickT_done, f_gT):
            pe.sem_inc(sig.sem, sig.ahead)

        def products(out, a_hi, a_lo, b_hi, b_lo, first, last):
            pe.matmul(out, a_hi, b_hi, start=first, stop=False, skip_group_check=True)
            pe.matmul(out, a_hi, b_lo, start=False, stop=False, skip_group_check=True)
            return pe.matmul(out, a_lo, b_hi, start=False, stop=last, skip_group_check=True)

        def unit_ready():
            pe.wait_ge(hi_made.sem, prog.unit(1))
            pe.wait_ge(lo_made.sem, prog.unit(1))
            s = prog.u % SPLIT
            return hi[s], lo[s]

        def unit_over(ins):
            ins.then_inc(unit_used.sem, 1)
            prog.u += 1

        def turn_input(src, idx, L):
            for j in range(4):
                for kk in range(2):
                    for t in range(TT):
                        k = 2 * j + kk
                        ins = pe.transpose(PS[:, 4 + j, (2 * kk + t) * P:(2 * kk + t + 1) * P],
                                           src[:, t, k * P:(k + 1) * P], ident)
                ins.then_inc(turned.sem, 1)
            pe.wait_ge(actT_lo_made.sem, actT_lo_made.at(L, idx + 3))

        def group_T(pair):
            for half in range(2):
                w_hi, w_lo = unit_ready()
                for ct in range(4):
                    out = PS[:, 2 * pair + ct // 2, (ct % 2) * T:(ct % 2 + 1) * T]
                    for k in range(4):
                        a = half * 4 + k
                        c = slice(ct * P, (ct + 1) * P)
                        ins = products(out, unit_view(w_hi, 4)[:, k, c], unit_view(w_lo, 4)[:, k, c],
                                       actT_hi[:, a, :], actT_lo[:, a, :],
                                       first=half == 0 and k == 0 and ct % 2 == 0, last=half == 1 and k == 3)
                unit_over(ins)

        def group_nat(pair, lhs_hi=None, lhs_lo=None, halves=2):
            lhs_hi, lhs_lo = lhs_hi or actT_hi, lhs_lo or actT_lo
            for half in range(halves):
                w_hi, w_lo = unit_ready()
                for t in range(TT):
                    for k in range(4):
                        a = half * 4 + k
                        ins = products(PS[:, 2 * pair + t, :],
                                       lhs_hi[:, a, t * P:(t + 1) * P], lhs_lo[:, a, t * P:(t + 1) * P],
                                       unit_view(w_hi, 4)[:, k, :], unit_view(w_lo, 4)[:, k, :],
                                       first=half == 0 and k == 0, last=half == halves - 1 and k == 3)
                unit_over(ins)

        def heads(fn):
            for h in range(H):
                ins = fn(h)
            return ins

        def mm(out, a, b, first=True, last=True):
            return pe.matmul(out, a, b, start=first, stop=last)

        def hs(h):
            return slice(h * P, (h + 1) * P)

        pe.wait_ge(consts_here.sem, 32)
        pe.wait_ge(rows_here.sem, 16 * N_ROW_LOADS)
        pe.transpose(PS[:, 0, 0:R_N], rows[0:R_N, :], ident[0:R_N, 0:R_N]).then_inc(rows_T.sem, 1)
        pe.wait_ge(table_here.sem, 17)
        for g in range(GROUPS):
            ins = pe.matmul(PS[0:H, 1 + g, 0:DIST], table[:, g * H:(g + 1) * H], picks[:, g, :],
                            start=True, stop=True)
        ins.then_inc(by_dist_done.sem, 1)

        def spread_bias():
            pe.wait_ge(ab_read.sem, ab_read.at(0))
            pe.wait_ge(by_dist_kept.sem, 1)
            pe.wait_ge(hankel_here.sem, 16)
            for n in range(6):
                if n >= 3:
                    pe.wait_ge(bias_kept.sem, n - 2)
                ins = mm(PS[:, 4 + n % 3, :], consts[:, K_FLIP, :],
                         hankel[:, 2 * n:2 * n + 2, :].rearrange("p a b -> p (a b)"))
                ins.then_inc(bias_done.sem, 1)

        def mixer(L):
            pe.wait_ge(norm_made.sem, norm_made.at(L, 1))
            turn_input(hn, 0, L)
            for g in range(3):
                pair = g % 2
                if g == 0 and L == 0:
                    pe.wait_ge(rows_kept.sem, 1)
                    pe.wait_ge(by_dist_kept.sem, 1)
                if g == 2:
                    pe.wait_ge(a_raw.sem, a_raw.at(L, 1))
                group_T(pair)
                if g == 0:
                    pe.wait_ge(ab_split.sem, 2)
                    for t in range(TT):
                        for k in range(KT):
                            c = slice(t * P, (t + 1) * P)
                            ins = products(PS[:, 4, 8 * t:8 * t + 8], actT_hi[:, k, c], actT_lo[:, k, c],
                                           ab_hi[:, L, k, :], ab_lo[:, L, k, :], first=k == 0, last=k == KT - 1)
                    ins.then_inc(ab_done.sem, 1)
                if g == 1 and L == 0:
                    spread_bias()
            pe.wait_ge(a_raw.sem, a_raw.at(L, 3))
            group_nat(1)
            pe.wait_ge(*((ab_read.sem, ab_read.at(L)) if L else (bias_kept.sem, 4)))
            pe.wait_ge(a_g.sem, a_g.at(L))
            mm(PS[:, 4, 0:H], gt, a_s[:, 8, 0:H])
            mm(PS[:, 4, H:2 * H], le, a_s[:, 8, H:2 * H]).then_inc(a_cum.sem, 1)
            pe.wait_ge(a_raw.sem, a_raw.at(L, 5))
            group_T(0)
            pe.wait_ge(gate_made.sem, gate_made.at(L, 0))
            group_T(1)
            pe.wait_ge(gate_made.sem, gate_made.at(L, 1))
            group_nat(0)
            pe.wait_ge(bf_read.sem, bf_read.at(L))
            group_nat(1)
            deltanet(L)
            hgrn(L)
            dilated(L)
            branches(L)
            pe.wait_ge(mix_made.sem, mix_made.at(L, 5))
            turn_input(mix, 4, L)
            for half in range(2):
                group_nat(half)

        def deltanet(L):
            fwd_bank = (4, 5, 6, 7, 0, 1)
            pe.wait_ge(a_silu.sem, a_silu.at(L, 2))
            for c in range(TT):
                for g in range(3):
                    b = fwd_bank[3 * c + g]
                    if c == 0 and g == 0:
                        pe.wait_ge(a_cum_e.sem, a_cum_e.at(L))
                        if L == 0:
                            pe.wait_ge(bias_kept.sem, 6)
                    if b == 0:
                        pe.wait_ge(gate_made.sem, gate_made.at(L, 2))
                    heads(lambda h: pe.transpose(PS[:, b, hs(h)], a_act[:, g * H + h, c * P:(c + 1) * P], ident)).then_inc(a_fwd.sem, 1)
            for n, (made, c, src, b) in enumerate(((a_qn, 0, t_x, 2), (a_qn, 1, t_x, 3),
                                                   (a_kn, 0, k_nat, 6), (a_kn, 1, k_nat, 1))):
                free, k = (gate_tanh, 2) if n < 2 else (a_v, n - 2)
                pe.wait_ge(free.sem, free.at(L, k))
                pe.wait_ge(made.sem, made.at(L, c))
                heads(lambda h: pe.transpose(PS[:, b, hs(h)], src[:, c, h, :], ident)).then_inc(a_back.sem, 1)
            for n, (b, lhs, rhs) in enumerate(((4, le, t_m), (5, le, t_m), (7, gt, t_n), (0, gt, t_n))):
                pe.wait_ge(a_seg.sem, a_seg.at(L, n // 2))
                mm(PS[:, b, :], lhs, rhs[:, n % 2].rearrange("p h j -> p (h j)")).then_inc(a_dec.sem, 1)
            qT, kT = a_act[:, 0:H, :], a_act[:, H:2 * H, :]
            pe.wait_ge(a_T.sem, a_T.at(L, 3))
            for n, (b, c, rhs) in enumerate(((2, 0, kT), (3, 1, kT), (6, 0, qT), (1, 1, qT))):
                heads(lambda h: mm(PS[:, b, hs(h)], kT[:, h, c * P:(c + 1) * P], rhs[:, h, c * P:(c + 1) * P])).then_inc(a_kk.sem, 1)
            for c in range(TT):
                pe.wait_ge(a_exp.sem, a_exp.at(L, c))
                pe.wait_ge(a_M.sem, a_M.at(L, c))
                heads(lambda h: pe.transpose(PS[:, 4 + c, hs(h)], t_m[:, c, h, :], ident)).then_inc(a_N.sem, 1)
            for lv in range(1, LEVELS):
                for c in range(TT):
                    pe.wait_ge(a_No.sem, a_No.at(L, lv - 1))
                    pe.wait_ge(a_X.sem, a_X.at(L, 2 * lv - 3 + c if lv > 1 else 0))
                    heads(lambda h: mm(PS[:, 4 + c, hs(h)], t_w[:, c, h, :], t_x[:, c, h, :])).then_inc(a_P.sem, 1)
                for c in range(TT):
                    pe.wait_ge(a_Pc.sem, a_Pc.at(L, 2 * (lv - 1) + c))
                    pe.wait_ge(a_Y.sem, a_Y.at(L, 2 * lv - 3 + c if lv > 1 else 0))
                    if lv < LEVELS - 1:
                        heads(lambda h: mm(PS[:, 6 + c, hs(h)], t_y[:, c, h, :], t_m[:, c, h, :])).then_inc(a_XP.sem, 1)
                    heads(lambda h: mm(PS[:, c, hs(h)], t_m[:, c, h, :], t_y[:, c, h, :])).then_inc(a_YP.sem, 1)
            pe.wait_ge(a_r0.sem, a_r0.at(L))
            pe.wait_ge(a_Y.sem, a_Y.at(L, 11))
            heads(lambda h: mm(PS[:, 4, hs(h)], t_y[:, 0, h, :], t_w[:, 0, h, :])).then_inc(a_vn.sem, 1)
            pe.wait_ge(a_vc.sem, a_vc.at(L, 0))
            pe.wait_ge(a_kg.sem, a_kg.at(L))
            heads(lambda h: mm(PS[:, 5, hs(h)], t_v[:, 0, h, :], t_x[:, 0, h, :])).then_inc(a_S.sem, 1)
            pe.wait_ge(a_attn.sem, a_attn.at(L, 1))
            heads(lambda h: mm(PS[:, 2, hs(h)], attn[:, 0, h, :], t_x[:, 0, h, :])).then_inc(a_o.sem, 1)
            pe.wait_ge(a_Sc.sem, a_Sc.at(L))
            heads(lambda h: mm(PS[:, 6, hs(h)], kT[:, h, P:T], t_x[:, 1, h, :])).then_inc(a_kS.sem, 1)
            heads(lambda h: mm(PS[:, 7, hs(h)], qT[:, h, P:T], t_x[:, 1, h, :])).then_inc(a_qS.sem, 1)
            pe.wait_ge(a_r1.sem, a_r1.at(L))
            pe.wait_ge(a_Y.sem, a_Y.at(L, 12))
            heads(lambda h: mm(PS[:, 4, hs(h)], t_y[:, 1, h, :], t_w[:, 1, h, :])).then_inc(a_vn.sem, 1)
            pe.wait_ge(a_vc.sem, a_vc.at(L, 1))
            heads(lambda h: mm(PS[:, 3, hs(h)], attn[:, 1, h, :], t_m[:, 0, h, :])).then_inc(a_o.sem, 1)
            turn_output(L, 0, t_n)

        def turn_output(L, br, src):
            pe.wait_ge(o_made.sem, o_made.at(L, br))
            for h in range(H):
                for t in range(TT):
                    a = src[:, t, h, :] if len(src.shape) == 4 else src[:, t, hs(h)]
                    ins = pe.transpose(PS[:, 4 + h // 2, ((h % 2) * TT + t) * P:((h % 2) * TT + t + 1) * P],
                                       a, ident)
                if h % 2:
                    ins.then_inc(o_T.sem, 1)

        def hgrn(L):
            for n in range(LEVELS + 2):
                pe.wait_ge(b_qk.sem, b_qk.at(L, n))
                if n == LEVELS + 1:
                    heads(lambda h: mm(PS[:, 0, hs(h)], b_ke[:, h, 0:P], b_qe[:, h, P:T])).then_inc(b_att.sem, 1)
                    continue
                pair = (4, 6)[n % 2]
                k, q = (b_ke, b_qe) if n else (b_k, b_q)
                for c in range(TT):
                    for h in range(H):
                        t = slice(c * P, (c + 1) * P)
                        ins = mm(PS[:, pair + c, hs(h)], k[:, h, t], q[:, h, t])
                ins.then_inc(b_att.sem, 1)
            pe.wait_ge(b_masked.sem, b_masked.at(L, LEVELS + 1))
            for h in range(H):
                mm(PS[:, 2, hs(h)], b_attn[:, 0, h, :], b_i[:, 0, hs(h)])
                mm(PS[:, 3, hs(h)], b_attn[:, 1, h, :], b_i[:, 1, hs(h)], last=False)
                ins = mm(PS[:, 3, hs(h)], b_attn[:, 2, h, :], b_i[:, 0, hs(h)], first=False)
            ins.then_inc(b_od.sem, 1)
            turn_output(L, 1, b_o)

        def dilated(L):
            pe.wait_ge(oT_made.sem, oT_made.at(L, 1))
            with prog.loop(pe, GROUPS, 0) as g:
                pe.wait_ge(c_nm.sem, c_nm.count(L * 6 + 2 * g))
                group_nat(0)
                group_nat(1)

                def turn_c(j):
                    pe.wait_ge(c_nm.sem, c_nm.count(L * 6 + 2 * g + j + 1))
                    pe.wait_ge(c_Te.sem, c_Te.count(L * 6 + 2 * g + j))
                    for h in range(H):
                        for t in range(TT):
                            ins = pe.transpose(PS[:, 4 + h // 2, ((h % 2) * TT + t) * P:((h % 2) * TT + t + 1) * P],
                                               c_n[:, t, hs(h)], ident)
                    ins.then_inc(c_Td.sem, 1)

                turn_c(0)
                pe.wait_ge(c_vc.sem, c_vc.count(L * 3 + g))
                group_nat(3)
                turn_c(1)
            pe.wait_ge(c_nm.sem, c_nm.at(L, 5))
            pe.wait_ge(c_vc.sem, c_vc.at(L, 2))
            pe.wait_ge(c_Te.sem, c_Te.at(L, 5))
            def scores(n):
                t, h = divmod(n, H)
                b = 2 * (n % 2)
                keys = (t + 1) * P
                if n >= 2:
                    pe.wait_ge(c_sm.sem, c_sm.at(L, n - 2))
                for g in range(GROUPS):
                    out = PS[:, b + g // 2, (g % 2) * T:(g % 2) * T + keys]
                    ins = mm(out, c_qT[:, g * H + h, t * P:(t + 1) * P], c_kT[:, g * H + h, 0:keys])
                ins.then_inc(c_sd.sem, 1)

            def values(n):
                t, h = divmod(n, H)
                tiles = [(g, s) for g in range(GROUPS) for s in range(t + 1)]
                pe.wait_ge(c_e.sem, c_e.at(L, n))
                for m, (g, s) in enumerate(tiles):
                    at = g * T + s * P
                    ins = pe.transpose(PS[:, 4 + m // 4, (m % 4) * P:(m % 4 + 1) * P], c_p[:, at:at + P], ident)
                ins.then_inc(c_Pd.sem, 1)
                if n >= 2:
                    pe.wait_ge(c_oc.sem, c_oc.at(L, n - 2))
                pe.wait_ge(c_PTc.sem, c_PTc.at(L, n))
                for m, (g, s) in enumerate(tiles):
                    ins = mm(PS[:, 6 + n % 2, 0:P], c_pT[:, m * P:(m + 1) * P], c_v[:, s, g, hs(h)],
                             first=m == 0, last=m == len(tiles) - 1)
                ins.then_inc(c_od.sem, 1)

            scores(0)
            for n in range(TT * H):
                if n + 1 < TT * H:
                    scores(n + 1)
                values(n)
            turn_output(L, 2, c_o)

        def branches(L):
            with prog.loop(pe, 3, 0) as br:
                pe.wait_ge(g_prod_made.sem, g_prod_made.count(L * 6 + 2 * br))
                for half in range(2):
                    pe.wait_ge(g_tanh.sem, g_tanh.count(L * 6 + 2 * br + half))
                    group_nat(0)
                    if half == 0:
                        pe.wait_ge(o_lo_made.sem, L * 3 + br + 1)
                    pe.wait_ge(g_prod_made.sem, g_prod_made.count(L * 6 + 2 * br + half))
                    group_nat(1, o_hi, o_lo, halves=1)
            pe.wait_ge(g_prod_made.sem, g_prod_made.at(L, 5))

        def clear(banks, n):
            for b in banks:
                ins = pe.matmul(PS[:, b, :], zero[:, 0:P], zero[:, :], start=True, stop=False,
                                skip_group_check=True)

        def dense():
            pe.wait_ge(norm_made.sem, norm_made.at(0, 3))
            turn_input(fn, 8, 0)
            pe.wait_ge(f_zero.sem, 1)
            clear(range(4, 8), 0)

            def up(s, turn):
                pe.wait_ge(f_gm.sem, f_gm.count(turn + s - 1))
                for w in range(2):
                    w_hi, w_lo = unit_ready()
                    for j in range(2):
                        for k in range(KT):
                            c = slice(j * P, (j + 1) * P)
                            ins = products(PS[:, 2 * s + j, w * T:(w + 1) * T],
                                           unit_view(w_hi, 8)[:, k, c], unit_view(w_lo, 8)[:, k, c],
                                           actT_hi[:, k, :], actT_lo[:, k, :], first=k == 0, last=k == KT - 1)
                    unit_over(ins)

            def down(s, turn):
                pe.wait_ge(f_lo.sem, f_lo.count(turn + s + 1))
                w_hi, w_lo = unit_ready()
                for t in range(TT):
                    for half in range(2):
                        for k in range(2):
                            c, d = slice(t * P, (t + 1) * P), slice(half * 512, (half + 1) * 512)
                            ins = products(PS[:, 4 + 2 * t + half, :], fT_hi[s][:, k, c], fT_lo[s][:, k, c],
                                           unit_view(w_hi, 2)[:, k, d], unit_view(w_lo, 2)[:, k, d],
                                           first=False, last=False)
                unit_over(ins)

            with prog.loop(pe, PAIRS, 0) as i:
                up(0, 2 * i)
                up(1, 2 * i)
                down(0, 2 * i)
                down(1, 2 * i)
            up(0, 2 * PAIRS)
            down(0, 2 * PAIRS)

        def experts(turn):
            with prog.loop(pe, E, 0, rounds=EXPERT_R) as e:
                n = 8 * turn + e
                pe.wait_ge(pick_made.sem, n + 1)
                pe.wait_ge(s_read.sem, s_read.count(2 * n))
                pe.wait_ge(e_lo_made.sem, e_lo_made.count(2 * n))
                for t in range(TT):
                    ins = pe.transpose(PS[:, 2, t * P:(t + 1) * P], pick[:, t, :], ident)
                ins.then_inc(pickT_done.sem, 1)
                for k in range(KT):
                    for t in range(TT):
                        for part, src in enumerate((fn_hi, fn_lo)):
                            ins = pe.matmul(PS[:, 6 + k // 4, (k % 4) * P:(k % 4 + 1) * P],
                                            src[:, t, k * P:(k + 1) * P], pick_r[:, t, :],
                                            start=t == 0 and part == 0, stop=t == 1 and part == 1)
                    if k % 4 == 3:
                        ins.then_inc(e_done.sem, 1)
                pe.wait_ge(pickT_made.sem, n + 1)
                pe.wait_ge(e_lo_made.sem, e_lo_made.count(2 * n + 2))
                pe.wait_ge(y_lo_made.sem, y_lo_made.count(n))
                clear((4, 5), 1)
                base = STEPS_DENSE + 2 * EXPERT_PAIRS * n

                def up(s, at):
                    pe.wait_ge(f_gm.sem, f_gm.count(at + s - 1))
                    for w in range(2):
                        w_hi, w_lo = unit_ready()
                        for k in range(KT):
                            ins = products(PS[:, s, w * SUB:(w + 1) * SUB], e_hi[:, k, :], e_lo[:, k, :],
                                           unit_view(w_hi, 8)[:, k, :], unit_view(w_lo, 8)[:, k, :],
                                           first=k == 0, last=k == KT - 1)
                        unit_over(ins)

                def down(s, at):
                    pe.wait_ge(f_gm.sem, f_gm.count(at + s + 1))
                    for j in range(2):
                        ins = pe.transpose(PS[:, 2 + s, j * P:(j + 1) * P], f_g[s][:, j * P:(j + 1) * P], ident)
                    ins.then_inc(f_gT.sem, 1)
                    pe.wait_ge(f_lo.sem, f_lo.count(at + s + 1))
                    w_hi, w_lo = unit_ready()
                    for half in range(2):
                        for k in range(2):
                            d = slice(half * 512, (half + 1) * 512)
                            ins = products(PS[:, 4 + half, :], fT_hi[s][:, k, 0:P], fT_lo[s][:, k, 0:P],
                                           unit_view(w_hi, 2)[:, k, d], unit_view(w_lo, 2)[:, k, d],
                                           first=False, last=False)
                    unit_over(ins)

                with prog.loop(pe, EXPERT_PAIRS, 0) as c:
                    at = base + 2 * c
                    up(0, at)
                    up(1, at)
                    down(0, at)
                    down(1, at)
                pe.wait_ge(y_lo_made.sem, y_lo_made.count(n + 1))
                for t in range(TT):
                    for half in range(2):
                        for part, src in enumerate((y_hi, y_lo)):
                            ins = pe.matmul(PS[:, (6, 2)[t] + half, :], pickT[:, t, :],
                                            src[:, half * 512:(half + 1) * 512], start=part == 0, stop=part == 1)
                    ins.then_inc(s_done.sem, 1)

        def moe():
            pe.wait_ge(norm_made.sem, norm_made.at(1, 3))
            turn_input(fn, 8, 1)
            for t in range(TT):
                for k in range(KT):
                    c = slice(t * P, (t + 1) * P)
                    ins = products(PS[:, 0, 8 * t:8 * t + 8], actT_hi[:, k, c], actT_lo[:, k, c],
                                   ab_hi[:, 2, k, :], ab_lo[:, 2, k, :], first=k == 0, last=k == KT - 1)
            ins.then_inc(r_done.sem, 1)
            pe.wait_ge(r_sel.sem, 1)
            mm(PS[:, 1, 0:E], le, r_t[:, 12, 0:E])
            mm(PS[:, 1, E:2 * E], le, r_t[:, 12, E:2 * E], last=False)
            mm(PS[:, 1, E:2 * E], ones, r_t[:, 12, 0:E], first=False)
            mm(PS[:, 1, 2 * E:3 * E], ones, r_t[:, 12, 0:E], last=False)
            mm(PS[:, 1, 2 * E:3 * E], ones, r_t[:, 12, E:2 * E], first=False).then_inc(r_cnt.sem, 1)
            pe.wait_ge(f_zero.sem, 2)
            experts(0)
            more = second_turn(pe, prog)
            with pe.If(more > 0):
                experts(1)

        mixer(0)
        dense()
        mixer(1)
        moe()

    @block.scalar
    def _(act):
        prog = Program(act_step)
        for sig in (c_Te, c_vc, g_tanh):
            act.sem_inc(sig.sem, sig.ahead)
        SQ, EXP, LN, TANH, COPY, SILU = (ACT.Square, ACT.Exp, ACT.Ln, ACT.Tanh, ACT.Copy, ACT.Silu)

        def prep(count):
            for _ in range(count):
                slot = prog.u % RAW
                arrived = 16 * (prog.u // RAW + 1)
                act.wait_ge(raw_full[slot].sem, arrived if prog.rounds is None else arrived + prog.rounds * 16)
                if prog.u >= SPLIT:
                    act.wait_ge(unit_used.sem, prog.unit(1 - SPLIT))
                act.activation(hi[prog.u % SPLIT][:, :], raw[slot][:, :], COPY).then_inc(hi_made.sem, 1)
                prog.u += 1

        def used(L, n):
            act.wait_ge(unit_used.sem, LAYER_U[L] + n)

        def rsqrt_of(out, in_, scale, bias_out, sig):
            act.activation(out, in_, LN, bias=eps_t, scale=scale).then_inc(act_step.sem, 1)
            act.wait_ge(act_step.sem, prog.step())
            act.activation(out, out, EXP, bias=bias_out, scale=-0.5).then_inc(sig.sem, 1)

        act.wait_ge(tiny_made.sem, 4)
        act.wait_ge(rows_T.sem, 1)
        act.activation(small[:, :], PS[:, 0, 0:R_N], COPY).then_inc(rows_kept.sem, 1)
        act.wait_ge(rows_kept.sem, 1)
        act.wait_ge(lb_m.sem, 1)
        act.activation(lb[:, 4:6, :], lb[:, 4:6, :], EXP).then_inc(lb_e.sem, 1)
        act.wait_ge(par_here.sem, 32)
        act.activation(a_rate[:, :, :], a_par[:, 0, :, :], EXP).then_inc(a_rate_e.sem, 1)
        act.wait_ge(by_dist_done.sem, 1)
        act.activation(by_dist[:, :, :], PS[0:H, 1:1 + GROUPS, 0:DIST], COPY).then_inc(by_dist_kept.sem, 1)
        act.wait_ge(ab_here.sem, 48)
        act.activation(ab_hi[:, :, :, :], ab[:, :, :, :], COPY).then_inc(ab_split.sem, 1)

        def norm_scale(L, phase):
            if L == 0 and phase == 0:
                act.wait_ge(x_here.sem, 32)
            else:
                act.wait_ge(x_made.sem, x_made.at(L if phase else L - 1, 1 if phase else 2))
            dst = fn if phase else hn
            for t in range(TT):
                act.activation(dst[:, t, :], x[:, t, :], SQ, accum_out=stat[:, t:t + 1]).then_inc(act_step.sem, 1)
                act.wait_ge(act_step.sem, prog.step())
            act.activation(stat[:, 2:4], stat[:, 0:2], LN, bias=eps_t, scale=1.0 / D).then_inc(act_step.sem, 1)
            act.wait_ge(act_step.sem, prog.step())
            act.activation(stat[:, 4:6], stat[:, 2:4], EXP, scale=-0.5).then_inc(norm_r.sem, 1)

        def turn_input(idx, L, scale=1.0):
            for j in range(4):
                act.wait_ge(turned.sem, turned.at(L, idx + j))
                act.activation(actT_hi[:, 2 * j:2 * j + 2, :].rearrange("p a b -> p (a b)"),
                               PS[:, 4 + j, :], COPY, scale=scale).then_inc(actT_hi_made.sem, 1)

        def mixer(L):
            norm_scale(L, 0)
            turn_input(0, L)
            prep(2)

            def conv_in(g):
                used(L, 2 * g + 2)
                if g == 0:
                    act.wait_ge(pad_made.sem, L + 1)
                for b in range(2):
                    ct = g * H + 2 * b
                    act.activation(a_in[:, ct:ct + 2, 3:3 + T],
                                   PS[:, 2 * (g % 2) + b, :].rearrange("p (a b) -> p a b", a=2), COPY).then_inc(a_raw.sem, 1)

            def conv_tanh(g):
                act.wait_ge(a_conv.sem, a_conv.at(L, g))
                act.activation((t_x, t_y, t_w)[g][:, :, :, :].rearrange("p a b c -> p (a b c)"),
                               a_act[:, g * H:(g + 1) * H, :].rearrange("p a b -> p (a b)"), TANH, scale=0.5).then_inc(a_tanh.sem, 1)

            prep(2)
            conv_in(0)
            act.wait_ge(ab_read.sem, ab_read.at(L))
            act.activation(a_s[:, 3, :], a_s[:, 2, :], EXP, scale=-1.0).then_inc(act_step.sem, 1)
            act.wait_ge(act_step.sem, prog.step())
            act.activation(a_s[:, 5, :], a_s[:, 4, :], EXP, scale=-1.0).then_inc(a_e1.sem, 1)
            act.wait_ge(a_e1.sem, a_e1.at(L))
            act.activation(a_s[:, 6, :], a_s[:, 5, :], LN, bias=one_t).then_inc(a_e2.sem, 1)
            prep(2)
            conv_in(1)
            if L == 0:
                for n in range(6):
                    act.wait_ge(bias_done.sem, n + 1)
                    act.activation(bias[:, 2 * n:2 * n + 2, :].rearrange("p a b -> p (a b)"),
                                   PS[:, 4 + n % 3, :], COPY).then_inc(bias_kept.sem, 1)
            conv_tanh(0)
            prep(2)
            conv_in(2)
            conv_tanh(1)
            prep(2)
            used(L, 8)
            conv_tanh(2)
            act.activation(t_v[:, :, :, :].rearrange("p a b c -> p (a b c)"),
                           PS[:, 2:4, :].rearrange("p a b -> p (a b)"), TANH, scale=0.5).then_inc(gate_tanh.sem, 1)
            act.wait_ge(a_cum.sem, a_cum.at(L))
            act.activation(a_s[:, 11, :], PS[:, 4, 0:2 * H], EXP).then_inc(a_cum_e.sem, 1)
            prep(2)
            used(L, 10)
            act.activation(b_q[:, :, :].rearrange("p a b -> p (a b)"),
                           PS[:, 0:2, :].rearrange("p a b -> p (a b)"), TANH, scale=0.5).then_inc(gate_tanh.sem, 1)
            prep(2)
            act.wait_ge(bf_read.sem, bf_read.at(L))
            bf = b_f[:, :, :].rearrange("p a b -> p (a b)")
            act.activation(bf, bf, EXP, scale=-1.0).then_inc(act_step.sem, 1)
            act.wait_ge(act_step.sem, prog.step())
            act.activation(bf, bf, LN, bias=one_t).then_inc(act_step.sem, 1)
            act.wait_ge(act_step.sem, prog.step())
            act.activation(bf, bf, EXP, scale=-1.0).then_inc(bf_s.sem, 1)
            prep(2)
            used(L, 14)
            act.wait_ge(a_conv.sem, a_conv.at(L, 2))
            act.wait_ge(gate_made.sem, gate_made.at(L, 1))
            act.activation(b_i[:, :, :].rearrange("p a b -> p (a b)"),
                           PS[:, 0:2, :].rearrange("p a b -> p (a b)"), COPY).then_inc(gate_made.sem, 1)
            prep(2)
            used(L, 16)
            act.activation(b_gate[:, :, :].rearrange("p a b -> p (a b)"),
                           PS[:, 2:4, :].rearrange("p a b -> p (a b)"), TANH, scale=0.5).then_inc(gate_tanh.sem, 1)
            deltanet(L)
            hgrn(L)
            dilated(L)
            branches(L)
            turn_input(4, L)
            prep(2)

        def flat(t):
            return t[:, :, :, :].rearrange("p a b c -> p (a b c)") if len(t.shape) == 4 else \
                t[:, :, :].rearrange("p a b -> p (a b)")

        def bank(*b):
            return PS[:, b[0], :] if len(b) == 1 else PS[:, b[0]:b[1] + 1, :].rearrange("p a b -> p (a b)")

        def chunk(t, c):
            return t[:, c].rearrange("p h j -> p (h j)")

        def deltanet(L):
            for c in range(TT):
                for g, dst in ((0, t_w), (1, t_v)):
                    act.wait_ge(a_fwd.sem, a_fwd.at(L, 3 * c + g))
                    act.activation(chunk(dst, c), bank((4, 5, 6, 7, 0, 1)[3 * c + g]), SQ).then_inc(a_sq.sem, 1)
                act.wait_ge(a_fwd.sem, a_fwd.at(L, 3 * c + 2))
                act.activation(chunk(v_nat, c), bank((6, 1)[c]), COPY).then_inc(a_v.sem, 1)
            act.wait_ge(a_ss.sem, a_ss.at(L))
            act.activation(a_s[:, 13:15, :], a_s[:, 9:11, :], LN, bias=eps_t).then_inc(act_step.sem, 1)
            act.wait_ge(act_step.sem, prog.step())
            act.activation(a_s[:, 15, :], a_s[:, 13, :], EXP, bias=lnq_t, scale=-0.5).then_inc(act_step.sem, 1)
            act.wait_ge(act_step.sem, prog.step())
            act.activation(a_s[:, 16, :], a_s[:, 14, :], EXP, scale=-0.5).then_inc(a_r.sem, 1)
            for n, (b, ct, c) in enumerate(((2, 0, 0), (3, 0, 1), (6, H, 0), (1, H, 1))):
                act.wait_ge(a_back.sem, a_back.at(L, n))
                act.activation(a_act[:, ct:ct + H, c * P:(c + 1) * P],
                               bank(b).rearrange("p (h j) -> p h j", h=H), COPY).then_inc(a_T.sem, 1)
            for n, (b, dst) in enumerate(((4, t_x), (5, t_x), (7, t_y), (0, t_y))):
                act.wait_ge(a_dec.sem, a_dec.at(L, n))
                act.activation(chunk(dst, n % 2), bank(b), EXP).then_inc(a_exp.sem, 1)
            for c in range(TT):
                act.wait_ge(a_N.sem, a_N.at(L, c))
                act.activation(chunk(t_n, c), bank(4 + c), COPY).then_inc(a_Nc.sem, 1)
            for lv in range(1, LEVELS):
                for c in range(TT):
                    act.wait_ge(a_P.sem, a_P.at(L, 2 * (lv - 1) + c))
                    act.activation(chunk(t_m, c), bank(4 + c), COPY).then_inc(a_Pc.sem, 1)
            act.wait_ge(a_vn.sem, a_vn.at(L, 0))
            act.activation(chunk(t_x, 0), bank(4), COPY).then_inc(a_vc.sem, 1)
            act.wait_ge(a_S.sem, a_S.at(L))
            act.activation(chunk(t_x, 1), bank(5), COPY).then_inc(a_Sc.sem, 1)
            act.wait_ge(a_o.sem, a_o.at(L, 0))
            act.activation(chunk(t_n, 0), bank(2), COPY).then_inc(a_oc.sem, 1)
            act.wait_ge(a_vn.sem, a_vn.at(L, 1))
            act.activation(chunk(t_m, 0), bank(4), COPY).then_inc(a_vc.sem, 1)
            output_norm(L, 0, t_n, t_y, a_oc)
            turn_output(L, 0)

        def output_norm(L, br, src, tmp, made):
            act.wait_ge(made.sem, made.at(L, made.per_layer - 1))
            act.activation(flat(tmp), flat(src), SQ).then_inc(o_sq.sem, 1)
            act.wait_ge(o_ss.sem, o_ss.at(L, br))
            act.activation(a_s[:, 18, :], a_s[:, 17, :], LN, bias=eps_t, scale=1.0 / P).then_inc(act_step.sem, 1)
            act.wait_ge(act_step.sem, prog.step())
            act.activation(a_s[:, 19, :], a_s[:, 18, :], EXP, scale=-0.5).then_inc(o_r.sem, 1)

        def turn_output(L, br):
            act.wait_ge(o_T.sem, o_T.at(L, 2 * br + 1))
            col = (R_GA + L, R_GB + L, None)[br]
            act.activation(oT[:, br, :, :].rearrange("p a b -> p (a b)"), bank(4, 5), COPY,
                           scale=1.0 if col is None else small[:, col:col + 1]).then_inc(oT_made.sem, 1)

        def hgrn(L):
            act.wait_ge(b_clamp.sem, b_clamp.at(L))
            act.activation(flat(b_f), flat(b_f), LN).then_inc(b_g.sem, 1)
            for n in range(LEVELS + 1):
                s = 1 << n
                act.wait_ge(b_diff.sem, b_diff.at(L, n))
                v = flat(b_e).rearrange("p (n s) -> p n s", s=2 * s)
                act.activation(v[:, :, s:2 * s], v[:, :, s:2 * s], EXP).then_inc(act_step.sem, 1)
                act.wait_ge(act_step.sem, prog.step())
                act.activation(v[:, :, 0:s], v[:, :, 0:s], EXP, scale=-1.0).then_inc(b_exp.sem, 1)
            act.wait_ge(b_od.sem, b_od.at(L))
            act.activation(flat(b_o), bank(2, 3), COPY).then_inc(b_oc.sem, 1)
            output_norm(L, 1, b_o, b_o2, b_oc)
            turn_output(L, 1)

        def dilated(L):
            with prog.loop(act, GROUPS, 2) as g:
                u = LAYER_U[L] + U_C + 6 * g

                def square(j):
                    act.wait_ge(unit_used.sem, u + 2 * j + 2)
                    act.wait_ge(c_ss.sem, c_ss.count(L * 6 + 2 * g + j))
                    act.activation(flat(c_sq), bank(2 * j, 2 * j + 1), SQ).then_inc(c_sqd.sem, 1)
                    act.wait_ge(c_ss.sem, c_ss.count(L * 6 + 2 * g + j + 1))
                    rsqrt_of(stat[:, 8:16], stat[:, 0:8], 1.0 / P, zero_t, c_r)

                def turned_c(j):
                    act.wait_ge(c_Td.sem, c_Td.count(L * 6 + 2 * g + j + 1))
                    dst = (c_qT, c_kT)[j]
                    col = (R_QN, R_KN)[j] + L * GROUPS
                    act.activation(dst[:, bass.ds(g * H, H), :].rearrange("p a b -> p (a b)"), bank(4, 5),
                                   COPY, scale=small[:, bass.ds(g + col, 1)]).then_inc(c_Te.sem, 1)

                prep(2)
                square(0)
                prep(2)
                turned_c(0)
                square(1)
                prep(2)
                act.wait_ge(unit_used.sem, u + 6)
                act.activation(c_v[:, :, bass.ds(g, 1), :].rearrange("p t o n -> p t (o n)"),
                               PS[:, 6:8, :], COPY).then_inc(c_vc.sem, 1)
                turned_c(1)
            def copies(n):
                act.wait_ge(c_Pd.sem, c_Pd.at(L, n))
                if n:
                    act.wait_ge(c_od.sem, c_od.at(L, n - 1))
                w = GROUPS * (n // H + 1) * P
                act.activation(c_pT[:, 0:w], PS[:, 4:6, :].rearrange("p a b -> p (a b)")[:, 0:w], COPY).then_inc(c_PTc.sem, 1)

            for n in range(TT * H):
                t = n // H
                keys = (t + 1) * P
                act.wait_ge(c_mx.sem, c_mx.at(L, n))
                if n:
                    act.wait_ge(c_Pd.sem, c_Pd.at(L, n - 1))
                act.activation(c_p[:, :].rearrange("p (g s) -> p g s", g=GROUPS)[:, :, 0:keys],
                               c_s[:, :].rearrange("p (g s) -> p g s", g=GROUPS)[:, :, 0:keys],
                               EXP, bias=stat[:, 1:2], accum_out=stat[:, 2:3]).then_inc(c_e.sem, 1)
                copies(n)
            turn_output(L, 2)

        def branches(L):
            act.wait_ge(oT_made.sem, oT_made.at(L, 2))
            with prog.loop(act, 3, 0) as br:
                u = LAYER_U[L] + U_BR + 6 * br
                act.wait_ge(unit_used.sem, u)
                act.activation(flat(o_hi), oT[:, bass.ds(br, 1), :, :].rearrange("p o a b -> p (o a b)"),
                               COPY).then_inc(o_hi_made.sem, 1)

                def gate(half):
                    act.wait_ge(unit_used.sem, u + 3 * half + 2)
                    act.wait_ge(g_prod_made.sem, g_prod_made.count(L * 6 + 2 * br + half))
                    act.activation(flat(g_sig), bank(0, 1), TANH, scale=0.5).then_inc(g_tanh.sem, 1)

                prep(1)
                gate(0)
                prep(3)
                gate(1)
                prep(2)

        def dense():
            norm_scale(0, 1)
            turn_input(8, 0)
            U = LAYER_U[0] + U_FF

            def first(s, m):
                act.wait_ge(f_gm.sem, f_gm.count(m - 1))
                act.activation(f_s[s][:, :].rearrange("p (j t) -> p j t", j=2),
                               PS[:, 2 * s:2 * s + 2, 0:T], SILU).then_inc(f_silu.sem, 1)

            def second(s, m):
                act.wait_ge(f_gm.sem, f_gm.count(m + 1))
                act.activation(fT_hi[s][:, :, :].rearrange("p a b -> p (a b)"), f_g[s][:, :], COPY).then_inc(f_hi.sem, 1)

            with prog.loop(act, PAIRS, 0) as i:
                u, m = U + 6 * i, 2 * i
                prep(4)
                first(0, m)
                prep(1)
                second(0, m)
                prep(1)
                first(1, m + 1)
                second(1, m + 1)
            prep(2)
            act.wait_ge(unit_used.sem, U + 6 * PAIRS + 2)
            first(0, 2 * PAIRS)
            second(0, 2 * PAIRS)
            prep(1)

        def experts(turn):
            with prog.loop(act, E, 0, rounds=EXPERT_R) as e:
                n = 8 * turn + e
                u0_ = U_END + 8 * 6 * EXPERT_R * turn + 6 * EXPERT_R * e
                act.wait_ge(pickT_done.sem, pickT_done.count(n + 1))
                act.activation(flat(pickT), PS[:, 2, 0:T], COPY).then_inc(pickT_made.sem, 1)
                for j in range(2):
                    act.wait_ge(e_done.sem, e_done.count(2 * n + j + 1))
                    act.activation(e_hi[:, 4 * j:4 * j + 4, :].rearrange("p a b -> p (a b)"), bank(6 + j),
                                   COPY).then_inc(e_hi_made.sem, 1)
                base = STEPS_DENSE + 2 * EXPERT_PAIRS * n

                def first(s, m):
                    act.wait_ge(f_gm.sem, f_gm.count(m - 1))
                    act.activation(f_s[s][:, 0:SUB], PS[:, s, 0:SUB], SILU).then_inc(f_silu.sem, 1)

                def second(s, m):
                    act.wait_ge(f_gT.sem, f_gT.count(m - STEPS_DENSE + 1))
                    act.activation(fT_hi[s][:, :, 0:P], PS[:, 2 + s, 0:SUB].rearrange("p (j t) -> p j t", j=2),
                                   COPY).then_inc(f_hi.sem, 1)

                with prog.loop(act, EXPERT_PAIRS, 0) as c:
                    m = base + 2 * c
                    prep(4)
                    first(0, m)
                    prep(1)
                    second(0, m)
                    prep(1)
                    first(1, m + 1)
                    second(1, m + 1)
                act.wait_ge(unit_used.sem, u0_ + 6 * EXPERT_R)
                act.activation(y_hi[:, :], bank(4, 5), COPY).then_inc(y_hi_made.sem, 1)

        def moe():
            norm_scale(1, 1)
            turn_input(8, 1)
            act.wait_ge(norm_made.sem, norm_made.at(1, 3))
            act.activation(flat(fn_hi), flat(fn), COPY).then_inc(fn_hi_made.sem, 1)
            act.wait_ge(r_read.sem, 1)
            act.activation(r_t[:, 10, 0:TT], r_t[:, 9, 0:TT], EXP).then_inc(r_e.sem, 1)
            experts(0)
            more = second_turn(act, prog)
            with act.If(more > 0):
                experts(1)

        mixer(0)
        dense()
        mixer(1)
        moe()

    @block.vector
    def _(dve):
        prog = Program(dve_step)
        for sig in (c_nm, c_ss, g_prod_made, mix_made, f_gm, f_lo, s_read, e_lo_made, y_lo_made):
            dve.sem_inc(sig.sem, sig.ahead)

        def prep(count):
            for _ in range(count):
                s = prog.u % SPLIT
                dve.wait_ge(hi_made.sem, prog.unit(1))
                dve.tensor_tensor(lo[s][:, :], raw[prog.u % RAW][:, :], hi[s][:, :].bitcast(F32),
                                  ALU.subtract).then_inc(lo_made.sem, 1)
                prog.u += 1

        def used(L, n):
            dve.wait_ge(unit_used.sem, LAYER_U[L] + n)

        def flat(t):
            return t[:, :, :, :].rearrange("p a b c -> p (a b c)") if len(t.shape) == 4 else \
                t[:, :, :].rearrange("p a b -> p (a b)")

        def flat8(t):
            return t[:, :, :, :].rearrange("p a b c -> p (a b) c") if len(t.shape) == 4 else \
                t[:, :, :].rearrange("p a (b c) -> p (a b) c", c=P)

        def bank(*b):
            return PS[:, b[0], :] if len(b) == 1 else PS[:, b[0]:b[1] + 1, :].rearrange("p a b -> p (a b)")

        def bank4(b):
            return PS[:, b, :].rearrange("p (h j) -> p h j", h=H)

        def tt(out, a, b, op):
            return dve.tensor_tensor(out, a, b, op)

        def half_sigmoid(ap):
            return dve.tensor_scalar(ap, ap, 1.0, 0.5, ALU.add, ALU.mult)

        for n, v in enumerate((EPS, 1.0, math.log(P ** -0.5), 0.0)):
            dve.memset(tiny[:, n:n + 1], v).then_inc(tiny_made.sem, 1)
        dve.memset(ones_t[:, :], 1.0).then_inc(dve_step.sem, 1)
        dve.wait_ge(dve_step.sem, prog.step())
        dve.memset(table[BUCKETS:BUCKETS + 1, :], 1.0).then_inc(table_here.sem, 1)
        dve.wait_ge(rows_kept.sem, 1)
        lbr = small[:, R_LB:R_LB + 2 * H].rearrange("p (l h) -> p l h", l=2)
        tt(lb[:, 2, :], lbr[:, 0, :], lbr[:, 1, :], ALU.max).then_inc(dve_step.sem, 1)
        dve.wait_ge(dve_step.sem, prog.step())
        tt(lb[:, 4:6, :], lbr, over(lb[:, 2, :], 2), ALU.subtract).then_inc(lb_m.sem, 1)
        dve.wait_ge(lb_e.sem, 1)
        tt(lb[:, 2, :], lb[:, 4, :], lb[:, 5, :], ALU.add).then_inc(dve_step.sem, 1)
        dve.wait_ge(dve_step.sem, prog.step())
        dve.reciprocal(lb[:, 3, :], lb[:, 2, :]).then_inc(dve_step.sem, 1)
        dve.wait_ge(dve_step.sem, prog.step())
        tt(lb[:, 4:6, :], lb[:, 4:6, :], over(lb[:, 3, :], 2), ALU.mult).then_inc(dve_step.sem, 1)
        dve.wait_ge(dve_step.sem, prog.step())
        tt(lb[:, 2, :], lb[:, 4, :], lb[:, 5, :], ALU.add).then_inc(dve_step.sem, 1)
        dve.wait_ge(dve_step.sem, prog.step())
        tt(lb[:, 0, :], lb[:, 2, :], lb[:, 4, :], ALU.subtract).then_inc(dve_step.sem, 1)
        dve.wait_ge(dve_step.sem, prog.step())
        dve.tensor_scalar(lb[:, 1, :], lb[:, 0, :], -1.0, 1.0, ALU.mult, ALU.add).then_inc(dve_step.sem, 1)
        dve.wait_ge(dve_step.sem, prog.step())
        dve.wait_ge(a_rate_e.sem, 1)
        dve.tensor_scalar(a_rate[:, :, :], a_rate[:, :, :], -1.0, None, ALU.mult).then_inc(dve_step.sem, 1)
        dve.wait_ge(dve_step.sem, prog.step())
        dve.wait_ge(ab_split.sem, 1)
        tt(ab_lo[:, :, :, :], ab[:, :, :, :], ab_hi[:, :, :, :].bitcast(F32), ALU.subtract).then_inc(ab_split.sem, 1)

        def norm(L, phase):
            src = x
            dst, g = (fn, f_gain) if phase else (hn, gain)
            dve.wait_ge(norm_r.sem, norm_r.at(L, phase))
            dve.wait_ge(gain_here.sem, 16 * (2 * L + phase + 1))
            for t in range(TT):
                dve.scalar_tensor_tensor(dst[:, t, :], src[:, t, :], stat[:, 4 + t:5 + t], g[:, :],
                                         ALU.mult, ALU.mult).then_inc(norm_made.sem, 1)

        def turn_input(idx, L, scale=1.0):
            for j in range(4):
                dve.wait_ge(actT_hi_made.sem, actT_hi_made.at(L, idx + j))
                v = slice(2 * j, 2 * j + 2)
                dve.scalar_tensor_tensor(actT_lo[:, v, :].rearrange("p a b -> p (a b)"), bank(4 + j), scale,
                                         actT_hi[:, v, :].rearrange("p a b -> p (a b)").bitcast(F32),
                                         ALU.mult, ALU.subtract).then_inc(actT_lo_made.sem, 1)

        def mixer(L):
            norm(L, 0)
            turn_input(0, L)
            prep(2)
            dve.memset(a_in[:, :, 0:3], 0.0).then_inc(pad_made.sem, 1)
            dve.wait_ge(pad_made.sem, L + 1)

            def conv(g):
                dve.wait_ge(a_raw.sem, a_raw.at(L, 2 * g + 1))
                if g == 0 and L == 0:
                    dve.wait_ge(rows_kept.sem, 1)
                for tap in range(TAPS):
                    for n in range(H):
                        ct = g * H + n
                        col = R_CONV + (L * TAPS + tap) * CT + ct
                        src, w = a_in[:, ct, tap:tap + T], small[:, col:col + 1]
                        if tap == 0:
                            ins = dve.tensor_scalar(a_act[:, ct, :], src, w, None, ALU.mult)
                        else:
                            ins = dve.scalar_tensor_tensor(a_act[:, ct, :], src, w, a_act[:, ct, :],
                                                           ALU.mult, ALU.add)
                        if tap == TAPS - 1 and n == H - 1:
                            ins.then_inc(a_conv.sem, 1)
                        elif n == H - 1:
                            ins.then_inc(dve_step.sem, 1)
                            dve.wait_ge(dve_step.sem, prog.step())
                        else:
                            ins.then_inc(dve_step.sem, 1)
                            prog.step()

            def silu(g):
                th = (t_x, t_y, t_w)[g]
                act_g = a_act[:, g * H:(g + 1) * H, :].rearrange("p a b -> p (a b)")
                dve.wait_ge(a_tanh.sem, a_tanh.at(L, g))
                half_sigmoid(flat(th)).then_inc(dve_step.sem, 1)
                dve.wait_ge(dve_step.sem, prog.step())
                tt(act_g, act_g, flat(th), ALU.mult).then_inc(a_silu.sem, 1)

            prep(2)
            conv(0)
            dve.wait_ge(ab_done.sem, ab_done.at(L))
            logits = PS[:, 4, 0:16].rearrange("p (t c) -> p t c", t=TT)

            def a8(n):
                return a_s[:, n, :].rearrange("p (t h) -> p t h", t=TT)

            dve.wait_ge(par_here.sem, 32)
            tt(a8(1), logits[:, :, H:2 * H], over(a_par[:, 1, L, :], TT), ALU.add).then_inc(dve_step.sem, 1)
            dve.wait_ge(dve_step.sem, prog.step())
            dve.scalar_tensor_tensor(a_s[:, 4, :], a_s[:, 1, :], -1.0, a_s[:, 1, :], ALU.mult, ALU.max).then_inc(dve_step.sem, 1)
            dve.wait_ge(dve_step.sem, prog.step())
            dve.tensor_copy(a8(2), logits[:, :, 0:H]).then_inc(ab_read.sem, 1)
            dve.wait_ge(ab_read.sem, ab_read.at(L))
            dve.wait_ge(a_e1.sem, a_e1.at(L))
            dve.tensor_scalar(a_s[:, 3, :], a_s[:, 3, :], 1.0, None, ALU.add).then_inc(dve_step.sem, 1)
            dve.wait_ge(dve_step.sem, prog.step())
            dve.reciprocal(a_s[:, 0, :], a_s[:, 3, :]).then_inc(dve_step.sem, 1)
            dve.wait_ge(dve_step.sem, prog.step())
            dve.wait_ge(a_e2.sem, a_e2.at(L))
            dve.tensor_scalar(a_s[:, 7, :], a_s[:, 1, :], 0.0, None, ALU.max).then_inc(dve_step.sem, 1)
            dve.wait_ge(dve_step.sem, prog.step())
            tt(a_s[:, 7, :], a_s[:, 7, :], a_s[:, 6, :], ALU.add).then_inc(dve_step.sem, 1)
            dve.wait_ge(dve_step.sem, prog.step())
            tt(a8(8), a8(7), over(a_rate[:, L, :], TT), ALU.mult).then_inc(a_g.sem, 1)
            dve.wait_ge(a_g.sem, a_g.at(L))
            prep(2)
            conv(1)
            silu(0)
            prep(2)
            conv(2)
            silu(1)
            prep(2)
            silu(2)
            dve.wait_ge(gate_tanh.sem, gate_tanh.at(L, 0))
            half_sigmoid(flat(t_v)).then_inc(dve_step.sem, 1)
            dve.wait_ge(dve_step.sem, prog.step())
            dve.wait_ge(a_silu.sem, a_silu.at(L, 2))
            tt(flat(a_gate), bank(2, 3), flat(t_v), ALU.mult).then_inc(gate_made.sem, 1)
            dve.wait_ge(gate_made.sem, gate_made.at(L, 0))
            prep(2)
            dve.wait_ge(gate_tanh.sem, gate_tanh.at(L, 1))
            half_sigmoid(flat(b_q)).then_inc(dve_step.sem, 1)
            dve.wait_ge(dve_step.sem, prog.step())
            tt(flat(b_q), bank(0, 1), flat(b_q), ALU.mult).then_inc(gate_made.sem, 1)
            dve.wait_ge(gate_made.sem, gate_made.at(L, 1))
            prep(2)
            used(L, 12)
            dve.tensor_scalar(flat(b_f), bank(2, 3), -40.0, None, ALU.max).then_inc(bf_read.sem, 1)
            dve.wait_ge(bf_read.sem, bf_read.at(L))
            prep(2)
            dve.wait_ge(bf_s.sem, bf_s.at(L))
            if L == 1:
                for h in range(H):
                    ins = dve.tensor_scalar(b_f[:, h, :], b_f[:, h, :], lb[:, 1, h:h + 1], lb[:, 0, h:h + 1],
                                            ALU.mult, ALU.add)
                    ins.then_inc(dve_step.sem, 1)
                    dve.wait_ge(dve_step.sem, prog.step())
            prep(2)
            dve.wait_ge(gate_tanh.sem, gate_tanh.at(L, 2))
            half_sigmoid(flat(b_gate)).then_inc(gate_made.sem, 1)
            dve.wait_ge(gate_made.sem, gate_made.at(L, 3))
            deltanet(L)
            hgrn(L)
            dilated(L)
            branches(L)
            turn_input(4, L)
            prep(2)
            for half in range(2):
                used(L, U_OUT + 2 * half + 2)
                h = slice(half * 512, (half + 1) * 512)
                tt(x[:, :, h], x[:, :, h], PS[:, 2 * half:2 * half + 2, :], ALU.add).then_inc(x_made.sem, 1)
                dve.wait_ge(x_made.sem, x_made.at(L, half))

        def chunk(t, c):
            return t[:, c].rearrange("p h j -> p (h j)")

        def scale8(t):
            return wide(t, P)

        def deltanet(L):
            beta, g, r_q, r_k = (a_s[:, n, :] for n in (0, 8, 15, 16))
            for n, (src, k) in enumerate(((t_w, 0), (t_v, 1))):
                dve.wait_ge(a_sq.sem, a_sq.at(L, 2 + k))
                ins = dve.tensor_reduce(a_s[:, 9 + n, :], flat8(src), AX.X, ALU.add)
                if n:
                    ins.then_inc(a_ss.sem, 1)
                    dve.wait_ge(a_ss.sem, a_ss.at(L))
                else:
                    ins.then_inc(dve_step.sem, 1)
                    dve.wait_ge(dve_step.sem, prog.step())
            dve.wait_ge(a_r.sem, a_r.at(L))
            for c in range(TT):
                c4 = slice(c * H, (c + 1) * H)
                tt(t_x[:, c], bank4((4, 7)[c]), wide(r_q[:, c4], P), ALU.mult).then_inc(a_qn.sem, 1)
                tt(k_nat[:, c], bank4((5, 0)[c]), wide(r_k[:, c4], P), ALU.mult).then_inc(a_kn.sem, 1)
            tt(flat8(t_m), over(gt, 8), wide(g, P), ALU.mult).then_inc(a_seg.sem, 1)
            tt(flat8(t_n), over(le, 8), wide(g, P), ALU.mult).then_inc(a_seg.sem, 1)
            tt(flat8(t_w), over(gt, 8), wide(beta, P), ALU.mult).then_inc(dve_step.sem, 1)
            dve.wait_ge(dve_step.sem, prog.step())
            dve.wait_ge(a_exp.sem, a_exp.at(L, 1))
            tt(flat8(t_x), flat8(t_x), flat8(t_w), ALU.mult).then_inc(dve_step.sem, 1)
            dve.wait_ge(dve_step.sem, prog.step())
            dve.wait_ge(a_exp.sem, a_exp.at(L, 3))
            tt(flat8(t_y), flat8(t_y), over(le, 8), ALU.mult).then_inc(dve_step.sem, 1)
            dve.wait_ge(dve_step.sem, prog.step())
            for c in range(TT):
                dve.wait_ge(a_kk.sem, a_kk.at(L, c))
                tt(chunk(t_m, c), bank(2 + c), chunk(t_x, c), ALU.mult).then_inc(a_M.sem, 1)
                dve.wait_ge(a_M.sem, a_M.at(L, c))
            for c in range(TT):
                dve.wait_ge(a_kk.sem, a_kk.at(L, 2 + c))
                tt(chunk(attn, c), bank((6, 1)[c]), chunk(t_y, c), ALU.mult).then_inc(a_attn.sem, 1)
                dve.wait_ge(a_attn.sem, a_attn.at(L, c))
            tt(flat8(t_x), flat8(t_m), over(consts[:, K_M0, :], 8), ALU.mult).then_inc(dve_step.sem, 1)
            dve.wait_ge(dve_step.sem, prog.step())
            tt(flat8(t_x), over(ident, 8), flat8(t_x), ALU.subtract).then_inc(a_X.sem, 1)
            dve.wait_ge(a_X.sem, a_X.at(L, 0))
            dve.wait_ge(a_Nc.sem, a_Nc.at(L, 1))
            tt(flat8(t_y), flat8(t_n), over(consts[:, K_MT, :], 8), ALU.mult).then_inc(dve_step.sem, 1)
            dve.wait_ge(dve_step.sem, prog.step())
            tt(flat8(t_y), over(ident, 8), flat8(t_y), ALU.subtract).then_inc(a_Y.sem, 1)
            dve.wait_ge(a_Y.sem, a_Y.at(L, 0))

            def off(lv):
                tt(flat8(t_w), flat8(t_n), over(consts[:, K_MT + lv, :], 8), ALU.mult).then_inc(a_No.sem, 1)

            off(1)
            for lv in range(1, LEVELS):
                dve.wait_ge(a_P.sem, a_P.at(L, 2 * (lv - 1) + 1))
                if lv < LEVELS - 1:
                    off(lv + 1)
                else:
                    tt(t_w[:, 0], v_nat[:, 0], wide(beta[:, 0:H], P), ALU.mult).then_inc(a_r0.sem, 1)
                    dve.wait_ge(a_cum_e.sem, a_cum_e.at(L))
                    tt(t_v[:, 0], k_nat[:, 0], wide(a_s[:, 11, 0:H], P), ALU.mult).then_inc(a_kg.sem, 1)
                for c in range(TT):
                    if lv < LEVELS - 1:
                        dve.wait_ge(a_XP.sem, a_XP.at(L, 2 * (lv - 1) + c))
                        tt(chunk(t_x, c), chunk(t_x, c), bank(6 + c), ALU.subtract).then_inc(a_X.sem, 1)
                        dve.wait_ge(a_X.sem, a_X.at(L, 2 * lv - 1 + c))
                    dve.wait_ge(a_YP.sem, a_YP.at(L, 2 * (lv - 1) + c))
                    tt(chunk(t_y, c), chunk(t_y, c), bank(c), ALU.subtract).then_inc(a_Y.sem, 1)
                    dve.wait_ge(a_Y.sem, a_Y.at(L, 2 * lv - 1 + c))
            eg = wide(a_s[:, 11, H:2 * H], P)
            dve.wait_ge(a_kS.sem, a_kS.at(L))
            tt(t_v[:, 1], bank4(6), eg, ALU.mult).then_inc(dve_step.sem, 1)
            dve.wait_ge(dve_step.sem, prog.step())
            tt(t_v[:, 1], v_nat[:, 1], t_v[:, 1], ALU.subtract).then_inc(dve_step.sem, 1)
            dve.wait_ge(dve_step.sem, prog.step())
            tt(t_w[:, 1], t_v[:, 1], wide(beta[:, H:2 * H], P), ALU.mult).then_inc(a_r1.sem, 1)
            dve.wait_ge(a_qS.sem, a_qS.at(L))
            tt(t_m[:, 1], bank4(7), eg, ALU.mult).then_inc(dve_step.sem, 1)
            dve.wait_ge(dve_step.sem, prog.step())
            dve.wait_ge(a_o.sem, a_o.at(L, 1))
            dve.wait_ge(a_oc.sem, a_oc.at(L, 0))
            tt(chunk(t_n, 1), chunk(t_m, 1), bank(3), ALU.add).then_inc(a_oc.sem, 1)
            dve.wait_ge(a_oc.sem, a_oc.at(L, 1))
            output_norm(L, 0, t_n, t_y, a_gate)

        def output_norm(L, br, src, sq, gate):
            dve.wait_ge(o_sq.sem, o_sq.at(L, br))
            dve.tensor_reduce(a_s[:, 17, :], flat8(sq), AX.X, ALU.add).then_inc(o_ss.sem, 1)
            dve.wait_ge(o_r.sem, o_r.at(L, br))
            tt(flat8(src), flat8(src), wide(a_s[:, 19, :], P), ALU.mult).then_inc(dve_step.sem, 1)
            dve.wait_ge(dve_step.sem, prog.step())
            tt(flat8(src), flat8(src), flat8(gate), ALU.mult).then_inc(o_made.sem, 1)
            dve.wait_ge(o_made.sem, o_made.at(L, br))

        def hgrn(L):
            dve.wait_ge(oT_made.sem, oT_made.at(L, 0))
            dve.tensor_scalar(flat(b_k), flat(b_f), -1.0, 1.0, ALU.mult, ALU.add).then_inc(b_qk.sem, 1)
            dve.wait_ge(b_qk.sem, b_qk.at(L, 0))
            dve.tensor_scalar(flat(b_f), flat(b_f), 1e-18, None, ALU.max).then_inc(b_clamp.sem, 1)
            dve.wait_ge(b_clamp.sem, b_clamp.at(L))
            dve.memset(flat(b_attn), 0.0).then_inc(dve_step.sem, 1)
            dve.wait_ge(dve_step.sem, prog.step())
            dve.wait_ge(b_g.sem, b_g.at(L))
            for h in range(H):
                ins = dve.tensor_tensor_scan(b_gc[:, h, :], zero_t.broadcast_to([P, T]), b_f[:, h, :], 0.0,
                                             ALU.add, ALU.add)
                ins.then_inc(dve_step.sem, 1)
                dve.wait_ge(dve_step.sem, prog.step())

            def masked(n):
                dve.wait_ge(b_att.sem, b_att.at(L, n))
                if n == LEVELS + 1:
                    dve.tensor_copy(chunk(b_attn, 2), bank(0)).then_inc(b_masked.sem, 1)
                    dve.wait_ge(b_masked.sem, b_masked.at(L, n))
                    return
                pair = (4, 6)[n % 2]
                mask = ident if n == 0 else consts[:, K_MT + n - 1, :]
                dve.copy_predicated(b_attn[:, 0:2].rearrange("p c h j -> p (c h) j"),
                                    over(mask, 8).bitcast(I32),
                                    PS[:, pair:pair + 2, :].rearrange("p c (h j) -> p (c h) j", h=H)).then_inc(b_masked.sem, 1)
                dve.wait_ge(b_masked.sem, b_masked.at(L, n))

            for n in range(LEVELS + 1):
                s = 1 << n
                v = flat(b_gc).rearrange("p (n s) -> p n s", s=2 * s)
                mid = v[:, :, s - 1:s].broadcast_to([P, H * T // (2 * s), 2 * s])
                tt(flat(b_e).rearrange("p (n s) -> p n s", s=2 * s), v, mid, ALU.subtract).then_inc(b_diff.sem, 1)
                dve.wait_ge(b_diff.sem, b_diff.at(L, n))
                masked(n)
                dve.wait_ge(b_exp.sem, b_exp.at(L, n))
                tt(flat(b_qe), flat(b_q), flat(b_e), ALU.mult).then_inc(dve_step.sem, 1)
                dve.wait_ge(dve_step.sem, prog.step())
                tt(flat(b_ke), flat(b_k), flat(b_e), ALU.mult).then_inc(b_qk.sem, 1)
                dve.wait_ge(b_qk.sem, b_qk.at(L, n + 1))
            masked(LEVELS + 1)
            output_norm(L, 1, b_o, b_o2, b_gate)

        def dilated(L):
            with prog.loop(dve, GROUPS, 0) as g:
                def normed(j):
                    dve.wait_ge(c_sqd.sem, L * 6 + 2 * g + j + 1)
                    dve.tensor_reduce(stat[:, 0:8], flat8(c_sq), AX.X, ALU.add).then_inc(c_ss.sem, 1)
                    dve.wait_ge(c_r.sem, L * 6 + 2 * g + j + 1)
                    dve.wait_ge(c_Td.sem, c_Td.count(L * 6 + 2 * g + j))
                    tt(flat8(c_n), PS[:, 2 * j:2 * j + 2, :].rearrange("p t (h j) -> p (t h) j", h=H),
                       wide(stat[:, 8:16], P), ALU.mult).then_inc(c_nm.sem, 1)

                prep(2)
                normed(0)
                prep(2)
                normed(1)
                prep(2)

            for n in range(TT * H):
                t, h = divmod(n, H)
                keys = (t + 1) * P
                b = 2 * (n % 2)
                off = T - keys
                sv = c_s[:, :].rearrange("p (g s) -> p g s", g=GROUPS)
                bv = bias[:, :, :].rearrange("p (g h) s -> p g h s", g=GROUPS)
                dve.wait_ge(c_sd.sem, c_sd.at(L, n))
                if n:
                    dve.wait_ge(c_e.sem, c_e.at(L, n - 1))
                dve.scalar_tensor_tensor(sv[:, 0:2, 0:keys],
                                         PS[:, b, :].rearrange("p (g s) -> p g s", g=2)[:, :, 0:keys],
                                         P ** -0.5, bv[:, 0:2, h, off:T], ALU.mult, ALU.add).then_inc(dve_step.sem, 1)
                dve.wait_ge(dve_step.sem, prog.step())
                dve.scalar_tensor_tensor(sv[:, 2, 0:keys], PS[:, b + 1, 0:keys], P ** -0.5,
                                         bv[:, 2, h, off:T], ALU.mult, ALU.add).then_inc(c_sm.sem, 1)
                dve.wait_ge(c_sm.sem, c_sm.at(L, n))
                dve.tensor_reduce(stat[:, 0:1], sv[:, :, 0:keys], AX.XY, ALU.max).then_inc(dve_step.sem, 1)
                dve.wait_ge(dve_step.sem, prog.step())
                dve.tensor_scalar(stat[:, 1:2], stat[:, 0:1], -1.0, None, ALU.mult).then_inc(c_mx.sem, 1)
                dve.wait_ge(c_e.sem, c_e.at(L, n))
                dve.reciprocal(stat[:, 3:4], stat[:, 2:3]).then_inc(dve_step.sem, 1)
                dve.wait_ge(dve_step.sem, prog.step())
                dve.wait_ge(c_od.sem, c_od.at(L, n))
                ins = dve.tensor_scalar(c_o[:, t, h * P:(h + 1) * P], PS[:, 6 + n % 2, 0:P], stat[:, 3:4], None,
                                        ALU.mult)
                ins.then_inc(c_oc.sem, 1)
                dve.wait_ge(c_oc.sem, c_oc.at(L, n))
            dve.memset(stat[:, 5:6], 0.0).then_inc(o_made.sem, 1)
            dve.wait_ge(o_made.sem, o_made.at(L, 2))

        def branches(L):
            dve.wait_ge(oT_made.sem, oT_made.at(L, 2))
            dve.memset(flat(mix), 0.0).then_inc(dve_step.sem, 1)
            dve.wait_ge(dve_step.sem, prog.step())
            with prog.loop(dve, 3, 2) as br:
                dve.wait_ge(o_hi_made.sem, L * 3 + br + 1)
                tt(flat(o_lo), oT[:, bass.ds(br, 1), :, :].rearrange("p o a b -> p (o a b)"),
                   flat(o_hi).bitcast(F32), ALU.subtract).then_inc(o_lo_made.sem, 1)

                def product(half):
                    dve.wait_ge(unit_used.sem, LAYER_U[L] + U_BR + 6 * br + 3 * half + 3)
                    dve.wait_ge(mix_made.sem, mix_made.count(L * 6 + 2 * br + half))
                    ins = tt(flat(g_prod), flat(g_sig), bank(2, 3), ALU.mult)
                    ins.then_inc(g_prod_made.sem, 1)
                    dve.wait_ge(g_prod_made.sem, g_prod_made.count(L * 6 + 2 * br + half + 1))
                    h = slice(half * 512, (half + 1) * 512)
                    tt(mix[:, :, h], mix[:, :, h], g_prod[:, :, :], ALU.add).then_inc(mix_made.sem, 1)
                    dve.wait_ge(mix_made.sem, mix_made.count(L * 6 + 2 * br + half + 1))

                def gate(half):
                    dve.wait_ge(g_tanh.sem, g_tanh.count(L * 6 + 2 * br + half + 1))
                    half_sigmoid(flat(g_sig)).then_inc(dve_step.sem, 1)
                    dve.wait_ge(dve_step.sem, prog.step())

                prep(1)
                gate(0)
                prep(2)
                product(0)
                prep(1)
                gate(1)
                prep(2)
                product(1)

        def make_zeros(L):
            dve.memset(zero_f[:, :], 0.0).then_inc(dve_step.sem, 1)
            dve.wait_ge(dve_step.sem, prog.step())
            dve.tensor_copy(zero[:, :], zero_f[:, :]).then_inc(f_zero.sem, 1)
            dve.wait_ge(f_zero.sem, L + 1)

        def dense():
            norm(0, 1)
            make_zeros(0)
            turn_input(8, 0)

            def multiply(s, m):
                dve.wait_ge(f_silu.sem, m + 1)
                dve.wait_ge(f_lo.sem, f_lo.count(m))
                ins = tt(f_g[s][:, :].rearrange("p (j t) -> p j t", j=2),
                         f_s[s][:, :].rearrange("p (j t) -> p j t", j=2), PS[:, 2 * s:2 * s + 2, T:2 * T], ALU.mult)
                ins.then_inc(f_gm.sem, 1)
                dve.wait_ge(f_gm.sem, f_gm.count(m + 1))

            def low(s, m):
                dve.wait_ge(f_hi.sem, m + 1)
                tt(flat(fT_lo[s]), f_g[s][:, :], flat(fT_hi[s]).bitcast(F32), ALU.subtract).then_inc(f_lo.sem, 1)

            with prog.loop(dve, PAIRS, 0) as i:
                prep(4)
                multiply(0, 2 * i)
                prep(1)
                low(0, 2 * i)
                prep(1)
                multiply(1, 2 * i + 1)
                low(1, 2 * i + 1)
            prep(2)
            multiply(0, 2 * PAIRS)
            low(0, 2 * PAIRS)
            prep(1)
            dve.wait_ge(unit_used.sem, LAYER_U[1])
            tt(flat(x), flat(x), PS[:, 4:8, :].rearrange("p a b -> p (a b)"), ALU.add).then_inc(x_made.sem, 1)
            dve.wait_ge(x_made.sem, x_made.at(0, 2))

        def experts(turn):
            with prog.loop(dve, E, 1, rounds=EXPERT_R) as e:
                n = 8 * turn + e
                u0_ = U_END + 8 * 6 * EXPERT_R * turn + 6 * EXPERT_R * e
                dve.wait_ge(e_done.sem, e_done.count(2 * n))
                dve.wait_ge(pickT_done.sem, pickT_done.count(n))
                for t in range(TT):
                    ins = dve.tensor_scalar(pick[:, t, :], slots[:, turn * P:(turn + 1) * P],
                                            r_t[:, 14, bass.ds(e + t * E, 1)], None, ALU.is_equal)
                    if t == 0:
                        ins.then_inc(dve_step.sem, 1)
                        dve.wait_ge(dve_step.sem, prog.step())
                    else:
                        ins.then_inc(pick0.sem, 1)
                        dve.wait_ge(pick0.sem, n + 1)
                dve.tensor_copy(flat(pick_r), flat(pick)).then_inc(pick_made.sem, 1)
                for j in range(2):
                    dve.wait_ge(e_hi_made.sem, 2 * n + j + 1)
                    v = slice(4 * j, 4 * j + 4)
                    tt(e_lo[:, v, :].rearrange("p a b -> p (a b)"), bank(6 + j),
                       e_hi[:, v, :].rearrange("p a b -> p (a b)").bitcast(F32), ALU.subtract).then_inc(e_lo_made.sem, 1)
                base = STEPS_DENSE + 2 * EXPERT_PAIRS * n

                def multiply(s, m):
                    dve.wait_ge(f_silu.sem, m + 1)
                    dve.wait_ge(f_gT.sem, f_gT.count(m - STEPS_DENSE))
                    ins = tt(f_g[s][:, 0:SUB], f_s[s][:, 0:SUB], PS[:, s, SUB:2 * SUB], ALU.mult)
                    ins.then_inc(f_gm.sem, 1)

                def low(s, m):
                    dve.wait_ge(f_hi.sem, m + 1)
                    tt(fT_lo[s][:, :, 0:P], PS[:, 2 + s, 0:SUB].rearrange("p (j t) -> p j t", j=2),
                       fT_hi[s][:, :, 0:P].bitcast(F32), ALU.subtract).then_inc(f_lo.sem, 1)

                with prog.loop(dve, EXPERT_PAIRS, 0) as c:
                    m = base + 2 * c
                    prep(4)
                    multiply(0, m)
                    prep(1)
                    low(0, m)
                    prep(1)
                    multiply(1, m + 1)
                    low(1, m + 1)
                dve.wait_ge(y_hi_made.sem, n + 1)
                tt(y_lo[:, :], bank(4, 5), y_hi[:, :].bitcast(F32), ALU.subtract).then_inc(y_lo_made.sem, 1)
                for t in range(TT):
                    b = (6, 2)[t]
                    dve.wait_ge(s_done.sem, 2 * n + t + 1)
                    ins = dve.scalar_tensor_tensor(x[:, t, :], bank(b, b + 1), r_t[:, 15, bass.ds(e + t * E, 1)],
                                                   x[:, t, :], ALU.mult, ALU.add)
                    ins.then_inc(s_read.sem, 1)
                dve.wait_ge(s_read.sem, s_read.count(2 * n + 2))

        def moe():
            norm(1, 1)
            make_zeros(1)
            turn_input(8, 1)
            dve.wait_ge(fn_hi_made.sem, 1)
            tt(flat(fn_lo), flat(fn), flat(fn_hi).bitcast(F32), ALU.subtract).then_inc(fn_lo_made.sem, 1)
            dve.wait_ge(r_done.sem, 1)

            def r16(n):
                return r_t[:, n, :]

            def r8(n):
                return r_t[:, n, :].rearrange("p (t e) -> p t e", t=TT)

            dve.tensor_copy(r16(0), PS[:, 0, 0:TT * E]).then_inc(dve_step.sem, 1)
            dve.wait_ge(dve_step.sem, prog.step())
            for k in range(2):
                lg, eq, cs, first, v = 0 + k, 2, 3, 4 + k, r_t[:, 8, 2 * k:2 * k + 2]
                dve.tensor_reduce(v, r8(lg), AX.X, ALU.max).then_inc(dve_step.sem, 1)
                dve.wait_ge(dve_step.sem, prog.step())
                tt(r8(eq), r8(lg), wide(v, E), ALU.is_equal).then_inc(dve_step.sem, 1)
                dve.wait_ge(dve_step.sem, prog.step())
                for t in range(TT):
                    dve.tensor_tensor_scan(r_t[:, cs, t * E:(t + 1) * E], zero_t.broadcast_to([P, E]),
                                           r_t[:, eq, t * E:(t + 1) * E], 0.0, ALU.add, ALU.add).then_inc(dve_step.sem, 1)
                    dve.wait_ge(dve_step.sem, prog.step())
                dve.scalar_tensor_tensor(r16(first), r16(cs), 1.0, r16(eq), ALU.is_equal, ALU.mult).then_inc(dve_step.sem, 1)
                dve.wait_ge(dve_step.sem, prog.step())
                if k == 0:
                    dve.scalar_tensor_tensor(r16(1), r16(first), NEG, r16(0), ALU.mult, ALU.add).then_inc(dve_step.sem, 1)
                    dve.wait_ge(dve_step.sem, prog.step())
            tt(r_t[:, 9, 0:2], r_t[:, 8, 2:4], r_t[:, 8, 0:2], ALU.subtract).then_inc(r_read.sem, 1)
            dve.wait_ge(r_read.sem, 1)
            tt(r16(12), r16(4), r16(5), ALU.add).then_inc(r_sel.sem, 1)
            dve.wait_ge(r_sel.sem, 1)
            dve.wait_ge(r_e.sem, 1)
            dve.tensor_scalar(r_t[:, 9, 2:4], r_t[:, 10, 0:2], 1.0, None, ALU.add).then_inc(dve_step.sem, 1)
            dve.wait_ge(dve_step.sem, prog.step())
            dve.reciprocal(r_t[:, 11, 0:2], r_t[:, 9, 2:4]).then_inc(dve_step.sem, 1)
            dve.wait_ge(dve_step.sem, prog.step())
            tt(r_t[:, 11, 2:4], r_t[:, 11, 0:2], r_t[:, 10, 0:2], ALU.mult).then_inc(dve_step.sem, 1)
            dve.wait_ge(dve_step.sem, prog.step())
            tt(r8(6), r8(4), wide(r_t[:, 11, 0:2], E), ALU.mult).then_inc(dve_step.sem, 1)
            dve.wait_ge(dve_step.sem, prog.step())
            tt(r8(7), r8(5), wide(r_t[:, 11, 2:4], E), ALU.mult).then_inc(dve_step.sem, 1)
            dve.wait_ge(dve_step.sem, prog.step())
            tt(r16(15), r16(6), r16(7), ALU.add).then_inc(dve_step.sem, 1)
            dve.wait_ge(dve_step.sem, prog.step())
            dve.wait_ge(r_cnt.sem, 1)
            tt(r16(14), PS[:, 1, 0:2 * E], r16(12), ALU.mult).then_inc(dve_step.sem, 1)
            dve.wait_ge(dve_step.sem, prog.step())
            dve.tensor_scalar(r16(14), r16(14), -1.0, None, ALU.add).then_inc(dve_step.sem, 1)
            dve.wait_ge(dve_step.sem, prog.step())
            dve.tensor_reduce(r_t[:, 13, 0:1], PS[:, 1, 2 * E:3 * E], AX.X, ALU.max).then_inc(dve_step.sem, 1)
            dve.wait_ge(dve_step.sem, prog.step())
            dve.tensor_scalar(r_flag[:, 0:1], r_t[:, 13, 0:1], float(P), None, ALU.is_gt).then_inc(r_flag_made.sem, 1)
            dve.wait_ge(r_flag_made.sem, 1)
            dve.wait_ge(slots_here.sem, 2)
            experts(0)
            more = second_turn(dve, prog)
            with dve.If(more > 0):
                experts(1)
            dve.memset(stat[:, 8:9], 0.0).then_inc(x_last.sem, 1)

        mixer(0)
        dense()
        mixer(1)
        moe()

    @block.gpsimd
    def _(pool):
        pool.dma_start(gain[:, :], dram["norm_mix"][0:1, :].partition_broadcast(P)
                       .rearrange("q o d -> q (o d)")).then_inc(gain_here.sem, 16)
        pool.wait_ge(by_dist_kept.sem, 1)
        pool.dma_start(hankel_dram.rearrange("(g h) z -> h g z", g=GROUPS), by_dist[:, :, :])\
            .then_inc(by_dist_out.sem, 16)
        pool.wait_ge(by_dist_out.sem, 16)
        pool.dma_start(hankel[:, :, :], bass.AP(hankel_dram.tensor, 0, [[1, P], [DIST, GROUPS * H], [1, T]]))\
            .then_inc(hankel_here.sem, 16)
        for L in range(DEPTH):
            if L:
                pool.wait_ge(x_made.sem, x_made.at(L - 1, 2))
                pool.dma_start(gain[:, :], dram["norm_mix"][L:L + 1, :].partition_broadcast(P)
                               .rearrange("q o d -> q (o d)")).then_inc(gain_here.sem, 16)
            pool.wait_ge(oT_made.sem, oT_made.at(L, 2))
            pool.wait_ge(gain_here.sem, 16 * (2 * L + 1))
            pool.dma_start(f_gain[:, :], dram["norm_ffn"][L:L + 1, :].partition_broadcast(P)
                           .rearrange("q o d -> q (o d)")).then_inc(gain_here.sem, 16)
        pool.wait_ge(x_made.sem, x_made.at(1, 1))
        pool.iota(slots_i[:, :], pattern=[[1, 2 * P]], base=0, channel_multiplier=0).then_inc(slots_here.sem, 1)
        pool.wait_ge(slots_here.sem, 1)
        pool.tensor_copy(slots[:, :], slots_i[:, :]).then_inc(slots_here.sem, 1)

    @block.sync
    def _(sp):
        prog = Program(None)

        def load(dst, src, sig):
            sp.dma_start(dst, src).then_inc(sig.sem, 16)

        def unit(src, k):
            slot = prog.u % RAW
            if prog.u >= RAW:
                sp.wait_ge(lo_made.sem, prog.unit(1 - RAW))
            load(unit_view(raw[slot], k), src, raw_full[slot])
            prog.u += 1

        def rows_of(ap):
            return ap.rearrange("(k p) n -> p k n", p=P)

        def cols(L, c):
            for half in range(2):
                sl = bass.ds(c, 512) if not isinstance(c, int) else slice(c, c + 512)
                unit(rows_of(dram["w_in"][L, half * 512:(half + 1) * 512, sl]), 4)

        xr = dram["x"][0].rearrange("(t p) d -> t p d", p=P)
        for t in range(TT):
            load(x[:, t, :], xr[t], x_here)
        load(consts[:, :, :], dram["masks"], consts_here)
        load(picks[:, :, :], dram["buckets"], consts_here)
        rows_of_small = (
            (R_CONV, dram["conv_a"].rearrange("l t (c p) -> (l t c) p", p=P)),
            (R_LB, dram["lb_logits"].rearrange("l (h p) -> (l h) p", p=P)),
            (R_GA, dram["gnorm_a"]), (R_GB, dram["gnorm_b"]),
            (R_QN, dram["qnorm_c"].rearrange("l g p -> (l g) p")),
            (R_KN, dram["knorm_c"].rearrange("l g p -> (l g) p")))
        assert len(rows_of_small) == N_ROW_LOADS
        for r, src in rows_of_small:
            load(rows[r:r + src.shape[0], :], src, rows_here)
        load(table[0:BUCKETS, :], dram["rel_bias"], table_here)
        for n in range(DEPTH):
            load(ab[:, n, :, :], rows_of(dram["w_in"][n, :, C_AB:C_AB + 2 * H]), ab_here)
        load(ab[:, 2, :, :], rows_of(dram["router"][0]), ab_here)
        for n, name in enumerate(("a_log", "dt_bias")):
            load(a_par[:, n, :, :], dram[name].rearrange("(o l) h -> o l h", o=1).partition_broadcast(P)
                 .rearrange("q o l h -> q (o l) h"), par_here)

        def mixer(L):
            for g in range(3):
                cols(L, C_QKV + g * W)
            cols(L, C_AGATE)
            for g in range(4):
                cols(L, C_BQ + g * W)
            with prog.loop(sp, GROUPS, 0) as g:
                for j in range(3):
                    cols(L, g * W + (C_CQKV + j * GROUPS * W))
            with prog.loop(sp, 3, 0) as br:
                for half in range(2):
                    cols(L, br * D + (C_BR + half * 512))
                    unit(rows_of(dram["w_br"][bass.ds(br, 1), L, :, half * 512:(half + 1) * 512]
                                 .rearrange("o r n -> (o r) n")), 4)
            for half in range(2):
                for k in range(2):
                    unit(rows_of(dram["w_out"][L, k * 512:(k + 1) * 512, half * 512:(half + 1) * 512]), 4)

        def up(w1, w3, c):
            for w in (w1, w3):
                unit(rows_of(w[:, bass.ds(c, SUB)]), 8)

        def dense():
            w1, w3, w2 = (dram[n][0] for n in ("ffn_w1", "ffn_w3", "ffn_w2"))

            def down(c):
                unit(rows_of(w2[bass.ds(c, SUB), :]), 2)

            with prog.loop(sp, PAIRS, 0) as i:
                up(w1, w3, i * (2 * SUB))
                up(w1, w3, i * (2 * SUB) + SUB)
                down(i * (2 * SUB))
                down(i * (2 * SUB) + SUB)
            last = PAIRS * 2 * SUB
            up(w1, w3, last)
            down(last)

        def experts():
            with prog.loop(sp, E, 0, rounds=EXPERT_R) as e:
                w1, w3, w2 = (dram[n][0, bass.ds(e, 1), :, :].rearrange("o r n -> (o r) n")
                              for n in ("moe_w1", "moe_w3", "moe_w2"))
                with prog.loop(sp, EXPERT_PAIRS, 0) as c:
                    up(w1, w3, c * (2 * SUB))
                    up(w1, w3, c * (2 * SUB) + SUB)
                    for s in range(2):
                        unit(rows_of(dram["moe_w2"][0, bass.ds(e, 1), bass.ds(c * (2 * SUB) + s * SUB, SUB), :]
                                     .rearrange("o r n -> (o r) n")), 2)

        mixer(0)
        dense()
        mixer(1)
        experts()
        more = second_turn(sp, prog)
        with sp.If(more > 0):
            experts()
        sp.wait_ge(x_last.sem, 1)
        out = dram["out"][0].rearrange("(t p) d -> t p d", p=P)
        for t in range(TT):
            load(out[t], x[:, t, :], out_here)
        sp.wait_ge(out_here.sem, 32)


_NAMES = ["x", "w_in", "norm_mix", "conv_a", "a_log", "dt_bias", "gnorm_a", "lb_logits", "gnorm_b", "qnorm_c",
          "knorm_c", "rel_bias", "w_out", "norm_ffn", "ffn_w1", "ffn_w3", "ffn_w2", "router", "moe_w1",
          "moe_w3", "moe_w2"]


def kernel(**inputs):
    import concourse.bacc as _bacc
    from concourse.bass_utils import run_bass_kernel_spmd as _run

    nc = _bacc.Bacc("TRN2", target_bir_lowering=False, num_devices=1)
    masks, buckets = shape_constants()
    given = {name: np.ascontiguousarray(inputs[name]) for name in _NAMES}
    given["w_br"] = np.stack([np.asarray(inputs[n]) for n in ("w_br_a", "w_br_b", "w_br_c")])
    given["masks"], given["buckets"] = masks, buckets
    dram, arrays = {}, {}
    for name, a in given.items():
        arrays[f"in_{name}"] = a
        dram[name] = nc.dram_tensor(f"in_{name}", a.shape, mybir.dt.from_np(a.dtype), kind="ExternalInput").ap()
    dram["out"] = nc.dram_tensor("out_x", (1, T, D), F32, kind="ExternalOutput").ap()
    with ExitStack() as ctx:
        build(ctx, nc, dram)
    return _run(nc, [arrays], core_ids=[0]).results[0]["out_x"]
```

```python
import math
from contextlib import ExitStack, contextmanager

import concourse.bass as bass
import numpy as np
from concourse import mybir

F32 = mybir.dt.float32
F32R = mybir.dt.float32r
I32 = mybir.dt.int32
ALU = mybir.AluOpType
ACT = mybir.ActivationFunctionType
AX = mybir.AxisListType

P = 128
T = 256
TT = T // P
D = 1024
KT = D // P
DEPTH = 2
EPS = 1e-6
H = 4
W = H * P
TAPS = 4
CT = 3 * H
GROUPS = 3
DILATION = (1, 4, 16)
SPAN = 128
BUCKETS, MAX_DIST = 32, 2048
E = 8
FF, FFE = 2816, 3584
SUB = 256
UE = 2048

C_QKV = 0
C_AB = 3 * W
C_AGATE = C_AB + 2 * H
C_BQ = C_AGATE + W
C_CQKV = C_BQ + 4 * W
C_BR = C_CQKV + 9 * W
NEG = -1e30

RAW = 6
SPLIT = 3
U_A, U_AG, U_B, U_C, U_BR, U_OUT, U_FF = 0, 6, 8, 16, 34, 52, 56
U_DENSE = 3 * (FF // SUB)
LAYER_U = (0, U_FF + U_DENSE)
U_END = LAYER_U[1] + U_FF
STEPS_DENSE, STEPS_EXPERT = FF // SUB, FFE // SUB
N_ROW_LOADS = 6
EXPERT_R = STEPS_EXPERT // 2

K_ID, K_LE, K_GT, K_M0, K_MT, K_FLIP, K_N = 0, 1, 2, 3, 4, 11, 12
LEVELS = 7
R_CONV, R_LB, R_GA, R_GB, R_QN, R_KN, R_N = 0, 96, 104, 106, 108, 114, 120
DIST = 384


def shape_constants():
    i, j = np.arange(P)[:, None], np.arange(P)[None, :]
    tiles = [i == j, i <= j, i > j, (i // 2 == j // 2) & (i > j)]
    for n in range(LEVELS):
        s = 1 << n
        tiles.append((i // (2 * s) == j // (2 * s)) & (j % (2 * s) >= s) & (i % (2 * s) < s))
    tiles.append(i + j == P - 1)
    masks = np.stack([t.astype(np.float32) for t in tiles], 1)
    buckets = np.zeros((BUCKETS + 1, GROUPS, DIST), np.float32)
    exact = BUCKETS // 2
    for g, dil in enumerate(DILATION):
        for z in range(DIST):
            dist = T - 1 - z
            if dist < 0 or dist % dil or dist // dil > SPAN:
                buckets[BUCKETS, g, z] = NEG
                continue
            b = dist
            if dist >= exact:
                big = np.log(np.float32(dist) / np.float32(exact)) / np.float32(math.log(MAX_DIST / exact))
                b = min(exact + int(np.float32(big) * np.float32(BUCKETS - exact)), BUCKETS - 1)
            buckets[b, g, z] = 1.0
    return masks, buckets


class Signal:

    def __init__(self, ctx, nc, name, per_layer=1, ahead=0):
        self.sem = ctx.enter_context(nc.semaphore(name))
        self.per_layer, self.ahead = per_layer, ahead

    def at(self, layer, k=0):
        return self.ahead + layer * self.per_layer + k + 1

    def count(self, n):
        return n + self.ahead


class Program:

    def __init__(self, own):
        self.own = own
        self.n, self.turn = 0, None
        self.u, self.rounds = 0, None

    def step(self):
        self.n += 1
        return self.n if self.turn is None else self.n + self.turn

    def unit(self, k=0, each=1):
        n = (self.u + k) * each
        return n if self.rounds is None else n + self.rounds * (6 * each)

    @contextmanager
    def loop(self, eng, trips, steps, rounds=1):
        with eng.Fori(0, trips) as i:
            n, u, turn, r = self.n, self.u, self.turn, self.rounds
            self.turn = i * steps if turn is None else turn + i * steps
            self.rounds = i * rounds if r is None else r + i * rounds
            yield i
            assert self.n - n == steps, f"{self.n - n} steps in a turn, not {steps}"
            assert self.u - u == 6 * rounds, f"{self.u - u} units in a turn"
            self.turn, self.rounds = turn, r
        self.n, self.u = n + trips * steps, u + trips * 6 * rounds


def build(ctx, nc, dram):
    cursor = nc.sbuf_base + (-nc.sbuf_base) % 64

    def sb(name, shape, dtype=F32, at=None):
        nonlocal cursor
        size = int(np.prod(shape[1:])) * 4
        size += (-size) % 64
        if at is None:
            at, cursor = cursor, cursor + size
        assert at + size <= nc.sbuf_usable_end, (name, at + size - nc.sbuf_usable_end)
        return nc.alloc_sbuf_tensor_at(name, shape, dtype, offset=at)

    w0 = cursor
    raw = [sb(f"raw{s}", [P, UE]) for s in range(RAW)]
    lo = [sb(f"lo{s}", [P, UE], F32R, at=w0 + s * UE * 4) for s in range(RAW)]
    hi = [sb(f"hi{s}", [P, UE], F32R) for s in range(SPLIT)]
    x = sb("x", [P, TT, D])
    ones_t = sb("ones_t", [P, P])
    actT_hi = sb("actT_hi", [P, KT, T], F32R)
    actT_lo = sb("actT_lo", [P, KT, T], F32R)
    consts = sb("consts", [P, K_N, P])
    bias = sb("bias", [P, GROUPS * H, T])
    small = sb("small", [P, R_N])
    ab = sb("ab", [P, 3, KT, 8])
    ab_hi = sb("ab_hi", [P, 3, KT, 8], F32R)
    ab_lo = sb("ab_lo", [P, 3, KT, 8], F32R)
    a_par = sb("a_par", [P, 2, DEPTH, H])
    a_rate = sb("a_rate", [P, DEPTH, H])
    lb = sb("lb", [P, 8, H])
    tiny = sb("tiny", [P, 8])
    stat = sb("stat", [P, 16])
    ident, le, gt = consts[:, K_ID, :], consts[:, K_LE, :], consts[:, K_GT, :]
    eps_t, one_t, lnq_t, zero_t = (tiny[:, n:n + 1] for n in range(4))

    u0 = cursor
    a_in = sb("a_in", [P, CT, 3 + T])
    u1 = cursor
    a_act = sb("a_act", [P, CT, T])
    b_q = sb("b_q", [P, H, T])
    b_f = sb("b_f", [P, H, T])
    oT = sb("oT", [P, 3, H, T])
    c0 = cursor
    cursor = c0 + 36 * 1024
    a_s = sb("a_s", [P, 20, TT * H])
    a_gate = sb("a_gate", [P, TT, W], at=u0)
    b_i = sb("b_i", [P, TT, W], at=u0 + 4096)
    b_gate = sb("b_gate", [P, TT, W], at=u0 + 8192)
    gain = sb("gain", [P, D], at=u1)
    b_gc = sb("b_gc", [P, H, T], at=u1)
    b_qe = sb("b_qe", [P, H, T], at=u1 + 4096)
    b_ke = sb("b_ke", [P, H, T], at=u1 + 8192)
    hn = sb("hn", [P, TT, D], at=c0)
    S8 = [P, TT, H, P]
    k_nat, v_nat, attn, t_m, t_n, t_x, t_y, t_w, t_v = (
        sb(name, S8, at=c0 + 4096 * n)
        for n, name in enumerate(("k_nat", "v_nat", "attn", "t_m", "t_n", "t_x", "t_y", "t_w", "t_v")))
    b_attn = sb("b_attn", [P, 3, H, P], at=c0)
    b_e = sb("b_e", [P, H, T], at=c0 + 6144)
    b_o = sb("b_o", [P, TT, W], at=c0 + 10240)
    b_o2 = sb("b_o2", [P, TT, W], at=c0 + 14336)
    b_k = sb("b_k", [P, H, T], at=c0 + 18432)
    c_qT = sb("c_qT", [P, GROUPS * H, T], at=c0)
    c_kT = sb("c_kT", [P, GROUPS * H, T], at=c0 + 12288)
    c_v = sb("c_v", [P, TT, GROUPS, W], at=c0 + 24576)
    c_sq = sb("c_sq", [P, TT, W], at=u0)
    c_n = sb("c_n", [P, TT, W], at=u0 + 4096)
    c_s = sb("c_s", [P, GROUPS * T], at=u0 + 8192)
    c_p = sb("c_p", [P, GROUPS * T], at=u0 + 11264)
    c_pT = sb("c_pT", [P, 2 * GROUPS * P], at=u0 + 14336)
    c_o = sb("c_o", [P, TT, W], at=u0 + 17408)
    g_sig = sb("g_sig", [P, TT, W], at=c0)
    g_prod = sb("g_prod", [P, TT, W], at=c0 + 4096)
    mix = sb("mix", [P, TT, D], at=c0 + 8192)
    o_hi = sb("o_hi", [P, H, T], F32R, at=c0 + 16384)
    o_lo = sb("o_lo", [P, H, T], F32R, at=c0 + 20480)
    rows = sb("rows", [P, P], at=u0)
    picks = sb("picks", [BUCKETS + 1, GROUPS, DIST], at=u0 + 512)
    table = sb("table", [BUCKETS + 1, GROUPS * H], at=u0 + 512 + 4608)
    by_dist = sb("by_dist", [H, GROUPS, DIST], at=u1 + 12288)
    hankel = sb("hankel", [P, GROUPS * H, T], at=u1 + 12288 + 8192)

    cursor = u0
    fn = sb("fn", [P, TT, D])
    f_gain = sb("f_gain", [P, D])
    f_s = [sb(f"f_s{s}", [P, 512]) for s in range(2)]
    f_g = [sb(f"f_g{s}", [P, 512]) for s in range(2)]
    fT_hi = [sb(f"fT_hi{s}", [P, 2, T], F32R) for s in range(2)]
    fT_lo = [sb(f"fT_lo{s}", [P, 2, T], F32R) for s in range(2)]
    r_t = sb("r_t", [P, 20, TT * E])
    r_flag = sb("r_flag", [P, 2], I32)
    slots = sb("slots", [P, 2 * P])
    slots_i = sb("slots_i", [P, 2 * P], I32)
    fn_hi = sb("fn_hi", [P, TT, D], F32R)
    fn_lo = sb("fn_lo", [P, TT, D], F32R)
    pick = sb("pick", [P, TT, P])
    pick_r = sb("pick_r", [P, TT, P], F32R)
    pickT = sb("pickT", [P, TT, P], F32R)
    e_hi = sb("e_hi", [P, KT, P], F32R)
    e_lo = sb("e_lo", [P, KT, P], F32R)
    y_hi = sb("y_hi", [P, D], F32R)
    y_lo = sb("y_lo", [P, D], F32R)

    PS = ctx.enter_context(nc.psum_tensor("PS", [P, 8, 512], F32))
    hankel_dram = nc.dram_tensor("hankel_dram", (GROUPS * H, DIST), F32, kind="Internal").ap()

    def signal(name, per_layer=1, ahead=0):
        return Signal(ctx, nc, name, per_layer, ahead)

    raw_full = [signal(f"raw_full{s}") for s in range(RAW)]
    hi_made = signal("hi_made")
    lo_made = signal("lo_made")
    unit_used = signal("unit_used")
    act_step = signal("act_step")
    dve_step = signal("dve_step")
    x_here = signal("x_here")
    consts_here = signal("consts_here")
    rows_here = signal("rows_here")
    table_here = signal("table_here")
    ab_here = signal("ab_here")
    par_here = signal("par_here")
    rows_T = signal("rows_T")
    rows_kept = signal("rows_kept")
    by_dist_done = signal("by_dist_done")
    by_dist_kept = signal("by_dist_kept")
    by_dist_out = signal("by_dist_out")
    hankel_here = signal("hankel_here")
    bias_done = signal("bias_done")
    bias_kept = signal("bias_kept")
    ab_split = signal("ab_split")
    lb_m = signal("lb_m")
    lb_e = signal("lb_e")
    a_rate_e = signal("a_rate_e")
    tiny_made = signal("tiny_made")
    gain_here = signal("gain_here")
    norm_r = signal("norm_r", 2)
    norm_made = signal("norm_made", 4)
    turned = signal("turned", 12)
    actT_hi_made = signal("actT_hi_made", 12)
    actT_lo_made = signal("actT_lo_made", 12)
    x_made = signal("x_made", 3)
    a_raw = signal("a_raw", 6)
    pad_made = signal("pad_made")
    a_conv = signal("a_conv", 3)
    a_tanh = signal("a_tanh", 3)
    a_silu = signal("a_silu", 3)
    ab_done = signal("ab_done")
    ab_read = signal("ab_read")
    a_e1 = signal("a_e1")
    a_e2 = signal("a_e2")
    a_g = signal("a_g")
    a_cum = signal("a_cum")
    a_cum_e = signal("a_cum_e")
    gate_tanh = signal("gate_tanh", 3)
    gate_made = signal("gate_made", 4)
    a_fwd = signal("a_fwd", 6)
    a_sq = signal("a_sq", 4)
    a_v = signal("a_v", 2)
    a_ss = signal("a_ss")
    a_r = signal("a_r")
    a_qn = signal("a_qn", 2)
    a_kn = signal("a_kn", 2)
    a_back = signal("a_back", 4)
    a_T = signal("a_T", 4)
    a_seg = signal("a_seg", 2)
    a_dec = signal("a_dec", 4)
    a_exp = signal("a_exp", 4)
    a_kk = signal("a_kk", 4)
    a_M = signal("a_M", 2)
    a_attn = signal("a_attn", 2)
    a_N = signal("a_N", 2)
    a_Nc = signal("a_Nc", 2)
    a_X = signal("a_X", 11)
    a_Y = signal("a_Y", 13)
    a_No = signal("a_No", 6)
    a_P = signal("a_P", 12)
    a_Pc = signal("a_Pc", 12)
    a_XP = signal("a_XP", 10)
    a_YP = signal("a_YP", 12)
    a_r0 = signal("a_r0")
    a_kg = signal("a_kg")
    a_vn = signal("a_vn", 2)
    a_vc = signal("a_vc", 2)
    a_S = signal("a_S")
    a_Sc = signal("a_Sc")
    a_kS = signal("a_kS")
    a_qS = signal("a_qS")
    a_r1 = signal("a_r1")
    a_o = signal("a_o", 2)
    a_oc = signal("a_oc", 2)
    o_sq = signal("o_sq", 2)
    o_ss = signal("o_ss", 2)
    o_r = signal("o_r", 2)
    o_made = signal("o_made", 3)
    o_T = signal("o_T", 6)
    oT_made = signal("oT_made", 3)
    bf_read = signal("bf_read")
    bf_s = signal("bf_s")
    b_clamp = signal("b_clamp")
    b_g = signal("b_g")
    b_diff = signal("b_diff", 8)
    b_exp = signal("b_exp", 8)
    b_qk = signal("b_qk", 9)
    b_att = signal("b_att", 9)
    b_masked = signal("b_masked", 9)
    b_od = signal("b_od")
    b_oc = signal("b_oc")
    c_sqd = signal("c_sqd", 6)
    c_ss = signal("c_ss", 6, ahead=1)
    c_r = signal("c_r", 6)
    c_nm = signal("c_nm", 6, ahead=1)
    c_Td = signal("c_Td", 6, ahead=1)
    c_Te = signal("c_Te", 6, ahead=1)
    c_vc = signal("c_vc", 3, ahead=1)
    c_sd = signal("c_sd", 8)
    c_sm = signal("c_sm", 8)
    c_mx = signal("c_mx", 8)
    c_e = signal("c_e", 8)
    c_Pd = signal("c_Pd", 8)
    c_PTc = signal("c_PTc", 8)
    c_od = signal("c_od", 8)
    c_oc = signal("c_oc", 8)
    o_hi_made = signal("o_hi_made", 3)
    o_lo_made = signal("o_lo_made", 3)
    g_tanh = signal("g_tanh", 6, ahead=1)
    g_prod_made = signal("g_prod_made", 6, ahead=1)
    mix_made = signal("mix_made", 6, ahead=1)
    f_silu = signal("f_silu")
    f_gm = signal("f_gm", 1, ahead=2)
    f_gT = signal("f_gT", 1, ahead=2)
    f_hi = signal("f_hi")
    f_lo = signal("f_lo", 1, ahead=2)
    r_done = signal("r_done")
    r_read = signal("r_read")
    r_e = signal("r_e")
    r_sel = signal("r_sel")
    r_cnt = signal("r_cnt")
    r_flag_made = signal("r_flag_made")
    slots_here = signal("slots_here")
    fn_hi_made = signal("fn_hi_made")
    fn_lo_made = signal("fn_lo_made")
    pick0 = signal("pick0")
    pick_made = signal("pick_made")
    pickT_done = signal("pickT_done", 1, ahead=1)
    pickT_made = signal("pickT_made")
    e_done = signal("e_done", 1, ahead=1)
    e_hi_made = signal("e_hi_made")
    e_lo_made = signal("e_lo_made", 1, ahead=1)
    y_hi_made = signal("y_hi_made")
    y_lo_made = signal("y_lo_made", 1, ahead=1)
    s_done = signal("s_done")
    s_read = signal("s_read", 1, ahead=1)
    x_last = signal("x_last")
    out_here = signal("out_here")

    def unit_view(t, k):
        return t[:, :].rearrange("p (k n) -> p k n", k=k)

    def wide(ap, n):
        return ap.unsqueeze(2).broadcast_to([P, ap.shape[1], n])

    def over(ap, m):
        return ap.unsqueeze(1).broadcast_to([P, m, ap.shape[1]])

    ones = ones_t[:, :]

    def second_turn(eng, prog):
        eng.wait_ge(r_flag_made.sem, 1)
        return eng.value_load(r_flag[0:1, 0:1], min_val=0, max_val=1)

    block = ctx.enter_context(nc.Block())

    @block.tensor
    def _(pe):
        prog = Program(None)
        for sig in (c_Td, e_done, pickT_done, f_gT):
            pe.sem_inc(sig.sem, sig.ahead)

        def products(out, a_hi, a_lo, b_hi, b_lo, first, last):
            pe.matmul(out, a_hi, b_hi, start=first, stop=False, skip_group_check=True)
            pe.matmul(out, a_hi, b_lo, start=False, stop=False, skip_group_check=True)
            return pe.matmul(out, a_lo, b_hi, start=False, stop=last, skip_group_check=True)

        def unit_ready():
            pe.wait_ge(hi_made.sem, prog.unit(1))
            pe.wait_ge(lo_made.sem, prog.unit(1))
            return hi[prog.u % SPLIT], lo[prog.u % RAW]

        def unit_over(ins):
            ins.then_inc(unit_used.sem, 1)
            prog.u += 1

        def turn_input(src, idx, L):
            for j in range(4):
                for kk in range(2):
                    for t in range(TT):
                        k = 2 * j + kk
                        ins = pe.transpose(PS[:, 4 + j, (2 * kk + t) * P:(2 * kk + t + 1) * P],
                                           src[:, t, k * P:(k + 1) * P], ident)
                ins.then_inc(turned.sem, 1)
            pe.wait_ge(actT_lo_made.sem, actT_lo_made.at(L, idx + 3))

        def group_T(pair):
            for half in range(2):
                w_hi, w_lo = unit_ready()
                for ct in range(4):
                    out = PS[:, 2 * pair + ct // 2, (ct % 2) * T:(ct % 2 + 1) * T]
                    for k in range(4):
                        a = half * 4 + k
                        c = slice(ct * P, (ct + 1) * P)
                        ins = products(out, unit_view(w_hi, 4)[:, k, c], unit_view(w_lo, 4)[:, k, c],
                                       actT_hi[:, a, :], actT_lo[:, a, :],
                                       first=half == 0 and k == 0 and ct % 2 == 0, last=half == 1 and k == 3)
                unit_over(ins)

        def group_nat(pair, lhs_hi=None, lhs_lo=None, halves=2):
            lhs_hi, lhs_lo = lhs_hi or actT_hi, lhs_lo or actT_lo
            for half in range(halves):
                w_hi, w_lo = unit_ready()
                for t in range(TT):
                    for k in range(4):
                        a = half * 4 + k
                        ins = products(PS[:, 2 * pair + t, :],
                                       lhs_hi[:, a, t * P:(t + 1) * P], lhs_lo[:, a, t * P:(t + 1) * P],
                                       unit_view(w_hi, 4)[:, k, :], unit_view(w_lo, 4)[:, k, :],
                                       first=half == 0 and k == 0, last=half == halves - 1 and k == 3)
                unit_over(ins)

        def heads(fn):
            for h in range(H):
                ins = fn(h)
            return ins

        def mm(out, a, b, first=True, last=True):
            return pe.matmul(out, a, b, start=first, stop=last)

        def hs(h):
            return slice(h * P, (h + 1) * P)

        pe.wait_ge(consts_here.sem, 32)
        pe.wait_ge(rows_here.sem, 16 * N_ROW_LOADS)
        pe.transpose(PS[:, 0, 0:R_N], rows[0:R_N, :], ident[0:R_N, 0:R_N]).then_inc(rows_T.sem, 1)
        pe.wait_ge(table_here.sem, 17)
        for g in range(GROUPS):
            ins = pe.matmul(PS[0:H, 1 + g, 0:DIST], table[:, g * H:(g + 1) * H], picks[:, g, :],
                            start=True, stop=True)
        ins.then_inc(by_dist_done.sem, 1)

        def spread_bias():
            pe.wait_ge(ab_read.sem, ab_read.at(0))
            pe.wait_ge(by_dist_kept.sem, 1)
            pe.wait_ge(hankel_here.sem, 16)
            for n in range(6):
                if n >= 3:
                    pe.wait_ge(bias_kept.sem, n - 2)
                ins = mm(PS[:, 4 + n % 3, :], consts[:, K_FLIP, :],
                         hankel[:, 2 * n:2 * n + 2, :].rearrange("p a b -> p (a b)"))
                ins.then_inc(bias_done.sem, 1)

        def mixer(L):
            pe.wait_ge(norm_made.sem, norm_made.at(L, 1))
            turn_input(hn, 0, L)
            for g in range(3):
                pair = g % 2
                if g == 0 and L == 0:
                    pe.wait_ge(rows_kept.sem, 1)
                    pe.wait_ge(by_dist_kept.sem, 1)
                if g == 2:
                    pe.wait_ge(a_raw.sem, a_raw.at(L, 1))
                group_T(pair)
                if g == 0:
                    pe.wait_ge(ab_split.sem, 2)
                    for t in range(TT):
                        for k in range(KT):
                            c = slice(t * P, (t + 1) * P)
                            ins = products(PS[:, 4, 8 * t:8 * t + 8], actT_hi[:, k, c], actT_lo[:, k, c],
                                           ab_hi[:, L, k, :], ab_lo[:, L, k, :], first=k == 0, last=k == KT - 1)
                    ins.then_inc(ab_done.sem, 1)
                if g == 1 and L == 0:
                    spread_bias()
            pe.wait_ge(a_raw.sem, a_raw.at(L, 3))
            group_nat(1)
            pe.wait_ge(*((ab_read.sem, ab_read.at(L)) if L else (bias_kept.sem, 4)))
            pe.wait_ge(a_g.sem, a_g.at(L))
            mm(PS[:, 4, 0:H], gt, a_s[:, 8, 0:H])
            mm(PS[:, 4, H:2 * H], le, a_s[:, 8, H:2 * H]).then_inc(a_cum.sem, 1)
            pe.wait_ge(a_raw.sem, a_raw.at(L, 5))
            group_T(0)
            pe.wait_ge(gate_made.sem, gate_made.at(L, 0))
            group_T(1)
            pe.wait_ge(gate_made.sem, gate_made.at(L, 1))
            group_nat(0)
            pe.wait_ge(bf_read.sem, bf_read.at(L))
            group_nat(1)
            deltanet(L)
            hgrn(L)
            dilated(L)
            branches(L)
            pe.wait_ge(mix_made.sem, mix_made.at(L, 5))
            turn_input(mix, 4, L)
            for half in range(2):
                group_nat(half)

        def deltanet(L):
            fwd_bank = (4, 5, 6, 7, 0, 1)
            pe.wait_ge(a_silu.sem, a_silu.at(L, 2))
            for c in range(TT):
                for g in range(3):
                    b = fwd_bank[3 * c + g]
                    if c == 0 and g == 0:
                        pe.wait_ge(a_cum_e.sem, a_cum_e.at(L))
                        if L == 0:
                            pe.wait_ge(bias_kept.sem, 6)
                    if b == 0:
                        pe.wait_ge(gate_made.sem, gate_made.at(L, 2))
                    heads(lambda h: pe.transpose(PS[:, b, hs(h)], a_act[:, g * H + h, c * P:(c + 1) * P], ident)).then_inc(a_fwd.sem, 1)
            for n, (made, c, src, b) in enumerate(((a_qn, 0, t_x, 2), (a_qn, 1, t_x, 3),
                                                   (a_kn, 0, k_nat, 6), (a_kn, 1, k_nat, 1))):
                free, k = (gate_tanh, 2) if n < 2 else (a_v, n - 2)
                pe.wait_ge(free.sem, free.at(L, k))
                pe.wait_ge(made.sem, made.at(L, c))
                heads(lambda h: pe.transpose(PS[:, b, hs(h)], src[:, c, h, :], ident)).then_inc(a_back.sem, 1)
            for n, (b, lhs, rhs) in enumerate(((4, le, t_m), (5, le, t_m), (7, gt, t_n), (0, gt, t_n))):
                pe.wait_ge(a_seg.sem, a_seg.at(L, n // 2))
                mm(PS[:, b, :], lhs, rhs[:, n % 2].rearrange("p h j -> p (h j)")).then_inc(a_dec.sem, 1)
            qT, kT = a_act[:, 0:H, :], a_act[:, H:2 * H, :]
            pe.wait_ge(a_T.sem, a_T.at(L, 3))
            for n, (b, c, rhs) in enumerate(((2, 0, kT), (3, 1, kT), (6, 0, qT), (1, 1, qT))):
                heads(lambda h: mm(PS[:, b, hs(h)], kT[:, h, c * P:(c + 1) * P], rhs[:, h, c * P:(c + 1) * P])).then_inc(a_kk.sem, 1)
            for c in range(TT):
                pe.wait_ge(a_exp.sem, a_exp.at(L, c))
                pe.wait_ge(a_M.sem, a_M.at(L, c))
                heads(lambda h: pe.transpose(PS[:, 4 + c, hs(h)], t_m[:, c, h, :], ident)).then_inc(a_N.sem, 1)
            for lv in range(1, LEVELS):
                for c in range(TT):
                    pe.wait_ge(a_No.sem, a_No.at(L, lv - 1))
                    pe.wait_ge(a_X.sem, a_X.at(L, 2 * lv - 3 + c if lv > 1 else 0))
                    heads(lambda h: mm(PS[:, 4 + c, hs(h)], t_w[:, c, h, :], t_x[:, c, h, :])).then_inc(a_P.sem, 1)
                for c in range(TT):
                    pe.wait_ge(a_Pc.sem, a_Pc.at(L, 2 * (lv - 1) + c))
                    pe.wait_ge(a_Y.sem, a_Y.at(L, 2 * lv - 3 + c if lv > 1 else 0))
                    if lv < LEVELS - 1:
                        heads(lambda h: mm(PS[:, 6 + c, hs(h)], t_y[:, c, h, :], t_m[:, c, h, :])).then_inc(a_XP.sem, 1)
                    heads(lambda h: mm(PS[:, c, hs(h)], t_m[:, c, h, :], t_y[:, c, h, :])).then_inc(a_YP.sem, 1)
            pe.wait_ge(a_r0.sem, a_r0.at(L))
            pe.wait_ge(a_Y.sem, a_Y.at(L, 11))
            heads(lambda h: mm(PS[:, 4, hs(h)], t_y[:, 0, h, :], t_w[:, 0, h, :])).then_inc(a_vn.sem, 1)
            pe.wait_ge(a_vc.sem, a_vc.at(L, 0))
            pe.wait_ge(a_kg.sem, a_kg.at(L))
            heads(lambda h: mm(PS[:, 5, hs(h)], t_v[:, 0, h, :], t_x[:, 0, h, :])).then_inc(a_S.sem, 1)
            pe.wait_ge(a_attn.sem, a_attn.at(L, 1))
            heads(lambda h: mm(PS[:, 2, hs(h)], attn[:, 0, h, :], t_x[:, 0, h, :])).then_inc(a_o.sem, 1)
            pe.wait_ge(a_Sc.sem, a_Sc.at(L))
            heads(lambda h: mm(PS[:, 6, hs(h)], kT[:, h, P:T], t_x[:, 1, h, :])).then_inc(a_kS.sem, 1)
            heads(lambda h: mm(PS[:, 7, hs(h)], qT[:, h, P:T], t_x[:, 1, h, :])).then_inc(a_qS.sem, 1)
            pe.wait_ge(a_r1.sem, a_r1.at(L))
            pe.wait_ge(a_Y.sem, a_Y.at(L, 12))
            heads(lambda h: mm(PS[:, 4, hs(h)], t_y[:, 1, h, :], t_w[:, 1, h, :])).then_inc(a_vn.sem, 1)
            pe.wait_ge(a_vc.sem, a_vc.at(L, 1))
            heads(lambda h: mm(PS[:, 3, hs(h)], attn[:, 1, h, :], t_m[:, 0, h, :])).then_inc(a_o.sem, 1)
            turn_output(L, 0, t_n)

        def turn_output(L, br, src):
            pe.wait_ge(o_made.sem, o_made.at(L, br))
            for h in range(H):
                for t in range(TT):
                    a = src[:, t, h, :] if len(src.shape) == 4 else src[:, t, hs(h)]
                    ins = pe.transpose(PS[:, 4 + h // 2, ((h % 2) * TT + t) * P:((h % 2) * TT + t + 1) * P],
                                       a, ident)
                if h % 2:
                    ins.then_inc(o_T.sem, 1)

        def hgrn(L):
            for n in range(LEVELS + 2):
                pe.wait_ge(b_qk.sem, b_qk.at(L, n))
                if n == LEVELS + 1:
                    heads(lambda h: mm(PS[:, 0, hs(h)], b_ke[:, h, 0:P], b_qe[:, h, P:T])).then_inc(b_att.sem, 1)
                    continue
                pair = (4, 6)[n % 2]
                k, q = (b_ke, b_qe) if n else (b_k, b_q)
                for c in range(TT):
                    for h in range(H):
                        t = slice(c * P, (c + 1) * P)
                        ins = mm(PS[:, pair + c, hs(h)], k[:, h, t], q[:, h, t])
                ins.then_inc(b_att.sem, 1)
            pe.wait_ge(b_masked.sem, b_masked.at(L, LEVELS + 1))
            for h in range(H):
                mm(PS[:, 2, hs(h)], b_attn[:, 0, h, :], b_i[:, 0, hs(h)])
                mm(PS[:, 3, hs(h)], b_attn[:, 1, h, :], b_i[:, 1, hs(h)], last=False)
                ins = mm(PS[:, 3, hs(h)], b_attn[:, 2, h, :], b_i[:, 0, hs(h)], first=False)
            ins.then_inc(b_od.sem, 1)
            turn_output(L, 1, b_o)

        def dilated(L):
            pe.wait_ge(oT_made.sem, oT_made.at(L, 1))
            with prog.loop(pe, GROUPS, 0) as g:
                pe.wait_ge(c_nm.sem, c_nm.count(L * 6 + 2 * g))
                group_nat(0)
                group_nat(1)

                def turn_c(j):
                    pe.wait_ge(c_nm.sem, c_nm.count(L * 6 + 2 * g + j + 1))
                    pe.wait_ge(c_Te.sem, c_Te.count(L * 6 + 2 * g + j))
                    for h in range(H):
                        for t in range(TT):
                            ins = pe.transpose(PS[:, 4 + h // 2, ((h % 2) * TT + t) * P:((h % 2) * TT + t + 1) * P],
                                               c_n[:, t, hs(h)], ident)
                    ins.then_inc(c_Td.sem, 1)

                turn_c(0)
                pe.wait_ge(c_vc.sem, c_vc.count(L * 3 + g))
                group_nat(3)
                turn_c(1)
            pe.wait_ge(c_nm.sem, c_nm.at(L, 5))
            pe.wait_ge(c_vc.sem, c_vc.at(L, 2))
            pe.wait_ge(c_Te.sem, c_Te.at(L, 5))
            def scores(n):
                t, h = divmod(n, H)
                b = 2 * (n % 2)
                keys = (t + 1) * P
                if n >= 2:
                    pe.wait_ge(c_sm.sem, c_sm.at(L, n - 2))
                for g in range(GROUPS):
                    out = PS[:, b + g // 2, (g % 2) * T:(g % 2) * T + keys]
                    ins = mm(out, c_qT[:, g * H + h, t * P:(t + 1) * P], c_kT[:, g * H + h, 0:keys])
                ins.then_inc(c_sd.sem, 1)

            def values(n):
                t, h = divmod(n, H)
                tiles = [(g, s) for g in range(GROUPS) for s in range(t + 1)]
                pe.wait_ge(c_e.sem, c_e.at(L, n))
                for m, (g, s) in enumerate(tiles):
                    at = g * T + s * P
                    ins = pe.transpose(PS[:, 4 + m // 4, (m % 4) * P:(m % 4 + 1) * P], c_p[:, at:at + P], ident)
                ins.then_inc(c_Pd.sem, 1)
                if n >= 2:
                    pe.wait_ge(c_oc.sem, c_oc.at(L, n - 2))
                pe.wait_ge(c_PTc.sem, c_PTc.at(L, n))
                for m, (g, s) in enumerate(tiles):
                    ins = mm(PS[:, 6 + n % 2, 0:P], c_pT[:, m * P:(m + 1) * P], c_v[:, s, g, hs(h)],
                             first=m == 0, last=m == len(tiles) - 1)
                ins.then_inc(c_od.sem, 1)

            scores(0)
            for n in range(TT * H):
                if n + 1 < TT * H:
                    scores(n + 1)
                values(n)
            turn_output(L, 2, c_o)

        def branches(L):
            with prog.loop(pe, 3, 0) as br:
                pe.wait_ge(g_prod_made.sem, g_prod_made.count(L * 6 + 2 * br))
                for half in range(2):
                    pe.wait_ge(g_tanh.sem, g_tanh.count(L * 6 + 2 * br + half))
                    group_nat(0)
                    if half == 0:
                        pe.wait_ge(o_lo_made.sem, L * 3 + br + 1)
                    pe.wait_ge(g_prod_made.sem, g_prod_made.count(L * 6 + 2 * br + half))
                    group_nat(1, o_hi, o_lo, halves=1)
            pe.wait_ge(g_prod_made.sem, g_prod_made.at(L, 5))

        def dense():
            pe.wait_ge(norm_made.sem, norm_made.at(0, 3))
            turn_input(fn, 8, 0)

            def up(m, s):
                pe.wait_ge(f_gm.sem, f_gm.count(m - 1))
                for w in range(2):
                    w_hi, w_lo = unit_ready()
                    for j in range(2):
                        for k in range(KT):
                            c = slice(j * P, (j + 1) * P)
                            ins = products(PS[:, 2 * s + j, w * T:(w + 1) * T],
                                           unit_view(w_hi, 8)[:, k, c], unit_view(w_lo, 8)[:, k, c],
                                           actT_hi[:, k, :], actT_lo[:, k, :], first=k == 0, last=k == KT - 1)
                    unit_over(ins)

            def down(m, s, first=False, last=False):
                pe.wait_ge(f_lo.sem, f_lo.count(m + 1))
                w_hi, w_lo = unit_ready()
                for t in range(TT):
                    for half in range(2):
                        for k in range(2):
                            c, d = slice(t * P, (t + 1) * P), slice(half * 512, (half + 1) * 512)
                            ins = products(PS[:, 4 + 2 * t + half, :], fT_hi[s][:, k, c], fT_lo[s][:, k, c],
                                           unit_view(w_hi, 2)[:, k, d], unit_view(w_lo, 2)[:, k, d],
                                           first=first and k == 0, last=last and k == 1)
                unit_over(ins)

            up(0, 0)
            up(1, 1)
            down(0, 0, first=True)
            with prog.loop(pe, STEPS_DENSE // 2 - 1, 0) as i:
                m = 2 * i + 2
                up(m, 0)
                down(m - 1, 1)
                up(m + 1, 1)
                down(m, 0)
            up(STEPS_DENSE - 1, 0)
            down(STEPS_DENSE - 2, 1)
            down(STEPS_DENSE - 1, 0, last=True)

        def gather(n):
            pe.wait_ge(pick_made.sem, n + 1)
            for k in range(KT):
                for t in range(TT):
                    for part, src in enumerate((fn_hi, fn_lo)):
                        ins = pe.matmul(PS[:, 6 + k // 4, (k % 4) * P:(k % 4 + 1) * P],
                                        src[:, t, k * P:(k + 1) * P], pick_r[:, t, :],
                                        start=t == 0 and part == 0, stop=t == 1 and part == 1)
                if k % 4 == 3:
                    ins.then_inc(e_done.sem, 1)

        def scatter(n):
            pe.wait_ge(pickT_made.sem, n + 1)
            pe.wait_ge(y_lo_made.sem, y_lo_made.count(n + 1))
            for t in range(TT):
                for half in range(2):
                    for part, src in enumerate((y_hi, y_lo)):
                        ins = pe.matmul(PS[:, 4 + 2 * t + half, :], pickT[:, t, :],
                                        src[:, half * 512:(half + 1) * 512], start=part == 0, stop=part == 1)
                ins.then_inc(s_done.sem, 1)

        def expert(n, first, last):
            base = STEPS_DENSE + STEPS_EXPERT * n

            def up(m, s):
                pe.wait_ge(f_gm.sem, f_gm.count(m - 1))
                for w in range(2):
                    w_hi, w_lo = unit_ready()
                    for k in range(KT):
                        ins = products(PS[:, s, w * SUB:(w + 1) * SUB], e_hi[:, k, :], e_lo[:, k, :],
                                       unit_view(w_hi, 8)[:, k, :], unit_view(w_lo, 8)[:, k, :],
                                       first=k == 0, last=k == KT - 1)
                    unit_over(ins)

            def turn(m, s):
                pe.wait_ge(f_gm.sem, f_gm.count(m + 1))
                for j in range(2):
                    ins = pe.transpose(PS[:, 2, (2 * s + j) * P:(2 * s + j + 1) * P],
                                       f_g[s][:, j * P:(j + 1) * P], ident)
                ins.then_inc(f_gT.sem, 1)

            def down(m, s, first=False, last=False):
                pe.wait_ge(f_lo.sem, f_lo.count(m + 1))
                w_hi, w_lo = unit_ready()
                for half in range(2):
                    for k in range(2):
                        d = slice(half * 512, (half + 1) * 512)
                        ins = products(PS[:, 4 + half, :], fT_hi[s][:, k, 0:P], fT_lo[s][:, k, 0:P],
                                       unit_view(w_hi, 2)[:, k, d], unit_view(w_lo, 2)[:, k, d],
                                       first=first and k == 0, last=last and k == 1)
                unit_over(ins)

            pe.wait_ge(e_lo_made.sem, e_lo_made.count(2 * n + 2))
            up(base, 0)
            if not first:
                scatter(n - 1)
            for t in range(TT):
                ins = pe.transpose(PS[:, 3, t * P:(t + 1) * P], pick[:, t, :], ident)
            ins.then_inc(pickT_done.sem, 1)
            turn(base, 0)
            up(base + 1, 1)
            if not first:
                pe.wait_ge(s_read.sem, s_read.count(2 * n - 1))
            down(base, 0, first=True)
            turn(base + 1, 1)
            with prog.loop(pe, STEPS_EXPERT // 2 - 1, 0) as i:
                m = base + 2 + 2 * i
                up(m, 0)
                down(m - 1, 1)
                turn(m, 0)
                up(m + 1, 1)
                down(m, 0)
                turn(m + 1, 1)
            if not last:
                if not first:
                    pe.wait_ge(s_read.sem, s_read.count(2 * n))
                gather(n + 1)
            down(base + STEPS_EXPERT - 1, 1, last=True)

        def experts(turn):
            if turn:
                pe.wait_ge(s_read.sem, s_read.count(2 * E * turn))
            gather(E * turn)
            expert(E * turn, True, False)
            with prog.loop(pe, E - 2, 0, rounds=EXPERT_R) as e:
                expert(E * turn + 1 + e, False, False)
            expert(E * turn + E - 1, False, True)
            scatter(E * turn + E - 1)

        def moe():
            pe.wait_ge(norm_made.sem, norm_made.at(1, 3))
            turn_input(fn, 8, 1)
            for t in range(TT):
                for k in range(KT):
                    c = slice(t * P, (t + 1) * P)
                    ins = products(PS[:, 0, 8 * t:8 * t + 8], actT_hi[:, k, c], actT_lo[:, k, c],
                                   ab_hi[:, 2, k, :], ab_lo[:, 2, k, :], first=k == 0, last=k == KT - 1)
            ins.then_inc(r_done.sem, 1)
            pe.wait_ge(r_sel.sem, 1)
            mm(PS[:, 1, 0:E], le, r_t[:, 12, 0:E])
            mm(PS[:, 1, E:2 * E], le, r_t[:, 12, E:2 * E], last=False)
            mm(PS[:, 1, E:2 * E], ones, r_t[:, 12, 0:E], first=False)
            mm(PS[:, 1, 2 * E:3 * E], ones, r_t[:, 12, 0:E], last=False)
            mm(PS[:, 1, 2 * E:3 * E], ones, r_t[:, 12, E:2 * E], first=False).then_inc(r_cnt.sem, 1)
            experts(0)
            more = second_turn(pe, prog)
            with pe.If(more > 0):
                experts(1)

        mixer(0)
        dense()
        mixer(1)
        moe()

    @block.scalar
    def _(act):
        prog = Program(act_step)
        for sig in (c_Te, c_vc, g_tanh):
            act.sem_inc(sig.sem, sig.ahead)
        SQ, EXP, LN, TANH, COPY, SILU = (ACT.Square, ACT.Exp, ACT.Ln, ACT.Tanh, ACT.Copy, ACT.Silu)

        def prep(count):
            for _ in range(count):
                slot = prog.u % RAW
                arrived = 16 * (prog.u // RAW + 1)
                act.wait_ge(raw_full[slot].sem, arrived if prog.rounds is None else arrived + prog.rounds * 16)
                if prog.u >= SPLIT:
                    act.wait_ge(unit_used.sem, prog.unit(1 - SPLIT))
                act.activation(hi[prog.u % SPLIT][:, :], raw[slot][:, :], COPY).then_inc(hi_made.sem, 1)
                prog.u += 1

        def used(L, n):
            act.wait_ge(unit_used.sem, LAYER_U[L] + n)

        def rsqrt_of(out, in_, scale, bias_out, sig):
            act.activation(out, in_, LN, bias=eps_t, scale=scale).then_inc(act_step.sem, 1)
            act.wait_ge(act_step.sem, prog.step())
            act.activation(out, out, EXP, bias=bias_out, scale=-0.5).then_inc(sig.sem, 1)

        act.wait_ge(tiny_made.sem, 4)
        act.wait_ge(rows_T.sem, 1)
        act.activation(small[:, :], PS[:, 0, 0:R_N], COPY).then_inc(rows_kept.sem, 1)
        act.wait_ge(rows_kept.sem, 1)
        act.wait_ge(lb_m.sem, 1)
        act.activation(lb[:, 4:6, :], lb[:, 4:6, :], EXP).then_inc(lb_e.sem, 1)
        act.wait_ge(par_here.sem, 32)
        act.activation(a_rate[:, :, :], a_par[:, 0, :, :], EXP).then_inc(a_rate_e.sem, 1)
        act.wait_ge(by_dist_done.sem, 1)
        act.activation(by_dist[:, :, :], PS[0:H, 1:1 + GROUPS, 0:DIST], COPY).then_inc(by_dist_kept.sem, 1)
        act.wait_ge(ab_here.sem, 48)
        act.activation(ab_hi[:, :, :, :], ab[:, :, :, :], COPY).then_inc(ab_split.sem, 1)

        def norm_scale(L, phase):
            if L == 0 and phase == 0:
                act.wait_ge(x_here.sem, 32)
            else:
                act.wait_ge(x_made.sem, x_made.at(L if phase else L - 1, 1 if phase else 2))
            dst = fn if phase else hn
            for t in range(TT):
                act.activation(dst[:, t, :], x[:, t, :], SQ, accum_out=stat[:, t:t + 1]).then_inc(act_step.sem, 1)
                act.wait_ge(act_step.sem, prog.step())
            act.activation(stat[:, 2:4], stat[:, 0:2], LN, bias=eps_t, scale=1.0 / D).then_inc(act_step.sem, 1)
            act.wait_ge(act_step.sem, prog.step())
            act.activation(stat[:, 4:6], stat[:, 2:4], EXP, scale=-0.5).then_inc(norm_r.sem, 1)

        def turn_input(idx, L, scale=1.0):
            for j in range(4):
                act.wait_ge(turned.sem, turned.at(L, idx + j))
                act.activation(actT_hi[:, 2 * j:2 * j + 2, :].rearrange("p a b -> p (a b)"),
                               PS[:, 4 + j, :], COPY, scale=scale).then_inc(actT_hi_made.sem, 1)

        def mixer(L):
            if L:
                prep(2)
            norm_scale(L, 0)
            prep(1 if L else 3)
            turn_input(0, L)

            def conv_in(g):
                used(L, 2 * g + 2)
                if g == 0:
                    act.wait_ge(pad_made.sem, L + 1)
                for b in range(2):
                    ct = g * H + 2 * b
                    act.activation(a_in[:, ct:ct + 2, 3:3 + T],
                                   PS[:, 2 * (g % 2) + b, :].rearrange("p (a b) -> p a b", a=2), COPY).then_inc(a_raw.sem, 1)

            def conv_tanh(g):
                act.wait_ge(a_conv.sem, a_conv.at(L, g))
                act.activation((t_x, t_y, t_w)[g][:, :, :, :].rearrange("p a b c -> p (a b c)"),
                               a_act[:, g * H:(g + 1) * H, :].rearrange("p a b -> p (a b)"), TANH, scale=0.5).then_inc(a_tanh.sem, 1)

            prep(2)
            conv_in(0)
            act.wait_ge(ab_read.sem, ab_read.at(L))
            act.activation(a_s[:, 3, :], a_s[:, 2, :], EXP, scale=-1.0).then_inc(act_step.sem, 1)
            act.wait_ge(act_step.sem, prog.step())
            act.activation(a_s[:, 5, :], a_s[:, 4, :], EXP, scale=-1.0).then_inc(a_e1.sem, 1)
            act.wait_ge(a_e1.sem, a_e1.at(L))
            act.activation(a_s[:, 6, :], a_s[:, 5, :], LN, bias=one_t).then_inc(a_e2.sem, 1)
            prep(2)
            conv_in(1)
            if L == 0:
                for n in range(6):
                    act.wait_ge(bias_done.sem, n + 1)
                    act.activation(bias[:, 2 * n:2 * n + 2, :].rearrange("p a b -> p (a b)"),
                                   PS[:, 4 + n % 3, :], COPY).then_inc(bias_kept.sem, 1)
            conv_tanh(0)
            prep(2)
            conv_in(2)
            conv_tanh(1)
            prep(2)
            used(L, 8)
            conv_tanh(2)
            act.activation(t_v[:, :, :, :].rearrange("p a b c -> p (a b c)"),
                           PS[:, 2:4, :].rearrange("p a b -> p (a b)"), TANH, scale=0.5).then_inc(gate_tanh.sem, 1)
            act.wait_ge(a_cum.sem, a_cum.at(L))
            act.activation(a_s[:, 11, :], PS[:, 4, 0:2 * H], EXP).then_inc(a_cum_e.sem, 1)
            prep(2)
            used(L, 10)
            act.activation(b_q[:, :, :].rearrange("p a b -> p (a b)"),
                           PS[:, 0:2, :].rearrange("p a b -> p (a b)"), TANH, scale=0.5).then_inc(gate_tanh.sem, 1)
            prep(2)
            act.wait_ge(bf_read.sem, bf_read.at(L))
            bf = b_f[:, :, :].rearrange("p a b -> p (a b)")
            act.activation(bf, bf, EXP, scale=-1.0).then_inc(act_step.sem, 1)
            act.wait_ge(act_step.sem, prog.step())
            act.activation(bf, bf, LN, bias=one_t).then_inc(act_step.sem, 1)
            act.wait_ge(act_step.sem, prog.step())
            act.activation(bf, bf, EXP, scale=-1.0).then_inc(bf_s.sem, 1)
            prep(2)
            used(L, 14)
            act.wait_ge(a_conv.sem, a_conv.at(L, 2))
            act.wait_ge(gate_made.sem, gate_made.at(L, 1))
            act.activation(b_i[:, :, :].rearrange("p a b -> p (a b)"),
                           PS[:, 0:2, :].rearrange("p a b -> p (a b)"), COPY).then_inc(gate_made.sem, 1)
            prep(2)
            used(L, 16)
            act.activation(b_gate[:, :, :].rearrange("p a b -> p (a b)"),
                           PS[:, 2:4, :].rearrange("p a b -> p (a b)"), TANH, scale=0.5).then_inc(gate_tanh.sem, 1)
            deltanet(L)
            hgrn(L)
            dilated(L)
            branches(L)
            turn_input(4, L)
            prep(1)

        def flat(t):
            return t[:, :, :, :].rearrange("p a b c -> p (a b c)") if len(t.shape) == 4 else \
                t[:, :, :].rearrange("p a b -> p (a b)")

        def bank(*b):
            return PS[:, b[0], :] if len(b) == 1 else PS[:, b[0]:b[1] + 1, :].rearrange("p a b -> p (a b)")

        def chunk(t, c):
            return t[:, c].rearrange("p h j -> p (h j)")

        def deltanet(L):
            for c in range(TT):
                for g, dst in ((0, t_w), (1, t_v)):
                    act.wait_ge(a_fwd.sem, a_fwd.at(L, 3 * c + g))
                    act.activation(chunk(dst, c), bank((4, 5, 6, 7, 0, 1)[3 * c + g]), SQ).then_inc(a_sq.sem, 1)
                act.wait_ge(a_fwd.sem, a_fwd.at(L, 3 * c + 2))
                act.activation(chunk(v_nat, c), bank((6, 1)[c]), COPY).then_inc(a_v.sem, 1)
            act.wait_ge(a_ss.sem, a_ss.at(L))
            act.activation(a_s[:, 13:15, :], a_s[:, 9:11, :], LN, bias=eps_t).then_inc(act_step.sem, 1)
            act.wait_ge(act_step.sem, prog.step())
            act.activation(a_s[:, 15, :], a_s[:, 13, :], EXP, bias=lnq_t, scale=-0.5).then_inc(act_step.sem, 1)
            act.wait_ge(act_step.sem, prog.step())
            act.activation(a_s[:, 16, :], a_s[:, 14, :], EXP, scale=-0.5).then_inc(a_r.sem, 1)
            for n, (b, ct, c) in enumerate(((2, 0, 0), (3, 0, 1), (6, H, 0), (1, H, 1))):
                act.wait_ge(a_back.sem, a_back.at(L, n))
                act.activation(a_act[:, ct:ct + H, c * P:(c + 1) * P],
                               bank(b).rearrange("p (h j) -> p h j", h=H), COPY).then_inc(a_T.sem, 1)
            for n, (b, dst) in enumerate(((4, t_x), (5, t_x), (7, t_y), (0, t_y))):
                act.wait_ge(a_dec.sem, a_dec.at(L, n))
                act.activation(chunk(dst, n % 2), bank(b), EXP).then_inc(a_exp.sem, 1)
            for c in range(TT):
                act.wait_ge(a_N.sem, a_N.at(L, c))
                act.activation(chunk(t_n, c), bank(4 + c), COPY).then_inc(a_Nc.sem, 1)
            for lv in range(1, LEVELS):
                for c in range(TT):
                    act.wait_ge(a_P.sem, a_P.at(L, 2 * (lv - 1) + c))
                    act.activation(chunk(t_m, c), bank(4 + c), COPY).then_inc(a_Pc.sem, 1)
            act.wait_ge(a_vn.sem, a_vn.at(L, 0))
            act.activation(chunk(t_x, 0), bank(4), COPY).then_inc(a_vc.sem, 1)
            act.wait_ge(a_S.sem, a_S.at(L))
            act.activation(chunk(t_x, 1), bank(5), COPY).then_inc(a_Sc.sem, 1)
            act.wait_ge(a_o.sem, a_o.at(L, 0))
            act.activation(chunk(t_n, 0), bank(2), COPY).then_inc(a_oc.sem, 1)
            act.wait_ge(a_vn.sem, a_vn.at(L, 1))
            act.activation(chunk(t_m, 0), bank(4), COPY).then_inc(a_vc.sem, 1)
            output_norm(L, 0, t_n, t_y, a_oc)
            turn_output(L, 0)

        def output_norm(L, br, src, tmp, made):
            act.wait_ge(made.sem, made.at(L, made.per_layer - 1))
            act.activation(flat(tmp), flat(src), SQ).then_inc(o_sq.sem, 1)
            act.wait_ge(o_ss.sem, o_ss.at(L, br))
            act.activation(a_s[:, 18, :], a_s[:, 17, :], LN, bias=eps_t, scale=1.0 / P).then_inc(act_step.sem, 1)
            act.wait_ge(act_step.sem, prog.step())
            act.activation(a_s[:, 19, :], a_s[:, 18, :], EXP, scale=-0.5).then_inc(o_r.sem, 1)

        def turn_output(L, br):
            act.wait_ge(o_T.sem, o_T.at(L, 2 * br + 1))
            col = (R_GA + L, R_GB + L, None)[br]
            act.activation(oT[:, br, :, :].rearrange("p a b -> p (a b)"), bank(4, 5), COPY,
                           scale=1.0 if col is None else small[:, col:col + 1]).then_inc(oT_made.sem, 1)

        def hgrn(L):
            act.wait_ge(b_clamp.sem, b_clamp.at(L))
            act.activation(flat(b_f), flat(b_f), LN).then_inc(b_g.sem, 1)
            for n in range(LEVELS + 1):
                s = 1 << n
                act.wait_ge(b_diff.sem, b_diff.at(L, n))
                v = flat(b_e).rearrange("p (n s) -> p n s", s=2 * s)
                act.activation(v[:, :, s:2 * s], v[:, :, s:2 * s], EXP).then_inc(act_step.sem, 1)
                act.wait_ge(act_step.sem, prog.step())
                act.activation(v[:, :, 0:s], v[:, :, 0:s], EXP, scale=-1.0).then_inc(b_exp.sem, 1)
            act.wait_ge(b_od.sem, b_od.at(L))
            act.activation(flat(b_o), bank(2, 3), COPY).then_inc(b_oc.sem, 1)
            output_norm(L, 1, b_o, b_o2, b_oc)
            turn_output(L, 1)

        def dilated(L):
            with prog.loop(act, GROUPS, 2) as g:
                u = LAYER_U[L] + U_C + 6 * g

                def square(j):
                    act.wait_ge(unit_used.sem, u + 2 * j + 2)
                    act.wait_ge(c_ss.sem, c_ss.count(L * 6 + 2 * g + j))
                    act.activation(flat(c_sq), bank(2 * j, 2 * j + 1), SQ).then_inc(c_sqd.sem, 1)
                    act.wait_ge(c_ss.sem, c_ss.count(L * 6 + 2 * g + j + 1))
                    rsqrt_of(stat[:, 8:16], stat[:, 0:8], 1.0 / P, zero_t, c_r)

                def turned_c(j):
                    act.wait_ge(c_Td.sem, c_Td.count(L * 6 + 2 * g + j + 1))
                    dst = (c_qT, c_kT)[j]
                    col = (R_QN, R_KN)[j] + L * GROUPS
                    act.activation(dst[:, bass.ds(g * H, H), :].rearrange("p a b -> p (a b)"), bank(4, 5),
                                   COPY, scale=small[:, bass.ds(g + col, 1)]).then_inc(c_Te.sem, 1)

                prep(2)
                square(0)
                prep(2)
                turned_c(0)
                square(1)
                prep(2)
                act.wait_ge(unit_used.sem, u + 6)
                act.activation(c_v[:, :, bass.ds(g, 1), :].rearrange("p t o n -> p t (o n)"),
                               PS[:, 6:8, :], COPY).then_inc(c_vc.sem, 1)
                turned_c(1)
            def copies(n):
                act.wait_ge(c_Pd.sem, c_Pd.at(L, n))
                if n:
                    act.wait_ge(c_od.sem, c_od.at(L, n - 1))
                w = GROUPS * (n // H + 1) * P
                act.activation(c_pT[:, 0:w], PS[:, 4:6, :].rearrange("p a b -> p (a b)")[:, 0:w], COPY).then_inc(c_PTc.sem, 1)

            for n in range(TT * H):
                t = n // H
                keys = (t + 1) * P
                act.wait_ge(c_mx.sem, c_mx.at(L, n))
                if n:
                    act.wait_ge(c_Pd.sem, c_Pd.at(L, n - 1))
                act.activation(c_p[:, :].rearrange("p (g s) -> p g s", g=GROUPS)[:, :, 0:keys],
                               c_s[:, :].rearrange("p (g s) -> p g s", g=GROUPS)[:, :, 0:keys],
                               EXP, bias=stat[:, 1:2], accum_out=stat[:, 2:3]).then_inc(c_e.sem, 1)
                copies(n)
            turn_output(L, 2)

        def branches(L):
            act.wait_ge(oT_made.sem, oT_made.at(L, 2))
            with prog.loop(act, 3, 0) as br:
                u = LAYER_U[L] + U_BR + 6 * br
                act.wait_ge(unit_used.sem, u)
                act.activation(flat(o_hi), oT[:, bass.ds(br, 1), :, :].rearrange("p o a b -> p (o a b)"),
                               COPY).then_inc(o_hi_made.sem, 1)

                def gate(half):
                    act.wait_ge(unit_used.sem, u + 3 * half + 2)
                    act.wait_ge(g_prod_made.sem, g_prod_made.count(L * 6 + 2 * br + half))
                    act.activation(flat(g_sig), bank(0, 1), TANH, scale=0.5).then_inc(g_tanh.sem, 1)

                prep(1)
                gate(0)
                prep(3)
                gate(1)
                prep(2)

        def dense():
            prep(2)
            norm_scale(0, 1)
            prep(1)
            turn_input(8, 0)
            U = LAYER_U[0] + U_FF

            def half_step(m, s, used, preps=(1, 2)):
                act.wait_ge(unit_used.sem, used)
                act.wait_ge(f_gm.sem, f_gm.count(m - 1))
                act.activation(f_s[s][:, :].rearrange("p (j t) -> p j t", j=2),
                               PS[:, 2 * s:2 * s + 2, 0:T], SILU).then_inc(f_silu.sem, 1)
                prep(preps[0])
                act.wait_ge(f_gm.sem, f_gm.count(m + 1))
                act.activation(fT_hi[s][:, :, :].rearrange("p a b -> p (a b)"), f_g[s][:, :],
                               COPY).then_inc(f_hi.sem, 1)
                prep(preps[1])

            half_step(0, 0, U + 2)
            with prog.loop(act, STEPS_DENSE // 2 - 1, 0) as i:
                m = 2 * i + 1
                half_step(m, 1, U + 1 + 3 * m)
                half_step(m + 1, 0, U + 4 + 3 * m)
            m = STEPS_DENSE - 2
            half_step(m, 1, U + 1 + 3 * m)
            half_step(m + 1, 0, U + 4 + 3 * m, (0, 0))

        def tokens(n):
            for j in range(2):
                act.wait_ge(e_done.sem, e_done.count(2 * n + j + 1))
                act.activation(e_hi[:, 4 * j:4 * j + 4, :].rearrange("p a b -> p (a b)"), bank(6 + j),
                               COPY).then_inc(e_hi_made.sem, 1)

        def expert(n, U, last):
            base = STEPS_DENSE + STEPS_EXPERT * n

            def silu(m, s, used):
                act.wait_ge(unit_used.sem, used)
                act.wait_ge(f_gm.sem, f_gm.count(m - 1))
                act.activation(f_s[s][:, 0:SUB], PS[:, s, 0:SUB], SILU).then_inc(f_silu.sem, 1)

            def high(m, s):
                act.wait_ge(f_gT.sem, f_gT.count(m - STEPS_DENSE + 1))
                act.activation(fT_hi[s][:, :, 0:P],
                               PS[:, 2, s * SUB:(s + 1) * SUB].rearrange("p (j t) -> p j t", j=2), COPY).then_inc(f_hi.sem, 1)

            silu(base, 0, U + 2)
            prep(1)
            act.wait_ge(pickT_done.sem, pickT_done.count(n + 1))
            act.activation(flat(pickT), PS[:, 3, 0:T], COPY).then_inc(pickT_made.sem, 1)
            high(base, 0)
            prep(2)
            with prog.loop(act, STEPS_EXPERT // 2 - 1, 0) as i:
                for d, s in ((1, 1), (2, 0)):
                    silu(base + 2 * i + d, s, U + 6 * i + 1 + 3 * d)
                    prep(1)
                    high(base + 2 * i + d, s)
                    prep(2)
            m = STEPS_EXPERT - 1
            silu(base + m, 1, U + 1 + 3 * m)
            prep(0 if last else 1)
            high(base + m, 1)
            if not last:
                tokens(n + 1)
                prep(1)
            act.wait_ge(unit_used.sem, U + 3 * STEPS_EXPERT)
            act.activation(y_hi[:, :], bank(4, 5), COPY).then_inc(y_hi_made.sem, 1)
            prep(0 if last else 1)

        def experts(turn):
            U = U_END + E * 3 * STEPS_EXPERT * turn
            tokens(E * turn)
            expert(E * turn, U, False)
            with prog.loop(act, E - 2, 0, rounds=EXPERT_R) as e:
                expert(E * turn + 1 + e, U + (e + 1) * (3 * STEPS_EXPERT), False)
            expert(E * turn + E - 1, U + (E - 1) * 3 * STEPS_EXPERT, True)

        def moe():
            prep(2)
            norm_scale(1, 1)
            prep(1)
            turn_input(8, 1)
            act.wait_ge(norm_made.sem, norm_made.at(1, 3))
            act.activation(flat(fn_hi), flat(fn), COPY).then_inc(fn_hi_made.sem, 1)
            act.wait_ge(r_read.sem, 1)
            act.activation(r_t[:, 10, 0:TT], r_t[:, 9, 0:TT], EXP).then_inc(r_e.sem, 1)
            experts(0)
            more = second_turn(act, prog)
            with act.If(more > 0):
                prep(3)
                experts(1)

        mixer(0)
        dense()
        mixer(1)
        moe()

    @block.vector
    def _(dve):
        prog = Program(dve_step)
        for sig in (c_nm, c_ss, g_prod_made, mix_made, f_gm, f_lo, s_read, e_lo_made, y_lo_made):
            dve.sem_inc(sig.sem, sig.ahead)

        def prep(count):
            for _ in range(count):
                s = prog.u % SPLIT
                dve.wait_ge(hi_made.sem, prog.unit(1))
                dve.tensor_tensor(lo[prog.u % RAW][:, :], raw[prog.u % RAW][:, :], hi[s][:, :].bitcast(F32),
                                  ALU.subtract).then_inc(lo_made.sem, 1)
                prog.u += 1

        def used(L, n):
            dve.wait_ge(unit_used.sem, LAYER_U[L] + n)

        def flat(t):
            return t[:, :, :, :].rearrange("p a b c -> p (a b c)") if len(t.shape) == 4 else \
                t[:, :, :].rearrange("p a b -> p (a b)")

        def flat8(t):
            return t[:, :, :, :].rearrange("p a b c -> p (a b) c") if len(t.shape) == 4 else \
                t[:, :, :].rearrange("p a (b c) -> p (a b) c", c=P)

        def bank(*b):
            return PS[:, b[0], :] if len(b) == 1 else PS[:, b[0]:b[1] + 1, :].rearrange("p a b -> p (a b)")

        def bank4(b):
            return PS[:, b, :].rearrange("p (h j) -> p h j", h=H)

        def tt(out, a, b, op):
            return dve.tensor_tensor(out, a, b, op)

        def half_sigmoid(ap):
            return dve.tensor_scalar(ap, ap, 1.0, 0.5, ALU.add, ALU.mult)

        for n, v in enumerate((EPS, 1.0, math.log(P ** -0.5), 0.0)):
            dve.memset(tiny[:, n:n + 1], v).then_inc(tiny_made.sem, 1)
        dve.memset(ones_t[:, :], 1.0).then_inc(dve_step.sem, 1)
        dve.wait_ge(dve_step.sem, prog.step())
        dve.memset(table[BUCKETS:BUCKETS + 1, :], 1.0).then_inc(table_here.sem, 1)
        dve.wait_ge(rows_kept.sem, 1)
        lbr = small[:, R_LB:R_LB + 2 * H].rearrange("p (l h) -> p l h", l=2)
        tt(lb[:, 2, :], lbr[:, 0, :], lbr[:, 1, :], ALU.max).then_inc(dve_step.sem, 1)
        dve.wait_ge(dve_step.sem, prog.step())
        tt(lb[:, 4:6, :], lbr, over(lb[:, 2, :], 2), ALU.subtract).then_inc(lb_m.sem, 1)
        dve.wait_ge(lb_e.sem, 1)
        tt(lb[:, 2, :], lb[:, 4, :], lb[:, 5, :], ALU.add).then_inc(dve_step.sem, 1)
        dve.wait_ge(dve_step.sem, prog.step())
        dve.reciprocal(lb[:, 3, :], lb[:, 2, :]).then_inc(dve_step.sem, 1)
        dve.wait_ge(dve_step.sem, prog.step())
        tt(lb[:, 4:6, :], lb[:, 4:6, :], over(lb[:, 3, :], 2), ALU.mult).then_inc(dve_step.sem, 1)
        dve.wait_ge(dve_step.sem, prog.step())
        tt(lb[:, 2, :], lb[:, 4, :], lb[:, 5, :], ALU.add).then_inc(dve_step.sem, 1)
        dve.wait_ge(dve_step.sem, prog.step())
        tt(lb[:, 0, :], lb[:, 2, :], lb[:, 4, :], ALU.subtract).then_inc(dve_step.sem, 1)
        dve.wait_ge(dve_step.sem, prog.step())
        dve.tensor_scalar(lb[:, 1, :], lb[:, 0, :], -1.0, 1.0, ALU.mult, ALU.add).then_inc(dve_step.sem, 1)
        dve.wait_ge(dve_step.sem, prog.step())
        dve.wait_ge(a_rate_e.sem, 1)
        dve.tensor_scalar(a_rate[:, :, :], a_rate[:, :, :], -1.0, None, ALU.mult).then_inc(dve_step.sem, 1)
        dve.wait_ge(dve_step.sem, prog.step())
        dve.wait_ge(ab_split.sem, 1)
        tt(ab_lo[:, :, :, :], ab[:, :, :, :], ab_hi[:, :, :, :].bitcast(F32), ALU.subtract).then_inc(ab_split.sem, 1)

        def norm(L, phase):
            src = x
            dst, g = (fn, f_gain) if phase else (hn, gain)
            dve.wait_ge(norm_r.sem, norm_r.at(L, phase))
            dve.wait_ge(gain_here.sem, 16 * (2 * L + phase + 1))
            for t in range(TT):
                dve.scalar_tensor_tensor(dst[:, t, :], src[:, t, :], stat[:, 4 + t:5 + t], g[:, :],
                                         ALU.mult, ALU.mult).then_inc(norm_made.sem, 1)

        def turn_input(idx, L, scale=1.0):
            for j in range(4):
                dve.wait_ge(actT_hi_made.sem, actT_hi_made.at(L, idx + j))
                v = slice(2 * j, 2 * j + 2)
                dve.scalar_tensor_tensor(actT_lo[:, v, :].rearrange("p a b -> p (a b)"), bank(4 + j), scale,
                                         actT_hi[:, v, :].rearrange("p a b -> p (a b)").bitcast(F32),
                                         ALU.mult, ALU.subtract).then_inc(actT_lo_made.sem, 1)

        def mixer(L):
            norm(L, 0)
            prep(1 if L else 3)
            turn_input(0, L)
            dve.memset(a_in[:, :, 0:3], 0.0).then_inc(pad_made.sem, 1)
            dve.wait_ge(pad_made.sem, L + 1)

            def conv(g):
                dve.wait_ge(a_raw.sem, a_raw.at(L, 2 * g + 1))
                if g == 0 and L == 0:
                    dve.wait_ge(rows_kept.sem, 1)
                for tap in range(TAPS):
                    for n in range(H):
                        ct = g * H + n
                        col = R_CONV + (L * TAPS + tap) * CT + ct
                        src, w = a_in[:, ct, tap:tap + T], small[:, col:col + 1]
                        if tap == 0:
                            ins = dve.tensor_scalar(a_act[:, ct, :], src, w, None, ALU.mult)
                        else:
                            ins = dve.scalar_tensor_tensor(a_act[:, ct, :], src, w, a_act[:, ct, :],
                                                           ALU.mult, ALU.add)
                        if tap == TAPS - 1 and n == H - 1:
                            ins.then_inc(a_conv.sem, 1)
                        elif n == H - 1:
                            ins.then_inc(dve_step.sem, 1)
                            dve.wait_ge(dve_step.sem, prog.step())
                        else:
                            ins.then_inc(dve_step.sem, 1)
                            prog.step()

            def silu(g):
                th = (t_x, t_y, t_w)[g]
                act_g = a_act[:, g * H:(g + 1) * H, :].rearrange("p a b -> p (a b)")
                dve.wait_ge(a_tanh.sem, a_tanh.at(L, g))
                half_sigmoid(flat(th)).then_inc(dve_step.sem, 1)
                dve.wait_ge(dve_step.sem, prog.step())
                tt(act_g, act_g, flat(th), ALU.mult).then_inc(a_silu.sem, 1)

            prep(2)
            conv(0)
            dve.wait_ge(ab_done.sem, ab_done.at(L))
            logits = PS[:, 4, 0:16].rearrange("p (t c) -> p t c", t=TT)

            def a8(n):
                return a_s[:, n, :].rearrange("p (t h) -> p t h", t=TT)

            dve.wait_ge(par_here.sem, 32)
            tt(a8(1), logits[:, :, H:2 * H], over(a_par[:, 1, L, :], TT), ALU.add).then_inc(dve_step.sem, 1)
            dve.wait_ge(dve_step.sem, prog.step())
            dve.scalar_tensor_tensor(a_s[:, 4, :], a_s[:, 1, :], -1.0, a_s[:, 1, :], ALU.mult, ALU.max).then_inc(dve_step.sem, 1)
            dve.wait_ge(dve_step.sem, prog.step())
            dve.tensor_copy(a8(2), logits[:, :, 0:H]).then_inc(ab_read.sem, 1)
            dve.wait_ge(ab_read.sem, ab_read.at(L))
            dve.wait_ge(a_e1.sem, a_e1.at(L))
            dve.tensor_scalar(a_s[:, 3, :], a_s[:, 3, :], 1.0, None, ALU.add).then_inc(dve_step.sem, 1)
            dve.wait_ge(dve_step.sem, prog.step())
            dve.reciprocal(a_s[:, 0, :], a_s[:, 3, :]).then_inc(dve_step.sem, 1)
            dve.wait_ge(dve_step.sem, prog.step())
            dve.wait_ge(a_e2.sem, a_e2.at(L))
            dve.tensor_scalar(a_s[:, 7, :], a_s[:, 1, :], 0.0, None, ALU.max).then_inc(dve_step.sem, 1)
            dve.wait_ge(dve_step.sem, prog.step())
            tt(a_s[:, 7, :], a_s[:, 7, :], a_s[:, 6, :], ALU.add).then_inc(dve_step.sem, 1)
            dve.wait_ge(dve_step.sem, prog.step())
            tt(a8(8), a8(7), over(a_rate[:, L, :], TT), ALU.mult).then_inc(a_g.sem, 1)
            dve.wait_ge(a_g.sem, a_g.at(L))
            prep(2)
            conv(1)
            silu(0)
            prep(2)
            conv(2)
            silu(1)
            prep(2)
            silu(2)
            dve.wait_ge(gate_tanh.sem, gate_tanh.at(L, 0))
            half_sigmoid(flat(t_v)).then_inc(dve_step.sem, 1)
            dve.wait_ge(dve_step.sem, prog.step())
            dve.wait_ge(a_silu.sem, a_silu.at(L, 2))
            tt(flat(a_gate), bank(2, 3), flat(t_v), ALU.mult).then_inc(gate_made.sem, 1)
            dve.wait_ge(gate_made.sem, gate_made.at(L, 0))
            prep(2)
            dve.wait_ge(gate_tanh.sem, gate_tanh.at(L, 1))
            half_sigmoid(flat(b_q)).then_inc(dve_step.sem, 1)
            dve.wait_ge(dve_step.sem, prog.step())
            tt(flat(b_q), bank(0, 1), flat(b_q), ALU.mult).then_inc(gate_made.sem, 1)
            dve.wait_ge(gate_made.sem, gate_made.at(L, 1))
            prep(2)
            used(L, 12)
            dve.tensor_scalar(flat(b_f), bank(2, 3), -40.0, None, ALU.max).then_inc(bf_read.sem, 1)
            dve.wait_ge(bf_read.sem, bf_read.at(L))
            prep(2)
            dve.wait_ge(bf_s.sem, bf_s.at(L))
            if L == 1:
                for h in range(H):
                    ins = dve.tensor_scalar(b_f[:, h, :], b_f[:, h, :], lb[:, 1, h:h + 1], lb[:, 0, h:h + 1],
                                            ALU.mult, ALU.add)
                    ins.then_inc(dve_step.sem, 1)
                    dve.wait_ge(dve_step.sem, prog.step())
            prep(2)
            dve.wait_ge(gate_tanh.sem, gate_tanh.at(L, 2))
            half_sigmoid(flat(b_gate)).then_inc(gate_made.sem, 1)
            dve.wait_ge(gate_made.sem, gate_made.at(L, 3))
            deltanet(L)
            hgrn(L)
            dilated(L)
            branches(L)
            turn_input(4, L)
            prep(1)
            for half in range(2):
                used(L, U_OUT + 2 * half + 2)
                h = slice(half * 512, (half + 1) * 512)
                tt(x[:, :, h], x[:, :, h], PS[:, 2 * half:2 * half + 2, :], ALU.add).then_inc(x_made.sem, 1)
                dve.wait_ge(x_made.sem, x_made.at(L, half))
                prep(1)

        def chunk(t, c):
            return t[:, c].rearrange("p h j -> p (h j)")

        def scale8(t):
            return wide(t, P)

        def deltanet(L):
            beta, g, r_q, r_k = (a_s[:, n, :] for n in (0, 8, 15, 16))
            for n, (src, k) in enumerate(((t_w, 0), (t_v, 1))):
                dve.wait_ge(a_sq.sem, a_sq.at(L, 2 + k))
                ins = dve.tensor_reduce(a_s[:, 9 + n, :], flat8(src), AX.X, ALU.add)
                if n:
                    ins.then_inc(a_ss.sem, 1)
                    dve.wait_ge(a_ss.sem, a_ss.at(L))
                else:
                    ins.then_inc(dve_step.sem, 1)
                    dve.wait_ge(dve_step.sem, prog.step())
            dve.wait_ge(a_r.sem, a_r.at(L))
            for c in range(TT):
                c4 = slice(c * H, (c + 1) * H)
                tt(t_x[:, c], bank4((4, 7)[c]), wide(r_q[:, c4], P), ALU.mult).then_inc(a_qn.sem, 1)
                tt(k_nat[:, c], bank4((5, 0)[c]), wide(r_k[:, c4], P), ALU.mult).then_inc(a_kn.sem, 1)
            tt(flat8(t_m), over(gt, 8), wide(g, P), ALU.mult).then_inc(a_seg.sem, 1)
            tt(flat8(t_n), over(le, 8), wide(g, P), ALU.mult).then_inc(a_seg.sem, 1)
            tt(flat8(t_w), over(gt, 8), wide(beta, P), ALU.mult).then_inc(dve_step.sem, 1)
            dve.wait_ge(dve_step.sem, prog.step())
            dve.wait_ge(a_exp.sem, a_exp.at(L, 1))
            tt(flat8(t_x), flat8(t_x), flat8(t_w), ALU.mult).then_inc(dve_step.sem, 1)
            dve.wait_ge(dve_step.sem, prog.step())
            dve.wait_ge(a_exp.sem, a_exp.at(L, 3))
            tt(flat8(t_y), flat8(t_y), over(le, 8), ALU.mult).then_inc(dve_step.sem, 1)
            dve.wait_ge(dve_step.sem, prog.step())
            for c in range(TT):
                dve.wait_ge(a_kk.sem, a_kk.at(L, c))
                tt(chunk(t_m, c), bank(2 + c), chunk(t_x, c), ALU.mult).then_inc(a_M.sem, 1)
                dve.wait_ge(a_M.sem, a_M.at(L, c))
            for c in range(TT):
                dve.wait_ge(a_kk.sem, a_kk.at(L, 2 + c))
                tt(chunk(attn, c), bank((6, 1)[c]), chunk(t_y, c), ALU.mult).then_inc(a_attn.sem, 1)
                dve.wait_ge(a_attn.sem, a_attn.at(L, c))
            tt(flat8(t_x), flat8(t_m), over(consts[:, K_M0, :], 8), ALU.mult).then_inc(dve_step.sem, 1)
            dve.wait_ge(dve_step.sem, prog.step())
            tt(flat8(t_x), over(ident, 8), flat8(t_x), ALU.subtract).then_inc(a_X.sem, 1)
            dve.wait_ge(a_X.sem, a_X.at(L, 0))
            dve.wait_ge(a_Nc.sem, a_Nc.at(L, 1))
            tt(flat8(t_y), flat8(t_n), over(consts[:, K_MT, :], 8), ALU.mult).then_inc(dve_step.sem, 1)
            dve.wait_ge(dve_step.sem, prog.step())
            tt(flat8(t_y), over(ident, 8), flat8(t_y), ALU.subtract).then_inc(a_Y.sem, 1)
            dve.wait_ge(a_Y.sem, a_Y.at(L, 0))

            def off(lv):
                tt(flat8(t_w), flat8(t_n), over(consts[:, K_MT + lv, :], 8), ALU.mult).then_inc(a_No.sem, 1)

            off(1)
            for lv in range(1, LEVELS):
                dve.wait_ge(a_P.sem, a_P.at(L, 2 * (lv - 1) + 1))
                if lv < LEVELS - 1:
                    off(lv + 1)
                else:
                    tt(t_w[:, 0], v_nat[:, 0], wide(beta[:, 0:H], P), ALU.mult).then_inc(a_r0.sem, 1)
                    dve.wait_ge(a_cum_e.sem, a_cum_e.at(L))
                    tt(t_v[:, 0], k_nat[:, 0], wide(a_s[:, 11, 0:H], P), ALU.mult).then_inc(a_kg.sem, 1)
                for c in range(TT):
                    if lv < LEVELS - 1:
                        dve.wait_ge(a_XP.sem, a_XP.at(L, 2 * (lv - 1) + c))
                        tt(chunk(t_x, c), chunk(t_x, c), bank(6 + c), ALU.subtract).then_inc(a_X.sem, 1)
                        dve.wait_ge(a_X.sem, a_X.at(L, 2 * lv - 1 + c))
                    dve.wait_ge(a_YP.sem, a_YP.at(L, 2 * (lv - 1) + c))
                    tt(chunk(t_y, c), chunk(t_y, c), bank(c), ALU.subtract).then_inc(a_Y.sem, 1)
                    dve.wait_ge(a_Y.sem, a_Y.at(L, 2 * lv - 1 + c))
            eg = wide(a_s[:, 11, H:2 * H], P)
            dve.wait_ge(a_kS.sem, a_kS.at(L))
            tt(t_v[:, 1], bank4(6), eg, ALU.mult).then_inc(dve_step.sem, 1)
            dve.wait_ge(dve_step.sem, prog.step())
            tt(t_v[:, 1], v_nat[:, 1], t_v[:, 1], ALU.subtract).then_inc(dve_step.sem, 1)
            dve.wait_ge(dve_step.sem, prog.step())
            tt(t_w[:, 1], t_v[:, 1], wide(beta[:, H:2 * H], P), ALU.mult).then_inc(a_r1.sem, 1)
            dve.wait_ge(a_qS.sem, a_qS.at(L))
            tt(t_m[:, 1], bank4(7), eg, ALU.mult).then_inc(dve_step.sem, 1)
            dve.wait_ge(dve_step.sem, prog.step())
            dve.wait_ge(a_o.sem, a_o.at(L, 1))
            dve.wait_ge(a_oc.sem, a_oc.at(L, 0))
            tt(chunk(t_n, 1), chunk(t_m, 1), bank(3), ALU.add).then_inc(a_oc.sem, 1)
            dve.wait_ge(a_oc.sem, a_oc.at(L, 1))
            output_norm(L, 0, t_n, t_y, a_gate)

        def output_norm(L, br, src, sq, gate):
            dve.wait_ge(o_sq.sem, o_sq.at(L, br))
            dve.tensor_reduce(a_s[:, 17, :], flat8(sq), AX.X, ALU.add).then_inc(o_ss.sem, 1)
            dve.wait_ge(o_r.sem, o_r.at(L, br))
            tt(flat8(src), flat8(src), wide(a_s[:, 19, :], P), ALU.mult).then_inc(dve_step.sem, 1)
            dve.wait_ge(dve_step.sem, prog.step())
            tt(flat8(src), flat8(src), flat8(gate), ALU.mult).then_inc(o_made.sem, 1)
            dve.wait_ge(o_made.sem, o_made.at(L, br))

        def hgrn(L):
            dve.wait_ge(oT_made.sem, oT_made.at(L, 0))
            dve.tensor_scalar(flat(b_k), flat(b_f), -1.0, 1.0, ALU.mult, ALU.add).then_inc(b_qk.sem, 1)
            dve.wait_ge(b_qk.sem, b_qk.at(L, 0))
            dve.tensor_scalar(flat(b_f), flat(b_f), 1e-18, None, ALU.max).then_inc(b_clamp.sem, 1)
            dve.wait_ge(b_clamp.sem, b_clamp.at(L))
            dve.memset(flat(b_attn), 0.0).then_inc(dve_step.sem, 1)
            dve.wait_ge(dve_step.sem, prog.step())
            dve.wait_ge(b_g.sem, b_g.at(L))
            for h in range(H):
                ins = dve.tensor_tensor_scan(b_gc[:, h, :], zero_t.broadcast_to([P, T]), b_f[:, h, :], 0.0,
                                             ALU.add, ALU.add)
                ins.then_inc(dve_step.sem, 1)
                dve.wait_ge(dve_step.sem, prog.step())

            def masked(n):
                dve.wait_ge(b_att.sem, b_att.at(L, n))
                if n == LEVELS + 1:
                    dve.tensor_copy(chunk(b_attn, 2), bank(0)).then_inc(b_masked.sem, 1)
                    dve.wait_ge(b_masked.sem, b_masked.at(L, n))
                    return
                pair = (4, 6)[n % 2]
                mask = ident if n == 0 else consts[:, K_MT + n - 1, :]
                dve.copy_predicated(b_attn[:, 0:2].rearrange("p c h j -> p (c h) j"),
                                    over(mask, 8).bitcast(I32),
                                    PS[:, pair:pair + 2, :].rearrange("p c (h j) -> p (c h) j", h=H)).then_inc(b_masked.sem, 1)
                dve.wait_ge(b_masked.sem, b_masked.at(L, n))

            for n in range(LEVELS + 1):
                s = 1 << n
                v = flat(b_gc).rearrange("p (n s) -> p n s", s=2 * s)
                mid = v[:, :, s - 1:s].broadcast_to([P, H * T // (2 * s), 2 * s])
                tt(flat(b_e).rearrange("p (n s) -> p n s", s=2 * s), v, mid, ALU.subtract).then_inc(b_diff.sem, 1)
                dve.wait_ge(b_diff.sem, b_diff.at(L, n))
                masked(n)
                dve.wait_ge(b_exp.sem, b_exp.at(L, n))
                tt(flat(b_qe), flat(b_q), flat(b_e), ALU.mult).then_inc(dve_step.sem, 1)
                dve.wait_ge(dve_step.sem, prog.step())
                tt(flat(b_ke), flat(b_k), flat(b_e), ALU.mult).then_inc(b_qk.sem, 1)
                dve.wait_ge(b_qk.sem, b_qk.at(L, n + 1))
            masked(LEVELS + 1)
            output_norm(L, 1, b_o, b_o2, b_gate)

        def dilated(L):
            with prog.loop(dve, GROUPS, 0) as g:
                def normed(j):
                    dve.wait_ge(c_sqd.sem, L * 6 + 2 * g + j + 1)
                    dve.tensor_reduce(stat[:, 0:8], flat8(c_sq), AX.X, ALU.add).then_inc(c_ss.sem, 1)
                    dve.wait_ge(c_r.sem, L * 6 + 2 * g + j + 1)
                    dve.wait_ge(c_Td.sem, c_Td.count(L * 6 + 2 * g + j))
                    tt(flat8(c_n), PS[:, 2 * j:2 * j + 2, :].rearrange("p t (h j) -> p (t h) j", h=H),
                       wide(stat[:, 8:16], P), ALU.mult).then_inc(c_nm.sem, 1)

                prep(2)
                normed(0)
                prep(2)
                normed(1)
                prep(2)

            for n in range(TT * H):
                t, h = divmod(n, H)
                keys = (t + 1) * P
                b = 2 * (n % 2)
                off = T - keys
                sv = c_s[:, :].rearrange("p (g s) -> p g s", g=GROUPS)
                bv = bias[:, :, :].rearrange("p (g h) s -> p g h s", g=GROUPS)
                dve.wait_ge(c_sd.sem, c_sd.at(L, n))
                if n:
                    dve.wait_ge(c_e.sem, c_e.at(L, n - 1))
                dve.scalar_tensor_tensor(sv[:, 0:2, 0:keys],
                                         PS[:, b, :].rearrange("p (g s) -> p g s", g=2)[:, :, 0:keys],
                                         P ** -0.5, bv[:, 0:2, h, off:T], ALU.mult, ALU.add).then_inc(dve_step.sem, 1)
                dve.wait_ge(dve_step.sem, prog.step())
                dve.scalar_tensor_tensor(sv[:, 2, 0:keys], PS[:, b + 1, 0:keys], P ** -0.5,
                                         bv[:, 2, h, off:T], ALU.mult, ALU.add).then_inc(c_sm.sem, 1)
                dve.wait_ge(c_sm.sem, c_sm.at(L, n))
                dve.tensor_reduce(stat[:, 0:1], sv[:, :, 0:keys], AX.XY, ALU.max).then_inc(dve_step.sem, 1)
                dve.wait_ge(dve_step.sem, prog.step())
                dve.tensor_scalar(stat[:, 1:2], stat[:, 0:1], -1.0, None, ALU.mult).then_inc(c_mx.sem, 1)
                dve.wait_ge(c_e.sem, c_e.at(L, n))
                dve.reciprocal(stat[:, 3:4], stat[:, 2:3]).then_inc(dve_step.sem, 1)
                dve.wait_ge(dve_step.sem, prog.step())
                dve.wait_ge(c_od.sem, c_od.at(L, n))
                ins = dve.tensor_scalar(c_o[:, t, h * P:(h + 1) * P], PS[:, 6 + n % 2, 0:P], stat[:, 3:4], None,
                                        ALU.mult)
                ins.then_inc(c_oc.sem, 1)
                dve.wait_ge(c_oc.sem, c_oc.at(L, n))
            dve.memset(stat[:, 5:6], 0.0).then_inc(o_made.sem, 1)
            dve.wait_ge(o_made.sem, o_made.at(L, 2))

        def branches(L):
            dve.wait_ge(oT_made.sem, oT_made.at(L, 2))
            dve.memset(flat(mix), 0.0).then_inc(dve_step.sem, 1)
            dve.wait_ge(dve_step.sem, prog.step())
            with prog.loop(dve, 3, 2) as br:
                dve.wait_ge(o_hi_made.sem, L * 3 + br + 1)
                tt(flat(o_lo), oT[:, bass.ds(br, 1), :, :].rearrange("p o a b -> p (o a b)"),
                   flat(o_hi).bitcast(F32), ALU.subtract).then_inc(o_lo_made.sem, 1)

                def product(half):
                    dve.wait_ge(unit_used.sem, LAYER_U[L] + U_BR + 6 * br + 3 * half + 3)
                    dve.wait_ge(mix_made.sem, mix_made.count(L * 6 + 2 * br + half))
                    ins = tt(flat(g_prod), flat(g_sig), bank(2, 3), ALU.mult)
                    ins.then_inc(g_prod_made.sem, 1)
                    dve.wait_ge(g_prod_made.sem, g_prod_made.count(L * 6 + 2 * br + half + 1))
                    h = slice(half * 512, (half + 1) * 512)
                    tt(mix[:, :, h], mix[:, :, h], g_prod[:, :, :], ALU.add).then_inc(mix_made.sem, 1)
                    dve.wait_ge(mix_made.sem, mix_made.count(L * 6 + 2 * br + half + 1))

                def gate(half):
                    dve.wait_ge(g_tanh.sem, g_tanh.count(L * 6 + 2 * br + half + 1))
                    half_sigmoid(flat(g_sig)).then_inc(dve_step.sem, 1)
                    dve.wait_ge(dve_step.sem, prog.step())

                prep(1)
                gate(0)
                prep(2)
                product(0)
                prep(1)
                gate(1)
                prep(2)
                product(1)

        def dense():
            norm(0, 1)
            prep(1)
            turn_input(8, 0)

            def half_step(m, s, preps=(1, 2)):
                dve.wait_ge(f_silu.sem, m + 1)
                dve.wait_ge(f_lo.sem, f_lo.count(m - 1))
                dve.tensor_tensor(f_g[s][:, :].rearrange("p (j t) -> p j t", j=2),
                                  f_s[s][:, :].rearrange("p (j t) -> p j t", j=2),
                                  PS[:, 2 * s:2 * s + 2, T:2 * T], ALU.mult).then_inc(f_gm.sem, 1)
                prep(preps[0])
                dve.wait_ge(f_hi.sem, m + 1)
                dve.wait_ge(f_gm.sem, f_gm.count(m + 1))
                tt(flat(fT_lo[s]), f_g[s][:, :], flat(fT_hi[s]).bitcast(F32), ALU.subtract).then_inc(f_lo.sem, 1)
                prep(preps[1])

            half_step(0, 0)
            with prog.loop(dve, STEPS_DENSE // 2 - 1, 0) as i:
                half_step(2 * i + 1, 1)
                half_step(2 * i + 2, 0)
            half_step(STEPS_DENSE - 2, 1)
            half_step(STEPS_DENSE - 1, 0, (0, 0))
            dve.wait_ge(unit_used.sem, LAYER_U[1])
            tt(flat(x), flat(x), PS[:, 4:8, :].rearrange("p a b -> p (a b)"), ALU.add).then_inc(x_made.sem, 1)
            dve.wait_ge(x_made.sem, x_made.at(0, 2))
            prep(2)

        def choose(n, e, turn):
            dve.wait_ge(e_done.sem, e_done.count(2 * n))
            dve.wait_ge(pickT_done.sem, pickT_done.count(n))
            for t in range(TT):
                col = bass.ds(e + t * E, 1) if not isinstance(e, int) else slice(e + t * E, e + t * E + 1)
                dve.tensor_scalar(pick[:, t, :], slots[:, turn * P:(turn + 1) * P],
                                  r_t[:, 14, col], None, ALU.is_equal).then_inc(pick0.sem, 1)
            dve.wait_ge(pick0.sem, 2 * n + 2)
            dve.tensor_copy(flat(pick_r), flat(pick)).then_inc(pick_made.sem, 1)

        def tokens(n):
            for j in range(2):
                dve.wait_ge(e_hi_made.sem, 2 * n + j + 1)
                v = slice(4 * j, 4 * j + 4)
                tt(e_lo[:, v, :].rearrange("p a b -> p (a b)"), bank(6 + j),
                   e_hi[:, v, :].rearrange("p a b -> p (a b)").bitcast(F32), ALU.subtract).then_inc(e_lo_made.sem, 1)

        def add_to_x(n, e, t):
            dve.wait_ge(s_done.sem, 2 * n + t + 1)
            col = bass.ds(e + t * E, 1) if not isinstance(e, int) else slice(e + t * E, e + t * E + 1)
            dve.scalar_tensor_tensor(x[:, t, :], bank(4 + 2 * t, 5 + 2 * t), r_t[:, 15, col],
                                     x[:, t, :], ALU.mult, ALU.add).then_inc(s_read.sem, 1)

        def expert(n, e, turn, first, last):
            base = STEPS_DENSE + STEPS_EXPERT * n

            def multiply(m, s):
                dve.wait_ge(f_silu.sem, m + 1)
                dve.wait_ge(f_gT.sem, f_gT.count(m - STEPS_DENSE - 1))
                tt(f_g[s][:, 0:SUB], f_s[s][:, 0:SUB], PS[:, s, SUB:2 * SUB], ALU.mult).then_inc(f_gm.sem, 1)

            def low(m, s):
                dve.wait_ge(f_hi.sem, m + 1)
                tt(fT_lo[s][:, :, 0:P], PS[:, 2, s * SUB:(s + 1) * SUB].rearrange("p (j t) -> p j t", j=2),
                   fT_hi[s][:, :, 0:P].bitcast(F32),
                   ALU.subtract).then_inc(f_lo.sem, 1)

            multiply(base, 0)
            prep(1)
            if not first:
                add_to_x(n - 1, e - 1, 0)
            low(base, 0)
            prep(1)
            if not first:
                add_to_x(n - 1, e - 1, 1)
            prep(1)
            if not last:
                choose(n + 1, e + 1, turn)
            with prog.loop(dve, STEPS_EXPERT // 2 - 1, 0) as i:
                for d, s in ((1, 1), (2, 0)):
                    multiply(base + 2 * i + d, s)
                    prep(1)
                    low(base + 2 * i + d, s)
                    prep(2)
            multiply(base + STEPS_EXPERT - 1, 1)
            prep(0 if last else 1)
            low(base + STEPS_EXPERT - 1, 1)
            if not last:
                tokens(n + 1)
                prep(1)
            dve.wait_ge(y_hi_made.sem, n + 1)
            tt(y_lo[:, :], bank(4, 5), y_hi[:, :].bitcast(F32), ALU.subtract).then_inc(y_lo_made.sem, 1)
            prep(0 if last else 1)

        def experts(turn):
            n = E * turn
            choose(n, 0, turn)
            tokens(n)
            expert(n, 0, turn, True, False)
            with prog.loop(dve, E - 2, 0, rounds=EXPERT_R) as e:
                expert(n + 1 + e, e + 1, turn, False, False)
            expert(n + E - 1, E - 1, turn, False, True)
            for t in range(TT):
                add_to_x(n + E - 1, E - 1, t)
            dve.wait_ge(s_read.sem, s_read.count(2 * (n + E)))

        def moe():
            norm(1, 1)
            prep(1)
            turn_input(8, 1)
            dve.wait_ge(fn_hi_made.sem, 1)
            tt(flat(fn_lo), flat(fn), flat(fn_hi).bitcast(F32), ALU.subtract).then_inc(fn_lo_made.sem, 1)
            dve.wait_ge(r_done.sem, 1)

            def r16(n):
                return r_t[:, n, :]

            def r8(n):
                return r_t[:, n, :].rearrange("p (t e) -> p t e", t=TT)

            dve.tensor_copy(r16(0), PS[:, 0, 0:TT * E]).then_inc(dve_step.sem, 1)
            dve.wait_ge(dve_step.sem, prog.step())
            for k in range(2):
                lg, eq, cs, first, v = 0 + k, 2, 3, 4 + k, r_t[:, 8, 2 * k:2 * k + 2]
                dve.tensor_reduce(v, r8(lg), AX.X, ALU.max).then_inc(dve_step.sem, 1)
                dve.wait_ge(dve_step.sem, prog.step())
                tt(r8(eq), r8(lg), wide(v, E), ALU.is_equal).then_inc(dve_step.sem, 1)
                dve.wait_ge(dve_step.sem, prog.step())
                for t in range(TT):
                    dve.tensor_tensor_scan(r_t[:, cs, t * E:(t + 1) * E], zero_t.broadcast_to([P, E]),
                                           r_t[:, eq, t * E:(t + 1) * E], 0.0, ALU.add, ALU.add).then_inc(dve_step.sem, 1)
                    dve.wait_ge(dve_step.sem, prog.step())
                dve.scalar_tensor_tensor(r16(first), r16(cs), 1.0, r16(eq), ALU.is_equal, ALU.mult).then_inc(dve_step.sem, 1)
                dve.wait_ge(dve_step.sem, prog.step())
                if k == 0:
                    dve.scalar_tensor_tensor(r16(1), r16(first), NEG, r16(0), ALU.mult, ALU.add).then_inc(dve_step.sem, 1)
                    dve.wait_ge(dve_step.sem, prog.step())
            tt(r_t[:, 9, 0:2], r_t[:, 8, 2:4], r_t[:, 8, 0:2], ALU.subtract).then_inc(r_read.sem, 1)
            dve.wait_ge(r_read.sem, 1)
            tt(r16(12), r16(4), r16(5), ALU.add).then_inc(r_sel.sem, 1)
            dve.wait_ge(r_sel.sem, 1)
            dve.wait_ge(r_e.sem, 1)
            dve.tensor_scalar(r_t[:, 9, 2:4], r_t[:, 10, 0:2], 1.0, None, ALU.add).then_inc(dve_step.sem, 1)
            dve.wait_ge(dve_step.sem, prog.step())
            dve.reciprocal(r_t[:, 11, 0:2], r_t[:, 9, 2:4]).then_inc(dve_step.sem, 1)
            dve.wait_ge(dve_step.sem, prog.step())
            tt(r_t[:, 11, 2:4], r_t[:, 11, 0:2], r_t[:, 10, 0:2], ALU.mult).then_inc(dve_step.sem, 1)
            dve.wait_ge(dve_step.sem, prog.step())
            tt(r8(6), r8(4), wide(r_t[:, 11, 0:2], E), ALU.mult).then_inc(dve_step.sem, 1)
            dve.wait_ge(dve_step.sem, prog.step())
            tt(r8(7), r8(5), wide(r_t[:, 11, 2:4], E), ALU.mult).then_inc(dve_step.sem, 1)
            dve.wait_ge(dve_step.sem, prog.step())
            tt(r16(15), r16(6), r16(7), ALU.add).then_inc(dve_step.sem, 1)
            dve.wait_ge(dve_step.sem, prog.step())
            dve.wait_ge(r_cnt.sem, 1)
            tt(r16(14), PS[:, 1, 0:2 * E], r16(12), ALU.mult).then_inc(dve_step.sem, 1)
            dve.wait_ge(dve_step.sem, prog.step())
            dve.tensor_scalar(r16(14), r16(14), -1.0, None, ALU.add).then_inc(dve_step.sem, 1)
            dve.wait_ge(dve_step.sem, prog.step())
            dve.tensor_reduce(r_t[:, 13, 0:1], PS[:, 1, 2 * E:3 * E], AX.X, ALU.max).then_inc(dve_step.sem, 1)
            dve.wait_ge(dve_step.sem, prog.step())
            dve.tensor_scalar(r_flag[:, 0:1], r_t[:, 13, 0:1], float(P), None, ALU.is_gt).then_inc(r_flag_made.sem, 1)
            dve.wait_ge(r_flag_made.sem, 1)
            dve.wait_ge(slots_here.sem, 2)
            experts(0)
            more = second_turn(dve, prog)
            with dve.If(more > 0):
                prep(3)
                experts(1)
            dve.memset(stat[:, 8:9], 0.0).then_inc(x_last.sem, 1)

        mixer(0)
        dense()
        mixer(1)
        moe()

    @block.gpsimd
    def _(pool):
        pool.dma_start(gain[:, :], dram["norm_mix"][0:1, :].partition_broadcast(P)
                       .rearrange("q o d -> q (o d)")).then_inc(gain_here.sem, 16)
        pool.wait_ge(by_dist_kept.sem, 1)
        pool.dma_start(hankel_dram.rearrange("(g h) z -> h g z", g=GROUPS), by_dist[:, :, :])\
            .then_inc(by_dist_out.sem, 16)
        pool.wait_ge(by_dist_out.sem, 16)
        pool.dma_start(hankel[:, :, :], bass.AP(hankel_dram.tensor, 0, [[1, P], [DIST, GROUPS * H], [1, T]]))\
            .then_inc(hankel_here.sem, 16)
        for L in range(DEPTH):
            if L:
                pool.wait_ge(x_made.sem, x_made.at(L - 1, 2))
                pool.dma_start(gain[:, :], dram["norm_mix"][L:L + 1, :].partition_broadcast(P)
                               .rearrange("q o d -> q (o d)")).then_inc(gain_here.sem, 16)
            pool.wait_ge(oT_made.sem, oT_made.at(L, 2))
            pool.wait_ge(gain_here.sem, 16 * (2 * L + 1))
            pool.dma_start(f_gain[:, :], dram["norm_ffn"][L:L + 1, :].partition_broadcast(P)
                           .rearrange("q o d -> q (o d)")).then_inc(gain_here.sem, 16)
        pool.wait_ge(x_made.sem, x_made.at(1, 1))
        pool.iota(slots_i[:, :], pattern=[[1, 2 * P]], base=0, channel_multiplier=0).then_inc(slots_here.sem, 1)
        pool.wait_ge(slots_here.sem, 1)
        pool.tensor_copy(slots[:, :], slots_i[:, :]).then_inc(slots_here.sem, 1)

    @block.sync
    def _(sp):
        prog = Program(None)

        def load(dst, src, sig):
            sp.dma_start(dst, src).then_inc(sig.sem, 16)

        def unit(src, k):
            slot = prog.u % RAW
            if prog.u >= RAW:
                sp.wait_ge(unit_used.sem, prog.unit(1 - RAW))
            load(unit_view(raw[slot], k), src, raw_full[slot])
            prog.u += 1

        def rows_of(ap):
            return ap.rearrange("(k p) n -> p k n", p=P)

        def cols(L, c):
            for half in range(2):
                sl = bass.ds(c, 512) if not isinstance(c, int) else slice(c, c + 512)
                unit(rows_of(dram["w_in"][L, half * 512:(half + 1) * 512, sl]), 4)

        xr = dram["x"][0].rearrange("(t p) d -> t p d", p=P)
        for t in range(TT):
            load(x[:, t, :], xr[t], x_here)
        load(consts[:, :, :], dram["masks"], consts_here)
        load(picks[:, :, :], dram["buckets"], consts_here)
        rows_of_small = (
            (R_CONV, dram["conv_a"].rearrange("l t (c p) -> (l t c) p", p=P)),
            (R_LB, dram["lb_logits"].rearrange("l (h p) -> (l h) p", p=P)),
            (R_GA, dram["gnorm_a"]), (R_GB, dram["gnorm_b"]),
            (R_QN, dram["qnorm_c"].rearrange("l g p -> (l g) p")),
            (R_KN, dram["knorm_c"].rearrange("l g p -> (l g) p")))
        assert len(rows_of_small) == N_ROW_LOADS
        for r, src in rows_of_small:
            load(rows[r:r + src.shape[0], :], src, rows_here)
        load(table[0:BUCKETS, :], dram["rel_bias"], table_here)
        for n in range(DEPTH):
            load(ab[:, n, :, :], rows_of(dram["w_in"][n, :, C_AB:C_AB + 2 * H]), ab_here)
        load(ab[:, 2, :, :], rows_of(dram["router"][0]), ab_here)
        for n, name in enumerate(("a_log", "dt_bias")):
            load(a_par[:, n, :, :], dram[name].rearrange("(o l) h -> o l h", o=1).partition_broadcast(P)
                 .rearrange("q o l h -> q (o l) h"), par_here)

        def mixer(L):
            for g in range(3):
                cols(L, C_QKV + g * W)
            cols(L, C_AGATE)
            for g in range(4):
                cols(L, C_BQ + g * W)
            with prog.loop(sp, GROUPS, 0) as g:
                for j in range(3):
                    cols(L, g * W + (C_CQKV + j * GROUPS * W))
            with prog.loop(sp, 3, 0) as br:
                for half in range(2):
                    cols(L, br * D + (C_BR + half * 512))
                    unit(rows_of(dram["w_br"][bass.ds(br, 1), L, :, half * 512:(half + 1) * 512]
                                 .rearrange("o r n -> (o r) n")), 4)
            for half in range(2):
                for k in range(2):
                    unit(rows_of(dram["w_out"][L, k * 512:(k + 1) * 512, half * 512:(half + 1) * 512]), 4)

        def up(w1, w3, c):
            for w in (w1, w3):
                sl = bass.ds(c, SUB) if not isinstance(c, int) else slice(c, c + SUB)
                unit(rows_of(w[:, sl]), 8)

        def dense():
            w1, w3, w2 = (dram[n][0] for n in ("ffn_w1", "ffn_w3", "ffn_w2"))

            def down(c):
                rows = bass.ds(c, SUB) if not isinstance(c, int) else slice(c, c + SUB)
                unit(rows_of(w2[rows, :]), 2)

            up(w1, w3, 0)
            up(w1, w3, SUB)
            down(0)
            with prog.loop(sp, STEPS_DENSE // 2 - 1, 0) as i:
                for m in (2, 3):
                    up(w1, w3, i * (2 * SUB) + m * SUB)
                    down(i * (2 * SUB) + (m - 1) * SUB)
            up(w1, w3, (STEPS_DENSE - 1) * SUB)
            down((STEPS_DENSE - 2) * SUB)
            down((STEPS_DENSE - 1) * SUB)

        def experts():
            with prog.loop(sp, E, 0, rounds=EXPERT_R) as e:
                w1, w3, w2 = (dram[n][0, bass.ds(e, 1), :, :].rearrange("o r n -> (o r) n")
                              for n in ("moe_w1", "moe_w3", "moe_w2"))

                def down(c):
                    rows = bass.ds(c, SUB) if not isinstance(c, int) else slice(c, c + SUB)
                    unit(rows_of(dram["moe_w2"][0, bass.ds(e, 1), rows, :].rearrange("o r n -> (o r) n")), 2)

                up(w1, w3, 0)
                up(w1, w3, SUB)
                down(0)
                with prog.loop(sp, STEPS_EXPERT // 2 - 1, 0) as c:
                    for m in (2, 3):
                        up(w1, w3, c * (2 * SUB) + m * SUB)
                        down(c * (2 * SUB) + (m - 1) * SUB)
                down((STEPS_EXPERT - 1) * SUB)

        mixer(0)
        dense()
        mixer(1)
        experts()
        more = second_turn(sp, prog)
        with sp.If(more > 0):
            experts()
        sp.wait_ge(x_last.sem, 1)
        out = dram["out"][0].rearrange("(t p) d -> t p d", p=P)
        for t in range(TT):
            load(out[t], x[:, t, :], out_here)
        sp.wait_ge(out_here.sem, 32)


_NAMES = ["x", "w_in", "norm_mix", "conv_a", "a_log", "dt_bias", "gnorm_a", "lb_logits", "gnorm_b", "qnorm_c",
          "knorm_c", "rel_bias", "w_out", "norm_ffn", "ffn_w1", "ffn_w3", "ffn_w2", "router", "moe_w1",
          "moe_w3", "moe_w2"]


def kernel(**inputs):
    import concourse.bacc as _bacc
    from concourse.bass_utils import run_bass_kernel_spmd as _run

    nc = _bacc.Bacc("TRN2", target_bir_lowering=False, num_devices=1)
    masks, buckets = shape_constants()
    given = {name: np.ascontiguousarray(inputs[name]) for name in _NAMES}
    given["w_br"] = np.stack([np.asarray(inputs[n]) for n in ("w_br_a", "w_br_b", "w_br_c")])
    given["masks"], given["buckets"] = masks, buckets
    dram, arrays = {}, {}
    for name, a in given.items():
        arrays[f"in_{name}"] = a
        dram[name] = nc.dram_tensor(f"in_{name}", a.shape, mybir.dt.from_np(a.dtype), kind="ExternalInput").ap()
    dram["out"] = nc.dram_tensor("out_x", (1, T, D), F32, kind="ExternalOutput").ap()
    with ExitStack() as ctx:
        build(ctx, nc, dram)
    return _run(nc, [arrays], core_ids=[0]).results[0]["out_x"]
```

```python
import math
from contextlib import ExitStack, contextmanager

import concourse.bass as bass
import numpy as np
from concourse import mybir

F32 = mybir.dt.float32
F32R = mybir.dt.float32r
I32 = mybir.dt.int32
ALU = mybir.AluOpType
ACT = mybir.ActivationFunctionType
AX = mybir.AxisListType

P = 128
T = 256
TT = T // P
D = 1024
KT = D // P
DEPTH = 2
EPS = 1e-6
H = 4
W = H * P
TAPS = 4
CT = 3 * H
GROUPS = 3
DILATION = (1, 4, 16)
SPAN = 128
BUCKETS, MAX_DIST = 32, 2048
E = 8
FF, FFE = 2816, 3584
SUB = 256
UE = 2048

C_QKV = 0
C_AB = 3 * W
C_AGATE = C_AB + 2 * H
C_BQ = C_AGATE + W
C_CQKV = C_BQ + 4 * W
C_BR = C_CQKV + 9 * W
NEG = -1e30
LN_SET = "natural_log"
LN_EXP_SET = "natural_log_exp_and_others"

RAW = 6
SPLIT = 3
U_GATES, U_C, U_BR, U_OUT, U_FF = 16, 28, 46, 52, 56
U_DENSE = 3 * (FF // SUB)
LAYER_U = (0, U_FF + U_DENSE)
U_END = LAYER_U[1] + U_FF
STEPS_DENSE, STEPS_EXPERT = FF // SUB, FFE // SUB
N_ROW_LOADS = 6
EXPERT_R = STEPS_EXPERT // 2

K_ID, K_LE, K_GT, K_M0, K_MT, K_FLIP, K_N = 0, 1, 2, 3, 4, 11, 12
LEVELS = 7
R_CONV, R_LB, R_GA, R_GB, R_QN, R_KN, R_N = 0, 96, 104, 106, 108, 114, 120
DIST = 384


def shape_constants():
    i, j = np.arange(P)[:, None], np.arange(P)[None, :]
    tiles = [i == j, i <= j, i > j, (i // 2 == j // 2) & (i > j)]
    for n in range(LEVELS):
        s = 1 << n
        tiles.append((i // (2 * s) == j // (2 * s)) & (j % (2 * s) >= s) & (i % (2 * s) < s))
    tiles.append(i + j == P - 1)
    masks = np.stack([t.astype(np.float32) for t in tiles], 1)
    buckets = np.zeros((BUCKETS + 1, GROUPS, DIST), np.float32)
    exact = BUCKETS // 2
    for g, dil in enumerate(DILATION):
        for z in range(DIST):
            dist = T - 1 - z
            if dist < 0 or dist % dil or dist // dil > SPAN:
                buckets[BUCKETS, g, z] = NEG
                continue
            b = dist
            if dist >= exact:
                big = np.log(np.float32(dist) / np.float32(exact)) / np.float32(math.log(MAX_DIST / exact))
                b = min(exact + int(np.float32(big) * np.float32(BUCKETS - exact)), BUCKETS - 1)
            buckets[b, g, z] = 1.0
    return masks, buckets


class Signal:

    def __init__(self, ctx, nc, name, per_layer=1, ahead=0):
        self.sem = ctx.enter_context(nc.semaphore(name))
        self.per_layer, self.ahead = per_layer, ahead

    def at(self, layer, k=0):
        return self.ahead + layer * self.per_layer + k + 1

    def count(self, n):
        return n + self.ahead


class Program:

    def __init__(self, own):
        self.own = own
        self.n, self.turn = 0, None
        self.u, self.rounds = 0, None

    def step(self):
        self.n += 1
        return self.n if self.turn is None else self.n + self.turn

    def unit(self, k=0, each=1):
        n = (self.u + k) * each
        return n if self.rounds is None else n + self.rounds * (6 * each)

    @contextmanager
    def loop(self, eng, trips, steps, rounds=1):
        with eng.Fori(0, trips) as i:
            n, u, turn, r = self.n, self.u, self.turn, self.rounds
            self.turn = i * steps if turn is None else turn + i * steps
            self.rounds = i * rounds if r is None else r + i * rounds
            yield i
            assert self.n - n == steps, f"{self.n - n} steps in a turn, not {steps}"
            assert self.u - u == 6 * rounds, f"{self.u - u} units in a turn"
            self.turn, self.rounds = turn, r
        self.n, self.u = n + trips * steps, u + trips * 6 * rounds


def build(ctx, nc, dram):
    cursor = nc.sbuf_base + (-nc.sbuf_base) % 64

    def sb(name, shape, dtype=F32, at=None):
        nonlocal cursor
        size = int(np.prod(shape[1:])) * 4
        size += (-size) % 64
        if at is None:
            at, cursor = cursor, cursor + size
        assert at + size <= nc.sbuf_usable_end, (name, at + size - nc.sbuf_usable_end)
        return nc.alloc_sbuf_tensor_at(name, shape, dtype, offset=at)

    w0 = cursor
    raw = [sb(f"raw{s}", [P, UE]) for s in range(RAW)]
    lo = [sb(f"lo{s}", [P, UE], F32R, at=w0 + s * UE * 4) for s in range(RAW)]
    hi = [sb(f"hi{s}", [P, UE], F32R) for s in range(SPLIT)]
    x = sb("x", [P, TT, D])
    ones_t = sb("ones_t", [P, P])
    o0 = cursor
    actT_hi = sb("actT_hi", [P, KT, T], F32R)
    actT_lo = sb("actT_lo", [P, KT, T], F32R)
    consts = sb("consts", [P, K_N, P])
    bias = sb("bias", [P, GROUPS * H, T])
    small = sb("small", [P, R_N])
    ab = sb("ab", [P, 3, KT, 8])
    ab_hi = sb("ab_hi", [P, 3, KT, 8], F32R)
    ab_lo = sb("ab_lo", [P, 3, KT, 8], F32R)
    a_par = sb("a_par", [P, 2, DEPTH, H])
    a_rate = sb("a_rate", [P, DEPTH, H])
    lb = sb("lb", [P, 8, H])
    tiny = sb("tiny", [P, 8])
    stat = sb("stat", [P, 16])
    a_s = sb("a_s", [P, 20, TT * H])
    ident, le, gt = consts[:, K_ID, :], consts[:, K_LE, :], consts[:, K_GT, :]
    eps_t, one_t, lnq_t, zero_t = (tiny[:, n:n + 1] for n in range(4))

    u0 = cursor
    a_in = sb("a_in", [P, CT, 3 + T])
    u1 = cursor
    a_act = sb("a_act", [P, CT, T])
    b_q = sb("b_q", [P, H, T])
    b_f = sb("b_f", [P, H, T])
    t0 = cursor
    oT = sb("oT", [P, 3, H, T])
    c0 = cursor
    a_gate = sb("a_gate", [P, TT, W], at=u0)
    b_i = sb("b_i", [P, TT, W], at=u0 + 4096)
    b_gate = sb("b_gate", [P, TT, W], at=u0 + 8192)
    gain = sb("gain", [P, D], at=u1)
    b_gc = sb("b_gc", [P, H, T], at=u1)
    b_qe = sb("b_qe", [P, H, T], at=u1 + 4096)
    b_ke = sb("b_ke", [P, H, T], at=u1 + 8192)
    hn = sb("hn", [P, TT, D], at=c0)
    S8 = [P, TT, H, P]
    k_nat, v_nat, attn, t_m, t_n, t_x, t_y, t_w, t_v = (
        sb(name, S8, at=c0 + 4096 * n)
        for n, name in enumerate(("k_nat", "v_nat", "attn", "t_m", "t_n", "t_x", "t_y", "t_w", "t_v")))
    b_attn = sb("b_attn", [P, 3, H, P], at=c0)
    b_e = sb("b_e", [P, H, T], at=c0 + 6144)
    b_o = sb("b_o", [P, TT, W], at=t0 + 8192)
    b_o2 = sb("b_o2", [P, TT, W], at=c0 + 14336)
    b_k = sb("b_k", [P, H, T], at=c0 + 18432)
    gates = [sb(f"gate{k}", [P, TT, W], at=u0 if k == 5 else c0 + 24576 + 4096 * k) for k in range(6)]
    c_qT = sb("c_qT", [P, GROUPS * H, T], at=u0 + 17408)
    c_kT = sb("c_kT", [P, GROUPS * H, T], at=c0)
    c_v = sb("c_v", [P, TT, GROUPS, W], at=c0 + 12288)
    c_o = sb("c_o", [P, TT, W], at=u0 + 4096)
    c_sq = sb("c_sq", [P, TT, W], at=u0 + 8192)
    c_n = sb("c_n", [P, TT, W], at=u0 + 12288)
    c_s = sb("c_s", [P, GROUPS * T], at=u0 + 8192)
    c_p = sb("c_p", [P, GROUPS * T], at=u0 + 11264)
    c_pT = sb("c_pT", [P, 2 * GROUPS * P], at=u0 + 14336)
    o_hi = [sb(f"o_hi{n}", [P, H, T], F32R, at=o0 + 8192 * n) for n in range(2)]
    o_lo = [sb(f"o_lo{n}", [P, H, T], F32R, at=o0 + 8192 * n + 4096) for n in range(2)]
    narrow = sb("narrow", [8, T], at=c0 + 45056)
    rows = sb("rows", [P, P], at=u0)
    picks = sb("picks", [BUCKETS + 1, GROUPS, DIST], at=u0 + 512)
    table = sb("table", [BUCKETS + 1, GROUPS * H], at=u0 + 512 + 4608)
    by_dist = sb("by_dist", [H, GROUPS, DIST], at=u1 + 12288)
    hankel = sb("hankel", [P, GROUPS * H, T], at=u1 + 12288 + 8192)

    cursor = u0
    fn = sb("fn", [P, TT, D])
    f_gain = sb("f_gain", [P, D])
    f_s = [sb(f"f_s{s}", [P, 512]) for s in range(2)]
    f_g = [sb(f"f_g{s}", [P, 512]) for s in range(2)]
    fT_hi = [sb(f"fT_hi{s}", [P, 2, T], F32R) for s in range(2)]
    fT_lo = [sb(f"fT_lo{s}", [P, 2, T], F32R) for s in range(2)]
    r_t = sb("r_t", [P, 20, TT * E])
    r_flag = sb("r_flag", [P, 2], I32)
    slots = sb("slots", [P, 2 * P])
    slots_i = sb("slots_i", [P, 2 * P], I32)
    fn_hi = sb("fn_hi", [P, TT, D], F32R)
    fn_lo = sb("fn_lo", [P, TT, D], F32R)
    pick = sb("pick", [P, TT, P])
    pick_r = sb("pick_r", [P, TT, P], F32R)
    pickT = sb("pickT", [P, TT, P], F32R)
    e_hi = sb("e_hi", [P, KT, P], F32R)
    e_lo = sb("e_lo", [P, KT, P], F32R)
    y_hi = sb("y_hi", [P, D], F32R)
    y_lo = sb("y_lo", [P, D], F32R)

    PS = ctx.enter_context(nc.psum_tensor("PS", [P, 8, 512], F32))
    hankel_dram = nc.dram_tensor("hankel_dram", (GROUPS * H, DIST), F32, kind="Internal").ap()

    def signal(name, per_layer=1, ahead=0):
        return Signal(ctx, nc, name, per_layer, ahead)

    raw_full = [signal(f"raw_full{s}") for s in range(RAW)]
    hi_made = signal("hi_made")
    lo_made = signal("lo_made")
    unit_used = signal("unit_used")
    act_step = signal("act_step")
    dve_step = signal("dve_step")
    x_here = signal("x_here")
    consts_here = signal("consts_here")
    rows_here = signal("rows_here")
    table_here = signal("table_here")
    ab_here = signal("ab_here")
    par_here = signal("par_here")
    rows_T = signal("rows_T")
    rows_kept = signal("rows_kept")
    by_dist_done = signal("by_dist_done")
    by_dist_kept = signal("by_dist_kept")
    by_dist_out = signal("by_dist_out")
    hankel_here = signal("hankel_here")
    bias_done = signal("bias_done")
    bias_kept = signal("bias_kept")
    ab_split = signal("ab_split")
    lb_m = signal("lb_m")
    lb_e = signal("lb_e")
    a_rate_e = signal("a_rate_e")
    tiny_made = signal("tiny_made")
    gain_here = signal("gain_here")
    norm_r = signal("norm_r", 2)
    norm_made = signal("norm_made", 4)
    turned = signal("turned", 12)
    actT_hi_made = signal("actT_hi_made", 12)
    actT_lo_made = signal("actT_lo_made", 12)
    x_made = signal("x_made", 3)
    a_raw = signal("a_raw", 6)
    pad_made = signal("pad_made")
    a_conv = signal("a_conv", 3)
    a_tanh = signal("a_tanh", 3)
    a_silu = signal("a_silu", 3)
    n_done = signal("n_done")
    n_kept = signal("n_kept")
    ab_done = signal("ab_done")
    ab_read = signal("ab_read")
    a_e1 = signal("a_e1")
    a_e2 = signal("a_e2")
    a_g = signal("a_g")
    a_cum = signal("a_cum")
    a_cum_e = signal("a_cum_e")
    gate_tanh = signal("gate_tanh", 3)
    gate_made = signal("gate_made", 4)
    a_fwd = signal("a_fwd", 6)
    a_sq = signal("a_sq", 4)
    a_v = signal("a_v", 2)
    a_ss = signal("a_ss")
    a_r = signal("a_r")
    a_qn = signal("a_qn", 2)
    a_kn = signal("a_kn", 2)
    a_back = signal("a_back", 4)
    a_T = signal("a_T", 4)
    a_seg = signal("a_seg", 2)
    a_dec = signal("a_dec", 4)
    a_exp = signal("a_exp", 4)
    a_kk = signal("a_kk", 4)
    a_M = signal("a_M", 2)
    a_attn = signal("a_attn", 2)
    a_N = signal("a_N", 2)
    a_Nc = signal("a_Nc", 2)
    a_X = signal("a_X", 11)
    a_Y = signal("a_Y", 13)
    a_No = signal("a_No", 6)
    a_P = signal("a_P", 12)
    a_Pc = signal("a_Pc", 12)
    a_XP = signal("a_XP", 10)
    a_YP = signal("a_YP", 12)
    a_r0 = signal("a_r0")
    a_kg = signal("a_kg")
    a_vn = signal("a_vn", 2)
    a_vc = signal("a_vc", 2)
    a_S = signal("a_S")
    a_Sc = signal("a_Sc")
    a_kS = signal("a_kS")
    a_qS = signal("a_qS")
    a_r1 = signal("a_r1")
    a_o = signal("a_o", 2)
    a_oc = signal("a_oc", 2)
    o_sq = signal("o_sq", 2)
    o_ss = signal("o_ss", 2)
    o_r = signal("o_r", 2)
    o_made = signal("o_made", 2)
    o_T = signal("o_T", 6)
    oT_made = signal("oT_made", 2)
    bf_read = signal("bf_read")
    bf_s = signal("bf_s")
    b_clamp = signal("b_clamp")
    b_g = signal("b_g")
    b_diff = signal("b_diff", 8)
    b_exp = signal("b_exp", 8)
    b_qk = signal("b_qk", 9)
    b_att = signal("b_att", 9)
    b_masked = signal("b_masked", 9)
    b_od = signal("b_od")
    b_oc = signal("b_oc")
    c_sqd = signal("c_sqd", 6)
    c_ss = signal("c_ss", 6, ahead=1)
    c_r = signal("c_r", 6)
    c_nm = signal("c_nm", 6, ahead=1)
    c_Td = signal("c_Td", 6, ahead=1)
    c_Te = signal("c_Te", 6, ahead=1)
    c_vc = signal("c_vc", 3, ahead=1)
    c_sd = signal("c_sd", 8)
    c_sm = signal("c_sm", 8)
    c_mx = signal("c_mx", 8)
    c_e = signal("c_e", 8)
    c_Pd = signal("c_Pd", 8)
    c_PTc = signal("c_PTc", 8)
    c_od = signal("c_od", 8)
    c_oc = signal("c_oc", 8)
    o_hi_made = signal("o_hi_made", 3)
    o_lo_made = signal("o_lo_made", 3)
    g_tanh = signal("g_tanh", 6)
    g_prod_made = signal("g_prod_made", 6)
    mix_made = signal("mix_made", 4)
    f_silu = signal("f_silu")
    f_gm = signal("f_gm", 1, ahead=2)
    f_gT = signal("f_gT", 1, ahead=2)
    f_hi = signal("f_hi")
    f_lo = signal("f_lo", 1, ahead=2)
    r_done = signal("r_done")
    r_read = signal("r_read")
    r_e = signal("r_e")
    r_sel = signal("r_sel")
    r_cnt = signal("r_cnt")
    r_flag_made = signal("r_flag_made")
    slots_here = signal("slots_here")
    fn_hi_made = signal("fn_hi_made")
    fn_lo_made = signal("fn_lo_made")
    pick0 = signal("pick0")
    pick_made = signal("pick_made")
    pickT_done = signal("pickT_done", 1, ahead=1)
    pickT_made = signal("pickT_made")
    e_done = signal("e_done", 1, ahead=1)
    e_hi_made = signal("e_hi_made")
    e_lo_made = signal("e_lo_made", 1, ahead=1)
    y_hi_made = signal("y_hi_made")
    y_lo_made = signal("y_lo_made", 1, ahead=1)
    s_done = signal("s_done")
    s_read = signal("s_read", 1, ahead=1)
    x_last = signal("x_last")
    out_here = signal("out_here")

    def unit_view(t, k):
        return t[:, :].rearrange("p (k n) -> p k n", k=k)

    def wide(ap, n):
        return ap.unsqueeze(2).broadcast_to([P, ap.shape[1], n])

    def over(ap, m):
        return ap.unsqueeze(1).broadcast_to([P, m, ap.shape[1]])

    ones = ones_t[:, :]

    def second_turn(eng, prog):
        eng.wait_ge(r_flag_made.sem, 1)
        return eng.value_load(r_flag[0:1, 0:1], min_val=0, max_val=1)

    block = ctx.enter_context(nc.Block())

    @block.tensor
    def _(pe):
        prog = Program(None)
        for sig in (c_Td, e_done, pickT_done, f_gT):
            pe.sem_inc(sig.sem, sig.ahead)

        def products(out, a_hi, a_lo, b_hi, b_lo, first, last):
            pe.matmul(out, a_hi, b_hi, start=first, stop=False, skip_group_check=True)
            pe.matmul(out, a_hi, b_lo, start=False, stop=False, skip_group_check=True)
            return pe.matmul(out, a_lo, b_hi, start=False, stop=last, skip_group_check=True)

        def unit_ready():
            pe.wait_ge(hi_made.sem, prog.unit(1))
            pe.wait_ge(lo_made.sem, prog.unit(1))
            return hi[prog.u % SPLIT], lo[prog.u % RAW]

        def unit_over(ins):
            ins.then_inc(unit_used.sem, 1)
            prog.u += 1

        def turn_input(tile, idx, L, half_made=None):
            for j in range(4):
                if half_made and j % 2 == 0:
                    pe.wait_ge(half_made.sem, half_made.at(L, 2 + j // 2))
                for kk in range(2):
                    for t in range(TT):
                        k = 2 * j + kk
                        ins = pe.transpose(PS[:, 4 + j, (2 * kk + t) * P:(2 * kk + t + 1) * P],
                                           tile(t, k), ident)
                ins.then_inc(turned.sem, 1)
            pe.wait_ge(actT_lo_made.sem, actT_lo_made.at(L, idx + 3))

        def group_T(pair):
            for half in range(2):
                w_hi, w_lo = unit_ready()
                for ct in range(4):
                    out = PS[:, 2 * pair + ct // 2, (ct % 2) * T:(ct % 2 + 1) * T]
                    for k in range(4):
                        a = half * 4 + k
                        c = slice(ct * P, (ct + 1) * P)
                        ins = products(out, unit_view(w_hi, 4)[:, k, c], unit_view(w_lo, 4)[:, k, c],
                                       actT_hi[:, a, :], actT_lo[:, a, :],
                                       first=half == 0 and k == 0 and ct % 2 == 0, last=half == 1 and k == 3)
                unit_over(ins)

        def group_nat(pair, halves=(0, 1)):
            for half in halves:
                w_hi, w_lo = unit_ready()
                for t in range(TT):
                    for k in range(4):
                        a = half * 4 + k
                        ins = products(PS[:, 2 * pair + t, :],
                                       actT_hi[:, a, t * P:(t + 1) * P], actT_lo[:, a, t * P:(t + 1) * P],
                                       unit_view(w_hi, 4)[:, k, :], unit_view(w_lo, 4)[:, k, :],
                                       first=half == 0 and k == 0, last=half == 1 and k == 3)
                unit_over(ins)

        def heads(fn):
            for h in range(H):
                ins = fn(h)
            return ins

        def mm(out, a, b, first=True, last=True):
            return pe.matmul(out, a, b, start=first, stop=last)

        def hs(h):
            return slice(h * P, (h + 1) * P)

        pe.wait_ge(consts_here.sem, 32)
        pe.wait_ge(rows_here.sem, 16 * N_ROW_LOADS)
        pe.transpose(PS[:, 0, 0:R_N], rows[0:R_N, :], ident[0:R_N, 0:R_N]).then_inc(rows_T.sem, 1)
        pe.wait_ge(table_here.sem, 17)
        for g in range(GROUPS):
            ins = pe.matmul(PS[0:H, 1 + g, 0:DIST], table[:, g * H:(g + 1) * H], picks[:, g, :],
                            start=True, stop=True)
        ins.then_inc(by_dist_done.sem, 1)

        def spread_bias(first):
            pe.wait_ge(ab_read.sem, ab_read.at(0))
            pe.wait_ge(hankel_here.sem, 16)
            for n in range(first, first + 3):
                if n >= 3:
                    pe.wait_ge(bias_kept.sem, n - 2)
                mm(PS[:, 4 + n % 3, :], consts[:, K_FLIP, :],
                   hankel[:, 2 * n:2 * n + 2, :].rearrange("p a b -> p (a b)")).then_inc(bias_done.sem, 1)

        def narrow_product(b, w):
            for k in range(KT):
                ins = products(PS[0:8, b, 0:T], ab_hi[:, w, k, :], ab_lo[:, w, k, :],
                               actT_hi[:, k, :], actT_lo[:, k, :], first=k == 0, last=k == KT - 1)
            ins.then_inc(n_done.sem, 1)

        def turn_narrow(b, w):
            pe.wait_ge(n_kept.sem, w + 1)
            for t in range(TT):
                ins = pe.transpose(PS[:, b, 8 * t:8 * t + 8], narrow[:, t * P:(t + 1) * P], ident[0:8, 0:8])
            return ins

        def mixer(L):
            pe.wait_ge(norm_made.sem, norm_made.at(L, 1))
            turn_input(lambda t, k: hn[:, t, k * P:(k + 1) * P], 0, L)
            pe.wait_ge(ab_split.sem, 2)
            narrow_product(5, L)
            for g in range(3):
                pair = g % 2
                if g == 0 and L == 0:
                    pe.wait_ge(rows_kept.sem, 1)
                    pe.wait_ge(by_dist_kept.sem, 1)
                if g == 2:
                    pe.wait_ge(a_raw.sem, a_raw.at(L, 1))
                group_T(pair)
                if g == 0:
                    turn_narrow(4, L).then_inc(ab_done.sem, 1)
                if g and L == 0:
                    spread_bias(3 * (g - 1))
            pe.wait_ge(a_raw.sem, a_raw.at(L, 3))
            group_nat(1)
            pe.wait_ge(*((ab_read.sem, ab_read.at(L)) if L else (bias_kept.sem, 4)))
            pe.wait_ge(a_g.sem, a_g.at(L))
            mm(PS[:, 4, 0:H], gt, a_s[:, 8, 0:H])
            mm(PS[:, 4, H:2 * H], le, a_s[:, 8, H:2 * H]).then_inc(a_cum.sem, 1)
            pe.wait_ge(a_raw.sem, a_raw.at(L, 5))
            group_T(0)
            pe.wait_ge(gate_made.sem, gate_made.at(L, 0))
            group_T(1)
            deltanet(L)
            hgrn(L)
            dilated(L)
            branch_part(L, 4, 0, 3)
            branch_part(L, 4, 1, 3)
            branch_part(L, 5, 0, 0)
            branch_part(L, 5, 1, 0)
            turn_input(lambda t, k: gates[k // 4][:, t, hs(k % 4)], 4, L, mix_made)
            for half in range(2):
                group_nat(half)

        def deltanet(L):
            fwd_bank = (4, 5, 6, 7, 0, 1)
            pe.wait_ge(a_silu.sem, a_silu.at(L, 2))
            for c in range(TT):
                for g in range(3):
                    b = fwd_bank[3 * c + g]
                    if c == 0 and g == 0:
                        pe.wait_ge(a_cum_e.sem, a_cum_e.at(L))
                        if L == 0:
                            pe.wait_ge(bias_kept.sem, 6)
                    if b == 0:
                        pe.wait_ge(gate_made.sem, gate_made.at(L, 1))
                    heads(lambda h: pe.transpose(PS[:, b, hs(h)], a_act[:, g * H + h, c * P:(c + 1) * P], ident)).then_inc(a_fwd.sem, 1)
            pe.wait_ge(bf_read.sem, bf_read.at(L))
            group_nat(1)
            for n, (made, c, src, b) in enumerate(((a_qn, 0, t_x, 4), (a_qn, 1, t_x, 7),
                                                   (a_kn, 0, k_nat, 5), (a_kn, 1, k_nat, 0))):
                pe.wait_ge(made.sem, made.at(L, c))
                heads(lambda h: pe.transpose(PS[:, b, hs(h)], src[:, c, h, :], ident)).then_inc(a_back.sem, 1)
            pe.wait_ge(a_v.sem, a_v.at(L, 1))
            for n, (b, lhs, rhs) in enumerate(((6, le, t_m), (1, le, t_m), (2, gt, t_n), (3, gt, t_n))):
                if n == 2:
                    pe.wait_ge(gate_made.sem, gate_made.at(L, 2))
                pe.wait_ge(a_seg.sem, a_seg.at(L, n // 2))
                mm(PS[:, b, :], lhs, rhs[:, n % 2].rearrange("p h j -> p (h j)")).then_inc(a_dec.sem, 1)
            qT, kT = a_act[:, 0:H, :], a_act[:, H:2 * H, :]
            pe.wait_ge(a_T.sem, a_T.at(L, 3))
            for n, (b, c, rhs) in enumerate(((4, 0, kT), (7, 1, kT), (5, 0, qT), (0, 1, qT))):
                heads(lambda h: mm(PS[:, b, hs(h)], kT[:, h, c * P:(c + 1) * P],
                                   rhs[:, h, c * P:(c + 1) * P])).then_inc(a_kk.sem, 1)
            pe.wait_ge(a_exp.sem, a_exp.at(L, 3))
            group_nat(1, (0,))
            for c in range(TT):
                pe.wait_ge(a_M.sem, a_M.at(L, c))
                heads(lambda h: pe.transpose(PS[:, (6, 1)[c], hs(h)], t_m[:, c, h, :], ident)).then_inc(a_N.sem, 1)
            group_nat(1, (1,))
            for lv in range(1, LEVELS):
                for c in range(TT):
                    pe.wait_ge(a_No.sem, a_No.at(L, lv - 1))
                    pe.wait_ge(a_X.sem, a_X.at(L, 2 * lv - 3 + c if lv > 1 else 0))
                    heads(lambda h: mm(PS[:, 4 + c, hs(h)], t_w[:, c, h, :], t_x[:, c, h, :])).then_inc(a_P.sem, 1)
                for c in range(TT):
                    pe.wait_ge(a_Pc.sem, a_Pc.at(L, 2 * (lv - 1) + c))
                    pe.wait_ge(a_Y.sem, a_Y.at(L, 2 * lv - 3 + c if lv > 1 else 0))
                    if lv < LEVELS - 1:
                        heads(lambda h: mm(PS[:, 6 + c, hs(h)], t_y[:, c, h, :], t_m[:, c, h, :])).then_inc(a_XP.sem, 1)
                    heads(lambda h: mm(PS[:, c, hs(h)], t_m[:, c, h, :], t_y[:, c, h, :])).then_inc(a_YP.sem, 1)
            pe.wait_ge(a_r0.sem, a_r0.at(L))
            pe.wait_ge(a_Y.sem, a_Y.at(L, 11))
            heads(lambda h: mm(PS[:, 4, hs(h)], t_y[:, 0, h, :], t_w[:, 0, h, :])).then_inc(a_vn.sem, 1)
            pe.wait_ge(a_vc.sem, a_vc.at(L, 0))
            pe.wait_ge(a_kg.sem, a_kg.at(L))
            heads(lambda h: mm(PS[:, 5, hs(h)], t_v[:, 0, h, :], t_x[:, 0, h, :])).then_inc(a_S.sem, 1)
            pe.wait_ge(a_attn.sem, a_attn.at(L, 1))
            pe.wait_ge(gate_tanh.sem, gate_tanh.at(L, 2))
            heads(lambda h: mm(PS[:, 2, hs(h)], attn[:, 0, h, :], t_x[:, 0, h, :])).then_inc(a_o.sem, 1)
            pe.wait_ge(a_Sc.sem, a_Sc.at(L))
            heads(lambda h: mm(PS[:, 6, hs(h)], kT[:, h, P:T], t_x[:, 1, h, :])).then_inc(a_kS.sem, 1)
            heads(lambda h: mm(PS[:, 7, hs(h)], qT[:, h, P:T], t_x[:, 1, h, :])).then_inc(a_qS.sem, 1)
            pe.wait_ge(a_r1.sem, a_r1.at(L))
            pe.wait_ge(a_Y.sem, a_Y.at(L, 12))
            heads(lambda h: mm(PS[:, 4, hs(h)], t_y[:, 1, h, :], t_w[:, 1, h, :])).then_inc(a_vn.sem, 1)
            pe.wait_ge(a_vc.sem, a_vc.at(L, 1))
            heads(lambda h: mm(PS[:, 3, hs(h)], attn[:, 1, h, :], t_m[:, 0, h, :])).then_inc(a_o.sem, 1)
            group_nat(0)
            turn_output(L, 0, t_n)

        def turn_output(L, br, src):
            if br < 2:
                pe.wait_ge(o_made.sem, o_made.at(L, br))
            else:
                pe.wait_ge(c_oc.sem, c_oc.at(L, 7))
            for h in range(H):
                for t in range(TT):
                    a = src[:, t, h, :] if len(src.shape) == 4 else src[:, t, hs(h)]
                    ins = pe.transpose(PS[:, 4 + h // 2, ((h % 2) * TT + t) * P:((h % 2) * TT + t + 1) * P],
                                       a, ident)
                if h % 2:
                    ins.then_inc(o_T.sem, 1)

        def hgrn(L):
            units = iter([(g, half) for g in range(1, 6) for half in range(2)])
            for n in range(LEVELS + 2):
                pe.wait_ge(b_qk.sem, b_qk.at(L, n))
                if n == LEVELS + 1:
                    pe.wait_ge(g_tanh.sem, g_tanh.at(L, 4))
                    heads(lambda h: mm(PS[:, 0, hs(h)], b_ke[:, h, 0:P], b_qe[:, h, P:T])).then_inc(b_att.sem, 1)
                else:
                    pair = (4, 6)[n % 2]
                    k, q = (b_ke, b_qe) if n else (b_k, b_q)
                    for c in range(TT):
                        for h in range(H):
                            t = slice(c * P, (c + 1) * P)
                            ins = mm(PS[:, pair + c, hs(h)], k[:, h, t], q[:, h, t])
                    ins.then_inc(b_att.sem, 1)
                for _ in range(1 if n else 2):
                    g, half = next(units)
                    if half == 0:
                        pe.wait_ge(g_tanh.sem, g_tanh.at(L, max(g - 2, 0)))
                    group_nat(g % 2, (half,))
            pe.wait_ge(b_masked.sem, b_masked.at(L, LEVELS + 1))
            for h in range(H):
                mm(PS[:, 4, hs(h)], b_attn[:, 0, h, :], b_i[:, 0, hs(h)])
                mm(PS[:, 5, hs(h)], b_attn[:, 1, h, :], b_i[:, 1, hs(h)], last=False)
                ins = mm(PS[:, 5, hs(h)], b_attn[:, 2, h, :], b_i[:, 0, hs(h)], first=False)
            ins.then_inc(b_od.sem, 1)

        def dilated(L):
            pe.wait_ge(g_tanh.sem, g_tanh.at(L, 5))
            with prog.loop(pe, GROUPS, 0) as g:
                pe.wait_ge(c_nm.sem, c_nm.count(L * 6 + 2 * g))
                group_nat(0)
                group_nat(1)

                def turn_c(j):
                    pe.wait_ge(c_nm.sem, c_nm.count(L * 6 + 2 * g + j + 1))
                    pe.wait_ge(c_Te.sem, c_Te.count(L * 6 + 2 * g + j))
                    for h in range(H):
                        for t in range(TT):
                            ins = pe.transpose(PS[:, 4 + h // 2, ((h % 2) * TT + t) * P:((h % 2) * TT + t + 1) * P],
                                               c_n[:, t, hs(h)], ident)
                    ins.then_inc(c_Td.sem, 1)

                turn_c(0)
                pe.wait_ge(c_vc.sem, c_vc.count(L * 3 + g))
                group_nat(3)
                turn_c(1)
            pe.wait_ge(c_nm.sem, c_nm.at(L, 5))
            pe.wait_ge(c_vc.sem, c_vc.at(L, 2))
            pe.wait_ge(c_Te.sem, c_Te.at(L, 5))
            turn_output(L, 1, b_o)
            def scores(n):
                t, h = divmod(n, H)
                keys = (t + 1) * P
                if n:
                    pe.wait_ge(c_sm.sem, c_sm.at(L, n - 1))
                for g in range(GROUPS):
                    out = PS[:, g // 2, (g % 2) * T:(g % 2) * T + keys]
                    ins = mm(out, c_qT[:, g * H + h, t * P:(t + 1) * P], c_kT[:, g * H + h, 0:keys])
                ins.then_inc(c_sd.sem, 1)

            def tiles(n):
                return [(g, s) for g in range(GROUPS) for s in range(n // H + 1)]

            def turn_p(n):
                if n == 0:
                    pe.wait_ge(oT_made.sem, oT_made.at(L, 1))
                pe.wait_ge(c_e.sem, c_e.at(L, n))
                for m, (g, s) in enumerate(tiles(n)):
                    at = g * T + s * P
                    ins = pe.transpose(PS[:, 4 + m // 4, (m % 4) * P:(m % 4 + 1) * P], c_p[:, at:at + P], ident)
                ins.then_inc(c_Pd.sem, 1)

            def values(n):
                if n >= 2:
                    pe.wait_ge(c_oc.sem, c_oc.at(L, n - 2))
                pe.wait_ge(c_PTc.sem, c_PTc.at(L, n))
                for m, (g, s) in enumerate(tiles(n)):
                    ins = mm(PS[:, 2 + n % 2, 0:P], c_pT[:, m * P:(m + 1) * P],
                             c_v[:, s, g, hs(n % H)], first=m == 0, last=m == len(tiles(n)) - 1)
                ins.then_inc(c_od.sem, 1)

            scores(0)
            branch_part(L, 0, 0, 3)
            for n in range(TT * H):
                if n + 1 < TT * H:
                    scores(n + 1)
                turn_p(n)
                if n + 1 < TT * H:
                    branch_part(L, (n + 1) // 2, (n + 1) % 2, 3)
                values(n)
            turn_output(L, 2, c_o)

        def branch_part(L, k, t, pair):
            n = k // 2 % 2
            if t == 0:
                pe.wait_ge(o_lo_made.sem, o_lo_made.at(L, k // 2))
                if k:
                    pe.wait_ge(g_prod_made.sem, g_prod_made.at(L, k - 1))
            w_hi, w_lo = unit_ready()
            for j in range(H):
                ins = products(PS[:, 2 * pair + t, :], o_hi[n][:, j, t * P:(t + 1) * P],
                               o_lo[n][:, j, t * P:(t + 1) * P], unit_view(w_hi, 4)[:, j, :],
                               unit_view(w_lo, 4)[:, j, :], first=j == 0, last=j == H - 1)
            if t == TT - 1:
                unit_over(ins)

        def dense():
            pe.wait_ge(norm_made.sem, norm_made.at(0, 3))
            turn_input(lambda t, k: fn[:, t, k * P:(k + 1) * P], 8, 0)

            def up(m, s):
                pe.wait_ge(f_gm.sem, f_gm.count(m - 1))
                for w in range(2):
                    w_hi, w_lo = unit_ready()
                    for j in range(2):
                        for k in range(KT):
                            c = slice(j * P, (j + 1) * P)
                            ins = products(PS[:, 2 * s + j, w * T:(w + 1) * T],
                                           unit_view(w_hi, 8)[:, k, c], unit_view(w_lo, 8)[:, k, c],
                                           actT_hi[:, k, :], actT_lo[:, k, :], first=k == 0, last=k == KT - 1)
                    unit_over(ins)

            def down(m, s, first=False, last=False):
                pe.wait_ge(f_lo.sem, f_lo.count(m + 1))
                w_hi, w_lo = unit_ready()
                for t in range(TT):
                    for half in range(2):
                        for k in range(2):
                            c, d = slice(t * P, (t + 1) * P), slice(half * 512, (half + 1) * 512)
                            ins = products(PS[:, 4 + 2 * t + half, :], fT_hi[s][:, k, c], fT_lo[s][:, k, c],
                                           unit_view(w_hi, 2)[:, k, d], unit_view(w_lo, 2)[:, k, d],
                                           first=first and k == 0, last=last and k == 1)
                unit_over(ins)

            up(0, 0)
            up(1, 1)
            down(0, 0, first=True)
            with prog.loop(pe, STEPS_DENSE // 2 - 1, 0) as i:
                m = 2 * i + 2
                up(m, 0)
                down(m - 1, 1)
                up(m + 1, 1)
                down(m, 0)
            up(STEPS_DENSE - 1, 0)
            down(STEPS_DENSE - 2, 1)
            down(STEPS_DENSE - 1, 0, last=True)

        def gather(n):
            pe.wait_ge(pick_made.sem, n + 1)
            for k in range(KT):
                for t in range(TT):
                    for part, src in enumerate((fn_hi, fn_lo)):
                        ins = pe.matmul(PS[:, 6 + k // 4, (k % 4) * P:(k % 4 + 1) * P],
                                        src[:, t, k * P:(k + 1) * P], pick_r[:, t, :],
                                        start=t == 0 and part == 0, stop=t == 1 and part == 1)
                if k % 4 == 3:
                    ins.then_inc(e_done.sem, 1)

        def scatter(n):
            pe.wait_ge(pickT_made.sem, n + 1)
            pe.wait_ge(y_lo_made.sem, y_lo_made.count(n + 1))
            for t in range(TT):
                for half in range(2):
                    for part, src in enumerate((y_hi, y_lo)):
                        ins = pe.matmul(PS[:, 4 + 2 * t + half, :], pickT[:, t, :],
                                        src[:, half * 512:(half + 1) * 512], start=part == 0, stop=part == 1)
                ins.then_inc(s_done.sem, 1)

        def expert(n, first, last):
            base = STEPS_DENSE + STEPS_EXPERT * n

            def up(m, s):
                pe.wait_ge(f_gm.sem, f_gm.count(m - 1))
                for w in range(2):
                    w_hi, w_lo = unit_ready()
                    for k in range(KT):
                        ins = products(PS[:, s, w * SUB:(w + 1) * SUB], e_hi[:, k, :], e_lo[:, k, :],
                                       unit_view(w_hi, 8)[:, k, :], unit_view(w_lo, 8)[:, k, :],
                                       first=k == 0, last=k == KT - 1)
                    unit_over(ins)

            def turn(m, s):
                pe.wait_ge(f_gm.sem, f_gm.count(m + 1))
                for j in range(2):
                    ins = pe.transpose(PS[:, 2, (2 * s + j) * P:(2 * s + j + 1) * P],
                                       f_g[s][:, j * P:(j + 1) * P], ident)
                ins.then_inc(f_gT.sem, 1)

            def down(m, s, first=False, last=False):
                pe.wait_ge(f_lo.sem, f_lo.count(m + 1))
                w_hi, w_lo = unit_ready()
                for half in range(2):
                    for k in range(2):
                        d = slice(half * 512, (half + 1) * 512)
                        ins = products(PS[:, 4 + half, :], fT_hi[s][:, k, 0:P], fT_lo[s][:, k, 0:P],
                                       unit_view(w_hi, 2)[:, k, d], unit_view(w_lo, 2)[:, k, d],
                                       first=first and k == 0, last=last and k == 1)
                unit_over(ins)

            pe.wait_ge(e_lo_made.sem, e_lo_made.count(2 * n + 2))
            up(base, 0)
            if not first:
                scatter(n - 1)
            for t in range(TT):
                ins = pe.transpose(PS[:, 3, t * P:(t + 1) * P], pick[:, t, :], ident)
            ins.then_inc(pickT_done.sem, 1)
            turn(base, 0)
            up(base + 1, 1)
            if not first:
                pe.wait_ge(s_read.sem, s_read.count(2 * n - 1))
            down(base, 0, first=True)
            turn(base + 1, 1)
            with prog.loop(pe, STEPS_EXPERT // 2 - 1, 0) as i:
                m = base + 2 + 2 * i
                up(m, 0)
                down(m - 1, 1)
                turn(m, 0)
                up(m + 1, 1)
                down(m, 0)
                turn(m + 1, 1)
            if not last:
                if not first:
                    pe.wait_ge(s_read.sem, s_read.count(2 * n))
                gather(n + 1)
            down(base + STEPS_EXPERT - 1, 1, last=True)

        def experts(turn):
            if turn:
                pe.wait_ge(s_read.sem, s_read.count(2 * E * turn))
            gather(E * turn)
            expert(E * turn, True, False)
            with prog.loop(pe, E - 2, 0, rounds=EXPERT_R) as e:
                expert(E * turn + 1 + e, False, False)
            expert(E * turn + E - 1, False, True)
            scatter(E * turn + E - 1)

        def moe():
            pe.wait_ge(norm_made.sem, norm_made.at(1, 3))
            turn_input(lambda t, k: fn[:, t, k * P:(k + 1) * P], 8, 1)
            narrow_product(1, 2)
            turn_narrow(0, 2).then_inc(r_done.sem, 1)
            pe.wait_ge(r_sel.sem, 1)
            mm(PS[:, 1, 0:E], le, r_t[:, 12, 0:E])
            mm(PS[:, 1, E:2 * E], le, r_t[:, 12, E:2 * E], last=False)
            mm(PS[:, 1, E:2 * E], ones, r_t[:, 12, 0:E], first=False)
            mm(PS[:, 1, 2 * E:3 * E], ones, r_t[:, 12, 0:E], last=False)
            mm(PS[:, 1, 2 * E:3 * E], ones, r_t[:, 12, E:2 * E], first=False).then_inc(r_cnt.sem, 1)
            experts(0)
            more = second_turn(pe, prog)
            with pe.If(more > 0):
                experts(1)

        mixer(0)
        dense()
        mixer(1)
        moe()

    @block.scalar
    def _(act):
        prog = Program(act_step)
        for sig in (c_Te, c_vc):
            act.sem_inc(sig.sem, sig.ahead)
        SQ, EXP, LN, TANH, COPY, SILU = (ACT.Square, ACT.Exp, ACT.Ln, ACT.Tanh, ACT.Copy, ACT.Silu)

        def prep(count):
            for _ in range(count):
                slot = prog.u % RAW
                arrived = 16 * (prog.u // RAW + 1)
                act.wait_ge(raw_full[slot].sem, arrived if prog.rounds is None else arrived + prog.rounds * 16)
                if prog.u >= SPLIT:
                    act.wait_ge(unit_used.sem, prog.unit(1 - SPLIT))
                act.activation(hi[prog.u % SPLIT][:, :], raw[slot][:, :], COPY).then_inc(hi_made.sem, 1)
                prog.u += 1

        def used(L, n):
            act.wait_ge(unit_used.sem, LAYER_U[L] + n)

        def rsqrt_of(out, in_, scale, bias_out, sig):
            act.activation(out, in_, LN, bias=eps_t, scale=scale).then_inc(act_step.sem, 1)
            act.wait_ge(act_step.sem, prog.step())
            act.activation(out, out, EXP, bias=bias_out, scale=-0.5).then_inc(sig.sem, 1)

        def load_tables():
            act.preload_act_table_set(LN_EXP_SET)

        def norm_scale(L, phase):
            load_tables()
            if L == 0 and phase == 0:
                act.wait_ge(x_here.sem, 32)
            else:
                act.wait_ge(x_made.sem, x_made.at(L if phase else L - 1, 1 if phase else 2))
            dst = fn if phase else hn
            for t in range(TT):
                act.activation(dst[:, t, :], x[:, t, :], SQ, accum_out=stat[:, t:t + 1]).then_inc(act_step.sem, 1)
                act.wait_ge(act_step.sem, prog.step())
            act.activation(stat[:, 2:4], stat[:, 0:2], LN, bias=eps_t, scale=1.0 / D).then_inc(act_step.sem, 1)
            act.wait_ge(act_step.sem, prog.step())
            act.activation(stat[:, 4:6], stat[:, 2:4], EXP, scale=-0.5).then_inc(norm_r.sem, 1)

        act.wait_ge(tiny_made.sem, 4)
        norm_scale(0, 0)
        act.wait_ge(rows_T.sem, 1)
        act.activation(small[:, :], PS[:, 0, 0:R_N], COPY).then_inc(rows_kept.sem, 1)
        act.wait_ge(rows_kept.sem, 1)
        act.wait_ge(lb_m.sem, 1)
        act.activation(lb[:, 4:6, :], lb[:, 4:6, :], EXP).then_inc(lb_e.sem, 1)
        act.wait_ge(par_here.sem, 32)
        act.activation(a_rate[:, :, :], a_par[:, 0, :, :], EXP).then_inc(a_rate_e.sem, 1)
        act.wait_ge(by_dist_done.sem, 1)
        act.activation(by_dist[:, :, :], PS[0:H, 1:1 + GROUPS, 0:DIST], COPY).then_inc(by_dist_kept.sem, 1)
        act.wait_ge(ab_here.sem, 48)
        act.activation(ab_hi[:, :, :, :], ab[:, :, :, :], COPY).then_inc(ab_split.sem, 1)

        def turn_input(idx, L, scale=1.0):
            for j in range(4):
                act.wait_ge(turned.sem, turned.at(L, idx + j))
                act.activation(actT_hi[:, 2 * j:2 * j + 2, :].rearrange("p a b -> p (a b)"),
                               PS[:, 4 + j, :], COPY, scale=scale).then_inc(actT_hi_made.sem, 1)

        def narrow_kept(b, w):
            act.wait_ge(n_done.sem, w + 1)
            act.activation(narrow[:, :], PS[0:8, b, 0:T], COPY).then_inc(n_kept.sem, 1)

        def mixer(L):
            if L:
                prep(2)
                norm_scale(L, 0)
                prep(1)
            turn_input(0, L)
            if L == 0:
                prep(3)
            narrow_kept(5, L)

            def conv_in(g):
                used(L, 2 * g + 2)
                if g == 0:
                    act.wait_ge(pad_made.sem, L + 1)
                for b in range(2):
                    ct = g * H + 2 * b
                    act.activation(a_in[:, ct:ct + 2, 3:3 + T],
                                   PS[:, 2 * (g % 2) + b, :].rearrange("p (a b) -> p a b", a=2), COPY).then_inc(a_raw.sem, 1)

            def bias_copies(L, first):
                if L == 0:
                    for n in range(first, first + 3):
                        act.wait_ge(bias_done.sem, n + 1)
                        act.activation(bias[:, 2 * n:2 * n + 2, :].rearrange("p a b -> p (a b)"),
                                       PS[:, 4 + n % 3, :], COPY).then_inc(bias_kept.sem, 1)

            def conv_tanh(g):
                act.wait_ge(a_conv.sem, a_conv.at(L, g))
                act.activation((t_x, t_y, t_w)[g][:, :, :, :].rearrange("p a b c -> p (a b c)"),
                               a_act[:, g * H:(g + 1) * H, :].rearrange("p a b -> p (a b)"), TANH, scale=0.5).then_inc(a_tanh.sem, 1)

            prep(2)
            conv_in(0)
            act.wait_ge(ab_read.sem, ab_read.at(L))
            act.activation(a_s[:, 3, :], a_s[:, 2, :], EXP, scale=-1.0).then_inc(act_step.sem, 1)
            act.wait_ge(act_step.sem, prog.step())
            act.activation(a_s[:, 5, :], a_s[:, 4, :], EXP, scale=-1.0).then_inc(a_e1.sem, 1)
            act.wait_ge(a_e1.sem, a_e1.at(L))
            act.preload_act_table_set(LN_SET)
            act.activation(a_s[:, 6, :], a_s[:, 5, :], LN, bias=one_t).then_inc(a_e2.sem, 1)
            prep(2)
            conv_in(1)
            bias_copies(L, 0)
            conv_tanh(0)
            prep(2)
            conv_in(2)
            bias_copies(L, 3)
            conv_tanh(1)
            prep(2)
            used(L, 8)
            conv_tanh(2)
            act.activation(t_v[:, :, :, :].rearrange("p a b c -> p (a b c)"),
                           PS[:, 2:4, :].rearrange("p a b -> p (a b)"), TANH, scale=0.5).then_inc(gate_tanh.sem, 1)
            act.wait_ge(a_cum.sem, a_cum.at(L))
            act.activation(a_s[:, 11, :], PS[:, 4, 0:2 * H], EXP).then_inc(a_cum_e.sem, 1)
            prep(2)
            used(L, 10)
            act.activation(b_q[:, :, :].rearrange("p a b -> p (a b)"),
                           PS[:, 0:2, :].rearrange("p a b -> p (a b)"), TANH, scale=0.5).then_inc(gate_tanh.sem, 1)
            prep(2)
            load_tables()
            act.wait_ge(bf_read.sem, bf_read.at(L))
            bf = b_f[:, :, :].rearrange("p a b -> p (a b)")
            act.activation(bf, bf, EXP, scale=-1.0).then_inc(act_step.sem, 1)
            act.wait_ge(act_step.sem, prog.step())
            act.activation(bf, bf, LN, bias=one_t).then_inc(act_step.sem, 1)
            act.wait_ge(act_step.sem, prog.step())
            act.activation(bf, bf, EXP, scale=-1.0).then_inc(bf_s.sem, 1)
            deltanet(L)
            hgrn(L)
            dilated(L)
            turn_input(4, L, scale=0.5)
            prep(1)

        def flat(t):
            return t[:, :, :, :].rearrange("p a b c -> p (a b c)") if len(t.shape) == 4 else \
                t[:, :, :].rearrange("p a b -> p (a b)")

        def bank(*b):
            return PS[:, b[0], :] if len(b) == 1 else PS[:, b[0]:b[1] + 1, :].rearrange("p a b -> p (a b)")

        def chunk(t, c):
            return t[:, c].rearrange("p h j -> p (h j)")

        def deltanet(L):
            for c in range(TT):
                for g, dst in ((0, t_w), (1, t_v)):
                    act.wait_ge(a_fwd.sem, a_fwd.at(L, 3 * c + g))
                    act.activation(chunk(dst, c), bank((4, 5, 6, 7, 0, 1)[3 * c + g]), SQ).then_inc(a_sq.sem, 1)
                act.wait_ge(a_fwd.sem, a_fwd.at(L, 3 * c + 2))
                act.activation(chunk(v_nat, c), bank((6, 1)[c]), COPY).then_inc(a_v.sem, 1)
            act.wait_ge(a_ss.sem, a_ss.at(L))
            act.activation(a_s[:, 13:15, :], a_s[:, 9:11, :], LN, bias=eps_t).then_inc(act_step.sem, 1)
            act.wait_ge(act_step.sem, prog.step())
            act.activation(a_s[:, 15, :], a_s[:, 13, :], EXP, bias=lnq_t, scale=-0.5).then_inc(act_step.sem, 1)
            act.wait_ge(act_step.sem, prog.step())
            act.activation(a_s[:, 16, :], a_s[:, 14, :], EXP, scale=-0.5).then_inc(a_r.sem, 1)
            prep(2)
            act.wait_ge(a_conv.sem, a_conv.at(L, 2))
            act.wait_ge(gate_made.sem, gate_made.at(L, 1))
            used(L, 14)
            act.activation(flat(b_i), bank(2, 3), COPY).then_inc(gate_made.sem, 1)
            for n, (b, ct, c) in enumerate(((4, 0, 0), (7, 0, 1), (5, H, 0), (0, H, 1))):
                act.wait_ge(a_back.sem, a_back.at(L, n))
                act.activation(a_act[:, ct:ct + H, c * P:(c + 1) * P],
                               bank(b).rearrange("p (h j) -> p h j", h=H), COPY).then_inc(a_T.sem, 1)
            for n, (b, dst) in enumerate(((6, t_x), (1, t_x), (2, t_y), (3, t_y))):
                act.wait_ge(a_dec.sem, a_dec.at(L, n))
                act.activation(chunk(dst, n % 2), bank(b), EXP).then_inc(a_exp.sem, 1)
            prep(1)
            for c in range(TT):
                act.wait_ge(a_N.sem, a_N.at(L, c))
                act.activation(chunk(t_n, c), bank((6, 1)[c]), COPY).then_inc(a_Nc.sem, 1)
            prep(1)
            used(L, 16)
            act.activation(flat(b_gate), bank(2, 3), TANH, scale=0.5).then_inc(gate_tanh.sem, 1)
            for lv in range(1, LEVELS):
                for c in range(TT):
                    act.wait_ge(a_P.sem, a_P.at(L, 2 * (lv - 1) + c))
                    act.activation(chunk(t_m, c), bank(4 + c), COPY).then_inc(a_Pc.sem, 1)
            act.wait_ge(a_vn.sem, a_vn.at(L, 0))
            act.activation(chunk(t_x, 0), bank(4), COPY).then_inc(a_vc.sem, 1)
            act.wait_ge(a_S.sem, a_S.at(L))
            act.activation(chunk(t_x, 1), bank(5), COPY).then_inc(a_Sc.sem, 1)
            act.wait_ge(a_o.sem, a_o.at(L, 0))
            act.activation(chunk(t_n, 0), bank(2), COPY).then_inc(a_oc.sem, 1)
            act.wait_ge(a_vn.sem, a_vn.at(L, 1))
            act.activation(chunk(t_m, 0), bank(4), COPY).then_inc(a_vc.sem, 1)
            output_norm(L, 0, t_n, t_y, a_oc)
            turn_output(L, 0)

        def output_norm(L, br, src, tmp, made):
            load_tables()
            act.wait_ge(made.sem, made.at(L, made.per_layer - 1))
            act.activation(flat(tmp), flat(src), SQ).then_inc(o_sq.sem, 1)
            act.wait_ge(o_ss.sem, o_ss.at(L, br))
            act.activation(a_s[:, 18, :], a_s[:, 17, :], LN, bias=eps_t, scale=1.0 / P).then_inc(act_step.sem, 1)
            act.wait_ge(act_step.sem, prog.step())
            act.activation(a_s[:, 19, :], a_s[:, 18, :], EXP, scale=-0.5).then_inc(o_r.sem, 1)

        def turn_output(L, br):
            act.wait_ge(o_T.sem, o_T.at(L, 2 * br + 1))
            col = (R_GA, R_GB)[br] + L
            act.activation(oT[:, br, :, :].rearrange("p a b -> p (a b)"), bank(4, 5), COPY,
                           scale=small[:, col:col + 1]).then_inc(oT_made.sem, 1)

        def hgrn(L):
            prep(1)
            act.preload_act_table_set(LN_SET)
            act.wait_ge(b_clamp.sem, b_clamp.at(L))
            act.activation(flat(b_f), flat(b_f), LN).then_inc(b_g.sem, 1)

            def gate(k):
                act.activation(flat(gates[k]), bank(2 * (k % 2), 2 * (k % 2) + 1), TANH,
                               scale=0.5).then_inc(g_tanh.sem, 1)

            def exps(n):
                s = 1 << n
                act.wait_ge(b_diff.sem, b_diff.at(L, n))
                v = flat(b_e).rearrange("p (n s) -> p n s", s=2 * s)
                act.activation(v[:, :, s:2 * s], v[:, :, s:2 * s], EXP).then_inc(act_step.sem, 1)
                act.wait_ge(act_step.sem, prog.step())
                act.activation(v[:, :, 0:s], v[:, :, 0:s], EXP, scale=-1.0).then_inc(b_exp.sem, 1)

            prep(1)
            used(L, U_GATES + 2)
            gate(0)
            exps(0)
            for n in range(LEVELS + 2):
                prep(1 if n else 2)
                if n < LEVELS:
                    exps(n + 1)
                if n % 2 == 0:
                    used(L, U_GATES + 4 + n)
                    gate(1 + n // 2)
            act.wait_ge(b_od.sem, b_od.at(L))
            act.activation(flat(b_o), bank(4, 5), COPY).then_inc(b_oc.sem, 1)
            output_norm(L, 1, b_o, b_o2, b_oc)

        def dilated(L):
            act.wait_ge(o_made.sem, o_made.at(L, 1))
            with prog.loop(act, GROUPS, 2) as g:
                u = LAYER_U[L] + U_C + 6 * g

                def square(j):
                    act.wait_ge(unit_used.sem, u + 2 * j + 2)
                    act.wait_ge(c_ss.sem, c_ss.count(L * 6 + 2 * g + j))
                    act.activation(flat(c_sq), bank(2 * j, 2 * j + 1), SQ).then_inc(c_sqd.sem, 1)
                    act.wait_ge(c_ss.sem, c_ss.count(L * 6 + 2 * g + j + 1))
                    rsqrt_of(stat[:, 8:16], stat[:, 0:8], 1.0 / P, zero_t, c_r)

                def turned_c(j):
                    act.wait_ge(c_Td.sem, c_Td.count(L * 6 + 2 * g + j + 1))
                    dst = (c_qT, c_kT)[j]
                    col = (R_QN, R_KN)[j] + L * GROUPS
                    act.activation(dst[:, bass.ds(g * H, H), :].rearrange("p a b -> p (a b)"), bank(4, 5),
                                   COPY, scale=small[:, bass.ds(g + col, 1)]).then_inc(c_Te.sem, 1)

                prep(2)
                square(0)
                prep(2)
                turned_c(0)
                square(1)
                prep(2)
                act.wait_ge(unit_used.sem, u + 6)
                act.activation(c_v[:, :, bass.ds(g, 1), :].rearrange("p t o n -> p t (o n)"),
                               PS[:, 6:8, :], COPY).then_inc(c_vc.sem, 1)
                turned_c(1)
            used(L, U_C + 18)
            split_branch(L, 0)
            turn_output(L, 1)

            def copies(n):
                act.wait_ge(c_Pd.sem, c_Pd.at(L, n))
                if n:
                    act.wait_ge(c_od.sem, c_od.at(L, n - 1))
                w = GROUPS * (n // H + 1) * P
                act.activation(c_pT[:, 0:w], PS[:, 4:6, :].rearrange("p a b -> p (a b)")[:, 0:w],
                               COPY).then_inc(c_PTc.sem, 1)

            def exps(n):
                keys = (n // H + 1) * P
                st = 4 * (n % 2)
                act.wait_ge(c_mx.sem, c_mx.at(L, n))
                act.activation(c_p[:, :].rearrange("p (g s) -> p g s", g=GROUPS)[:, :, 0:keys],
                               c_s[:, :].rearrange("p (g s) -> p g s", g=GROUPS)[:, :, 0:keys],
                               EXP, bias=stat[:, st + 1:st + 2],
                               accum_out=stat[:, st + 2:st + 3]).then_inc(c_e.sem, 1)

            exps(0)
            act.wait_ge(oT_made.sem, oT_made.at(L, 1))
            split_branch(L, 1)
            for n in range(TT * H):
                copies(n)
                if n + 1 < TT * H:
                    exps(n + 1)
                if n % 2 == 0:
                    prep(1)
            act.wait_ge(o_T.sem, o_T.at(L, 5))
            act.activation(flat(o_hi[0]), bank(4, 5), COPY).then_inc(o_hi_made.sem, 1)
            prep(2)

        def split_branch(L, br):
            act.activation(flat(o_hi[br % 2]), oT[:, br, :, :].rearrange("p a b -> p (a b)"),
                           COPY).then_inc(o_hi_made.sem, 1)

        def dense():
            prep(2)
            norm_scale(0, 1)
            prep(1)
            turn_input(8, 0)
            U = LAYER_U[0] + U_FF

            def half_step(m, s, used, preps=(1, 2)):
                act.wait_ge(unit_used.sem, used)
                act.wait_ge(f_gm.sem, f_gm.count(m - 1))
                act.activation(f_s[s][:, :].rearrange("p (j t) -> p j t", j=2),
                               PS[:, 2 * s:2 * s + 2, 0:T], SILU).then_inc(f_silu.sem, 1)
                prep(preps[0])
                act.wait_ge(f_gm.sem, f_gm.count(m + 1))
                act.activation(fT_hi[s][:, :, :].rearrange("p a b -> p (a b)"), f_g[s][:, :],
                               COPY).then_inc(f_hi.sem, 1)
                prep(preps[1])

            half_step(0, 0, U + 2)
            with prog.loop(act, STEPS_DENSE // 2 - 1, 0) as i:
                m = 2 * i + 1
                half_step(m, 1, U + 1 + 3 * m)
                half_step(m + 1, 0, U + 4 + 3 * m)
            m = STEPS_DENSE - 2
            half_step(m, 1, U + 1 + 3 * m)
            half_step(m + 1, 0, U + 4 + 3 * m, (0, 0))

        def tokens(n):
            for j in range(2):
                act.wait_ge(e_done.sem, e_done.count(2 * n + j + 1))
                act.activation(e_hi[:, 4 * j:4 * j + 4, :].rearrange("p a b -> p (a b)"), bank(6 + j),
                               COPY).then_inc(e_hi_made.sem, 1)

        def expert(n, U, last):
            base = STEPS_DENSE + STEPS_EXPERT * n

            def silu(m, s, used):
                act.wait_ge(unit_used.sem, used)
                act.wait_ge(f_gm.sem, f_gm.count(m - 1))
                act.activation(f_s[s][:, 0:SUB], PS[:, s, 0:SUB], SILU).then_inc(f_silu.sem, 1)

            def high(m, s):
                act.wait_ge(f_gT.sem, f_gT.count(m - STEPS_DENSE + 1))
                act.activation(fT_hi[s][:, :, 0:P],
                               PS[:, 2, s * SUB:(s + 1) * SUB].rearrange("p (j t) -> p j t", j=2), COPY).then_inc(f_hi.sem, 1)

            silu(base, 0, U + 2)
            prep(1)
            act.wait_ge(pickT_done.sem, pickT_done.count(n + 1))
            act.activation(flat(pickT), PS[:, 3, 0:T], COPY).then_inc(pickT_made.sem, 1)
            high(base, 0)
            prep(2)
            with prog.loop(act, STEPS_EXPERT // 2 - 1, 0) as i:
                for d, s in ((1, 1), (2, 0)):
                    silu(base + 2 * i + d, s, U + 6 * i + 1 + 3 * d)
                    prep(1)
                    high(base + 2 * i + d, s)
                    prep(2)
            m = STEPS_EXPERT - 1
            silu(base + m, 1, U + 1 + 3 * m)
            prep(0 if last else 1)
            high(base + m, 1)
            if not last:
                tokens(n + 1)
                prep(1)
            act.wait_ge(unit_used.sem, U + 3 * STEPS_EXPERT)
            act.activation(y_hi[:, :], bank(4, 5), COPY).then_inc(y_hi_made.sem, 1)
            prep(0 if last else 1)

        def experts(turn):
            U = U_END + E * 3 * STEPS_EXPERT * turn
            tokens(E * turn)
            expert(E * turn, U, False)
            with prog.loop(act, E - 2, 0, rounds=EXPERT_R) as e:
                expert(E * turn + 1 + e, U + (e + 1) * (3 * STEPS_EXPERT), False)
            expert(E * turn + E - 1, U + (E - 1) * 3 * STEPS_EXPERT, True)

        def moe():
            prep(2)
            norm_scale(1, 1)
            prep(1)
            turn_input(8, 1)
            narrow_kept(1, 2)
            act.wait_ge(norm_made.sem, norm_made.at(1, 3))
            act.activation(flat(fn_hi), flat(fn), COPY).then_inc(fn_hi_made.sem, 1)
            act.wait_ge(r_read.sem, 1)
            act.activation(r_t[:, 10, 0:TT], r_t[:, 9, 0:TT], EXP).then_inc(r_e.sem, 1)
            experts(0)
            more = second_turn(act, prog)
            with act.If(more > 0):
                prep(3)
                experts(1)

        mixer(0)
        dense()
        mixer(1)
        moe()

    @block.vector
    def _(dve):
        prog = Program(dve_step)
        for sig in (c_nm, c_ss, f_gm, f_lo, s_read, e_lo_made, y_lo_made):
            dve.sem_inc(sig.sem, sig.ahead)

        def prep(count):
            for _ in range(count):
                s = prog.u % SPLIT
                dve.wait_ge(hi_made.sem, prog.unit(1))
                dve.tensor_tensor(lo[prog.u % RAW][:, :], raw[prog.u % RAW][:, :], hi[s][:, :].bitcast(F32),
                                  ALU.subtract).then_inc(lo_made.sem, 1)
                prog.u += 1

        def used(L, n):
            dve.wait_ge(unit_used.sem, LAYER_U[L] + n)

        def flat(t):
            return t[:, :, :, :].rearrange("p a b c -> p (a b c)") if len(t.shape) == 4 else \
                t[:, :, :].rearrange("p a b -> p (a b)")

        def flat8(t):
            return t[:, :, :, :].rearrange("p a b c -> p (a b) c") if len(t.shape) == 4 else \
                t[:, :, :].rearrange("p a (b c) -> p (a b) c", c=P)

        def bank(*b):
            return PS[:, b[0], :] if len(b) == 1 else PS[:, b[0]:b[1] + 1, :].rearrange("p a b -> p (a b)")

        def bank4(b):
            return PS[:, b, :].rearrange("p (h j) -> p h j", h=H)

        def tt(out, a, b, op):
            return dve.tensor_tensor(out, a, b, op)

        def half_sigmoid(ap):
            return dve.tensor_scalar(ap, ap, 1.0, 0.5, ALU.add, ALU.mult)

        for n, v in enumerate((EPS, 1.0, math.log(P ** -0.5), 0.0)):
            dve.memset(tiny[:, n:n + 1], v).then_inc(tiny_made.sem, 1)
        dve.memset(ones_t[:, :], 1.0).then_inc(dve_step.sem, 1)
        dve.wait_ge(dve_step.sem, prog.step())
        dve.memset(table[BUCKETS:BUCKETS + 1, :], 1.0).then_inc(table_here.sem, 1)
        def norm(L, phase):
            src = x
            dst, g = (fn, f_gain) if phase else (hn, gain)
            dve.wait_ge(norm_r.sem, norm_r.at(L, phase))
            dve.wait_ge(gain_here.sem, 16 * (2 * L + phase + 1))
            for t in range(TT):
                dve.scalar_tensor_tensor(dst[:, t, :], src[:, t, :], stat[:, 4 + t:5 + t], g[:, :],
                                         ALU.mult, ALU.mult).then_inc(norm_made.sem, 1)

        norm(0, 0)
        dve.wait_ge(rows_kept.sem, 1)
        lbr = small[:, R_LB:R_LB + 2 * H].rearrange("p (l h) -> p l h", l=2)
        tt(lb[:, 2, :], lbr[:, 0, :], lbr[:, 1, :], ALU.max).then_inc(dve_step.sem, 1)
        dve.wait_ge(dve_step.sem, prog.step())
        tt(lb[:, 4:6, :], lbr, over(lb[:, 2, :], 2), ALU.subtract).then_inc(lb_m.sem, 1)
        dve.wait_ge(lb_e.sem, 1)
        tt(lb[:, 2, :], lb[:, 4, :], lb[:, 5, :], ALU.add).then_inc(dve_step.sem, 1)
        dve.wait_ge(dve_step.sem, prog.step())
        dve.reciprocal(lb[:, 3, :], lb[:, 2, :]).then_inc(dve_step.sem, 1)
        dve.wait_ge(dve_step.sem, prog.step())
        tt(lb[:, 4:6, :], lb[:, 4:6, :], over(lb[:, 3, :], 2), ALU.mult).then_inc(dve_step.sem, 1)
        dve.wait_ge(dve_step.sem, prog.step())
        tt(lb[:, 2, :], lb[:, 4, :], lb[:, 5, :], ALU.add).then_inc(dve_step.sem, 1)
        dve.wait_ge(dve_step.sem, prog.step())
        tt(lb[:, 0, :], lb[:, 2, :], lb[:, 4, :], ALU.subtract).then_inc(dve_step.sem, 1)
        dve.wait_ge(dve_step.sem, prog.step())
        dve.tensor_scalar(lb[:, 1, :], lb[:, 0, :], -1.0, 1.0, ALU.mult, ALU.add).then_inc(dve_step.sem, 1)
        dve.wait_ge(dve_step.sem, prog.step())
        dve.wait_ge(a_rate_e.sem, 1)
        dve.tensor_scalar(a_rate[:, :, :], a_rate[:, :, :], -1.0, None, ALU.mult).then_inc(dve_step.sem, 1)
        dve.wait_ge(dve_step.sem, prog.step())
        dve.wait_ge(ab_split.sem, 1)
        tt(ab_lo[:, :, :, :], ab[:, :, :, :], ab_hi[:, :, :, :].bitcast(F32), ALU.subtract).then_inc(ab_split.sem, 1)

        def turn_input(idx, L, scale=1.0):
            for j in range(4):
                dve.wait_ge(actT_hi_made.sem, actT_hi_made.at(L, idx + j))
                v = slice(2 * j, 2 * j + 2)
                dve.scalar_tensor_tensor(actT_lo[:, v, :].rearrange("p a b -> p (a b)"), bank(4 + j), scale,
                                         actT_hi[:, v, :].rearrange("p a b -> p (a b)").bitcast(F32),
                                         ALU.mult, ALU.subtract).then_inc(actT_lo_made.sem, 1)

        def mixer(L):
            if L:
                norm(L, 0)
                prep(1)
            turn_input(0, L)
            if L == 0:
                prep(3)
            dve.memset(a_in[:, :, 0:3], 0.0).then_inc(pad_made.sem, 1)
            dve.wait_ge(pad_made.sem, L + 1)

            def conv(g):
                dve.wait_ge(a_raw.sem, a_raw.at(L, 2 * g + 1))
                if g == 0 and L == 0:
                    dve.wait_ge(rows_kept.sem, 1)
                for tap in range(TAPS):
                    for n in range(H):
                        ct = g * H + n
                        col = R_CONV + (L * TAPS + tap) * CT + ct
                        src, w = a_in[:, ct, tap:tap + T], small[:, col:col + 1]
                        if tap == 0:
                            ins = dve.tensor_scalar(a_act[:, ct, :], src, w, None, ALU.mult)
                        else:
                            ins = dve.scalar_tensor_tensor(a_act[:, ct, :], src, w, a_act[:, ct, :],
                                                           ALU.mult, ALU.add)
                        if tap == TAPS - 1 and n == H - 1:
                            ins.then_inc(a_conv.sem, 1)
                        elif n == H - 1:
                            ins.then_inc(dve_step.sem, 1)
                            dve.wait_ge(dve_step.sem, prog.step())
                        else:
                            ins.then_inc(dve_step.sem, 1)
                            prog.step()

            def silu(g):
                th = (t_x, t_y, t_w)[g]
                act_g = a_act[:, g * H:(g + 1) * H, :].rearrange("p a b -> p (a b)")
                dve.wait_ge(a_tanh.sem, a_tanh.at(L, g))
                half_sigmoid(flat(th)).then_inc(dve_step.sem, 1)
                dve.wait_ge(dve_step.sem, prog.step())
                tt(act_g, act_g, flat(th), ALU.mult).then_inc(a_silu.sem, 1)

            prep(2)
            conv(0)
            dve.wait_ge(ab_done.sem, ab_done.at(L))
            logits = PS[:, 4, 0:16].rearrange("p (t c) -> p t c", t=TT)

            def a8(n):
                return a_s[:, n, :].rearrange("p (t h) -> p t h", t=TT)

            dve.wait_ge(par_here.sem, 32)
            tt(a8(1), logits[:, :, H:2 * H], over(a_par[:, 1, L, :], TT), ALU.add).then_inc(dve_step.sem, 1)
            dve.wait_ge(dve_step.sem, prog.step())
            dve.scalar_tensor_tensor(a_s[:, 4, :], a_s[:, 1, :], -1.0, a_s[:, 1, :], ALU.mult, ALU.max).then_inc(dve_step.sem, 1)
            dve.wait_ge(dve_step.sem, prog.step())
            dve.tensor_copy(a8(2), logits[:, :, 0:H]).then_inc(ab_read.sem, 1)
            dve.wait_ge(ab_read.sem, ab_read.at(L))
            dve.wait_ge(a_e1.sem, a_e1.at(L))
            dve.tensor_scalar(a_s[:, 3, :], a_s[:, 3, :], 1.0, None, ALU.add).then_inc(dve_step.sem, 1)
            dve.wait_ge(dve_step.sem, prog.step())
            dve.reciprocal(a_s[:, 0, :], a_s[:, 3, :]).then_inc(dve_step.sem, 1)
            dve.wait_ge(dve_step.sem, prog.step())
            dve.wait_ge(a_e2.sem, a_e2.at(L))
            dve.tensor_scalar(a_s[:, 7, :], a_s[:, 1, :], 0.0, None, ALU.max).then_inc(dve_step.sem, 1)
            dve.wait_ge(dve_step.sem, prog.step())
            tt(a_s[:, 7, :], a_s[:, 7, :], a_s[:, 6, :], ALU.add).then_inc(dve_step.sem, 1)
            dve.wait_ge(dve_step.sem, prog.step())
            tt(a8(8), a8(7), over(a_rate[:, L, :], TT), ALU.mult).then_inc(a_g.sem, 1)
            dve.wait_ge(a_g.sem, a_g.at(L))
            prep(2)
            conv(1)
            silu(0)
            prep(2)
            conv(2)
            silu(1)
            prep(2)
            silu(2)
            dve.wait_ge(gate_tanh.sem, gate_tanh.at(L, 0))
            half_sigmoid(flat(t_v)).then_inc(dve_step.sem, 1)
            dve.wait_ge(dve_step.sem, prog.step())
            dve.wait_ge(a_silu.sem, a_silu.at(L, 2))
            tt(flat(a_gate), bank(2, 3), flat(t_v), ALU.mult).then_inc(gate_made.sem, 1)
            dve.wait_ge(gate_made.sem, gate_made.at(L, 0))
            prep(2)
            dve.wait_ge(gate_tanh.sem, gate_tanh.at(L, 1))
            half_sigmoid(flat(b_q)).then_inc(dve_step.sem, 1)
            dve.wait_ge(dve_step.sem, prog.step())
            tt(flat(b_q), bank(0, 1), flat(b_q), ALU.mult).then_inc(gate_made.sem, 1)
            dve.wait_ge(gate_made.sem, gate_made.at(L, 1))
            prep(2)
            used(L, 12)
            dve.tensor_scalar(flat(b_f), bank(2, 3), -40.0, None, ALU.max).then_inc(bf_read.sem, 1)
            dve.wait_ge(bf_read.sem, bf_read.at(L))
            dve.wait_ge(bf_s.sem, bf_s.at(L))
            if L == 1:
                for h in range(H):
                    ins = dve.tensor_scalar(b_f[:, h, :], b_f[:, h, :], lb[:, 1, h:h + 1], lb[:, 0, h:h + 1],
                                            ALU.mult, ALU.add)
                    ins.then_inc(dve_step.sem, 1)
                    dve.wait_ge(dve_step.sem, prog.step())
            deltanet(L)
            hgrn(L)
            dilated(L)
            for k in (4, 5):
                gated(L, k, 3 if k == 4 else 0)
                prep(1)
            turn_input(4, L, scale=0.5)
            prep(1)
            for half in range(2):
                used(L, U_OUT + 2 * half + 2)
                h = slice(half * 512, (half + 1) * 512)
                tt(x[:, :, h], x[:, :, h], PS[:, 2 * half:2 * half + 2, :], ALU.add).then_inc(x_made.sem, 1)
                dve.wait_ge(x_made.sem, x_made.at(L, half))
                prep(1)

        def chunk(t, c):
            return t[:, c].rearrange("p h j -> p (h j)")

        def scale8(t):
            return wide(t, P)

        def deltanet(L):
            beta, g, r_q, r_k = (a_s[:, n, :] for n in (0, 8, 15, 16))
            for n, (src, k) in enumerate(((t_w, 0), (t_v, 1))):
                dve.wait_ge(a_sq.sem, a_sq.at(L, 2 + k))
                ins = dve.tensor_reduce(a_s[:, 9 + n, :], flat8(src), AX.X, ALU.add)
                if n:
                    ins.then_inc(a_ss.sem, 1)
                    dve.wait_ge(a_ss.sem, a_ss.at(L))
                else:
                    ins.then_inc(dve_step.sem, 1)
                    dve.wait_ge(dve_step.sem, prog.step())
            dve.wait_ge(a_r.sem, a_r.at(L))
            for c in range(TT):
                c4 = slice(c * H, (c + 1) * H)
                tt(t_x[:, c], bank4((4, 7)[c]), wide(r_q[:, c4], P), ALU.mult).then_inc(a_qn.sem, 1)
                tt(k_nat[:, c], bank4((5, 0)[c]), wide(r_k[:, c4], P), ALU.mult).then_inc(a_kn.sem, 1)
            tt(flat8(t_m), over(gt, 8), wide(g, P), ALU.mult).then_inc(a_seg.sem, 1)
            tt(flat8(t_n), over(le, 8), wide(g, P), ALU.mult).then_inc(a_seg.sem, 1)
            prep(2)
            tt(flat8(t_w), over(gt, 8), wide(beta, P), ALU.mult).then_inc(dve_step.sem, 1)
            dve.wait_ge(dve_step.sem, prog.step())
            dve.wait_ge(a_exp.sem, a_exp.at(L, 1))
            tt(flat8(t_x), flat8(t_x), flat8(t_w), ALU.mult).then_inc(dve_step.sem, 1)
            dve.wait_ge(dve_step.sem, prog.step())
            dve.wait_ge(a_exp.sem, a_exp.at(L, 3))
            tt(flat8(t_y), flat8(t_y), over(le, 8), ALU.mult).then_inc(dve_step.sem, 1)
            dve.wait_ge(dve_step.sem, prog.step())
            for c in range(TT):
                dve.wait_ge(a_kk.sem, a_kk.at(L, c))
                tt(chunk(t_m, c), bank((4, 7)[c]), chunk(t_x, c), ALU.mult).then_inc(a_M.sem, 1)
                dve.wait_ge(a_M.sem, a_M.at(L, c))
            for c in range(TT):
                dve.wait_ge(a_kk.sem, a_kk.at(L, 2 + c))
                tt(chunk(attn, c), bank((5, 0)[c]), chunk(t_y, c), ALU.mult).then_inc(a_attn.sem, 1)
                dve.wait_ge(a_attn.sem, a_attn.at(L, c))
            tt(flat8(t_x), flat8(t_m), over(consts[:, K_M0, :], 8), ALU.mult).then_inc(dve_step.sem, 1)
            dve.wait_ge(dve_step.sem, prog.step())
            tt(flat8(t_x), over(ident, 8), flat8(t_x), ALU.subtract).then_inc(a_X.sem, 1)
            dve.wait_ge(a_X.sem, a_X.at(L, 0))
            prep(1)
            dve.wait_ge(a_Nc.sem, a_Nc.at(L, 1))
            tt(flat8(t_y), flat8(t_n), over(consts[:, K_MT, :], 8), ALU.mult).then_inc(dve_step.sem, 1)
            dve.wait_ge(dve_step.sem, prog.step())
            tt(flat8(t_y), over(ident, 8), flat8(t_y), ALU.subtract).then_inc(a_Y.sem, 1)
            dve.wait_ge(a_Y.sem, a_Y.at(L, 0))

            def off(lv):
                tt(flat8(t_w), flat8(t_n), over(consts[:, K_MT + lv, :], 8), ALU.mult).then_inc(a_No.sem, 1)

            off(1)
            prep(1)
            for lv in range(1, LEVELS):
                dve.wait_ge(a_P.sem, a_P.at(L, 2 * (lv - 1) + 1))
                if lv < LEVELS - 1:
                    off(lv + 1)
                else:
                    tt(t_w[:, 0], v_nat[:, 0], wide(beta[:, 0:H], P), ALU.mult).then_inc(a_r0.sem, 1)
                    dve.wait_ge(a_cum_e.sem, a_cum_e.at(L))
                    tt(t_v[:, 0], k_nat[:, 0], wide(a_s[:, 11, 0:H], P), ALU.mult).then_inc(a_kg.sem, 1)
                for c in range(TT):
                    if lv < LEVELS - 1:
                        dve.wait_ge(a_XP.sem, a_XP.at(L, 2 * (lv - 1) + c))
                        tt(chunk(t_x, c), chunk(t_x, c), bank(6 + c), ALU.subtract).then_inc(a_X.sem, 1)
                        dve.wait_ge(a_X.sem, a_X.at(L, 2 * lv - 1 + c))
                    dve.wait_ge(a_YP.sem, a_YP.at(L, 2 * (lv - 1) + c))
                    tt(chunk(t_y, c), chunk(t_y, c), bank(c), ALU.subtract).then_inc(a_Y.sem, 1)
                    dve.wait_ge(a_Y.sem, a_Y.at(L, 2 * lv - 1 + c))
            eg = wide(a_s[:, 11, H:2 * H], P)
            dve.wait_ge(a_kS.sem, a_kS.at(L))
            tt(t_v[:, 1], bank4(6), eg, ALU.mult).then_inc(dve_step.sem, 1)
            dve.wait_ge(dve_step.sem, prog.step())
            tt(t_v[:, 1], v_nat[:, 1], t_v[:, 1], ALU.subtract).then_inc(dve_step.sem, 1)
            dve.wait_ge(dve_step.sem, prog.step())
            tt(t_w[:, 1], t_v[:, 1], wide(beta[:, H:2 * H], P), ALU.mult).then_inc(a_r1.sem, 1)
            dve.wait_ge(a_qS.sem, a_qS.at(L))
            tt(t_m[:, 1], bank4(7), eg, ALU.mult).then_inc(dve_step.sem, 1)
            dve.wait_ge(dve_step.sem, prog.step())
            dve.wait_ge(a_o.sem, a_o.at(L, 1))
            dve.wait_ge(a_oc.sem, a_oc.at(L, 0))
            tt(chunk(t_n, 1), chunk(t_m, 1), bank(3), ALU.add).then_inc(a_oc.sem, 1)
            dve.wait_ge(a_oc.sem, a_oc.at(L, 1))
            output_norm(L, 0, t_n, t_y, a_gate)

        def output_norm(L, br, src, sq, gate):
            dve.wait_ge(o_sq.sem, o_sq.at(L, br))
            dve.tensor_reduce(a_s[:, 17, :], flat8(sq), AX.X, ALU.add).then_inc(o_ss.sem, 1)
            dve.wait_ge(o_r.sem, o_r.at(L, br))
            tt(flat8(src), flat8(src), wide(a_s[:, 19, :], P), ALU.mult).then_inc(dve_step.sem, 1)
            dve.wait_ge(dve_step.sem, prog.step())
            tt(flat8(src), flat8(src), flat8(gate), ALU.mult).then_inc(o_made.sem, 1)
            dve.wait_ge(o_made.sem, o_made.at(L, br))

        def hgrn(L):
            dve.wait_ge(oT_made.sem, oT_made.at(L, 0))
            dve.tensor_scalar(flat(b_k), flat(b_f), -1.0, 1.0, ALU.mult, ALU.add).then_inc(b_qk.sem, 1)
            dve.wait_ge(b_qk.sem, b_qk.at(L, 0))
            dve.tensor_scalar(flat(b_f), flat(b_f), 1e-18, None, ALU.max).then_inc(b_clamp.sem, 1)
            dve.wait_ge(b_clamp.sem, b_clamp.at(L))
            dve.memset(flat(b_attn), 0.0).then_inc(dve_step.sem, 1)
            dve.wait_ge(dve_step.sem, prog.step())
            prep(1)
            dve.wait_ge(b_g.sem, b_g.at(L))
            for h in range(H):
                ins = dve.tensor_tensor_scan(b_gc[:, h, :], zero_t.broadcast_to([P, T]), b_f[:, h, :], 0.0,
                                             ALU.add, ALU.add)
                ins.then_inc(dve_step.sem, 1)
                dve.wait_ge(dve_step.sem, prog.step())

            def masked(n):
                dve.wait_ge(b_att.sem, b_att.at(L, n))
                if n == LEVELS + 1:
                    dve.tensor_copy(chunk(b_attn, 2), bank(0)).then_inc(b_masked.sem, 1)
                    dve.wait_ge(b_masked.sem, b_masked.at(L, n))
                    return
                pair = (4, 6)[n % 2]
                mask = ident if n == 0 else consts[:, K_MT + n - 1, :]
                dve.copy_predicated(b_attn[:, 0:2].rearrange("p c h j -> p (c h) j"),
                                    over(mask, 8).bitcast(I32),
                                    PS[:, pair:pair + 2, :].rearrange("p c (h j) -> p (c h) j", h=H)).then_inc(b_masked.sem, 1)
                dve.wait_ge(b_masked.sem, b_masked.at(L, n))

            def diff(n):
                s = 1 << n
                v = flat(b_gc).rearrange("p (n s) -> p n s", s=2 * s)
                mid = v[:, :, s - 1:s].broadcast_to([P, H * T // (2 * s), 2 * s])
                tt(flat(b_e).rearrange("p (n s) -> p n s", s=2 * s), v, mid, ALU.subtract).then_inc(b_diff.sem, 1)
                dve.wait_ge(b_diff.sem, b_diff.at(L, n))

            diff(0)
            dve.wait_ge(gate_tanh.sem, gate_tanh.at(L, 2))
            half_sigmoid(flat(b_gate)).then_inc(gate_made.sem, 1)
            dve.wait_ge(gate_made.sem, gate_made.at(L, 3))
            prep(1)
            for n in range(LEVELS + 1):
                dve.wait_ge(b_exp.sem, b_exp.at(L, n))
                dve.wait_ge(b_att.sem, b_att.at(L, n))
                tt(flat(b_qe), flat(b_q), flat(b_e), ALU.mult).then_inc(dve_step.sem, 1)
                dve.wait_ge(dve_step.sem, prog.step())
                tt(flat(b_ke), flat(b_k), flat(b_e), ALU.mult).then_inc(b_qk.sem, 1)
                dve.wait_ge(b_qk.sem, b_qk.at(L, n + 1))
                if n < LEVELS:
                    diff(n + 1)
                masked(n)
                prep(1 if n else 2)
            masked(LEVELS + 1)
            prep(1)
            output_norm(L, 1, b_o, b_o2, b_gate)

        def dilated(L):
            with prog.loop(dve, GROUPS, 0) as g:
                def normed(j):
                    dve.wait_ge(c_sqd.sem, L * 6 + 2 * g + j + 1)
                    dve.tensor_reduce(stat[:, 0:8], flat8(c_sq), AX.X, ALU.add).then_inc(c_ss.sem, 1)
                    dve.wait_ge(c_r.sem, L * 6 + 2 * g + j + 1)
                    dve.wait_ge(c_Td.sem, c_Td.count(L * 6 + 2 * g + j))
                    tt(flat8(c_n), PS[:, 2 * j:2 * j + 2, :].rearrange("p t (h j) -> p (t h) j", h=H),
                       wide(stat[:, 8:16], P), ALU.mult).then_inc(c_nm.sem, 1)

                prep(2)
                normed(0)
                prep(2)
                normed(1)
                prep(2)

            split_branch(L, 0)
            def scaled(n):
                t, h = divmod(n, H)
                keys = (t + 1) * P
                st = 4 * (n % 2)
                off = T - keys
                sv = c_s[:, :].rearrange("p (g s) -> p g s", g=GROUPS)
                bv = bias[:, :, :].rearrange("p (g h) s -> p g h s", g=GROUPS)
                dve.wait_ge(c_sd.sem, c_sd.at(L, n))
                if n:
                    dve.wait_ge(c_e.sem, c_e.at(L, n - 1))
                dve.scalar_tensor_tensor(sv[:, 0:2, 0:keys],
                                         PS[:, 0, :].rearrange("p (g s) -> p g s", g=2)[:, :, 0:keys],
                                         P ** -0.5, bv[:, 0:2, h, off:T], ALU.mult,
                                         ALU.add).then_inc(dve_step.sem, 1)
                dve.wait_ge(dve_step.sem, prog.step())
                dve.scalar_tensor_tensor(sv[:, 2, 0:keys], PS[:, 1, 0:keys], P ** -0.5,
                                         bv[:, 2, h, off:T], ALU.mult, ALU.add).then_inc(c_sm.sem, 1)
                dve.wait_ge(c_sm.sem, c_sm.at(L, n))
                dve.tensor_reduce(stat[:, st:st + 1], sv[:, :, 0:keys], AX.XY, ALU.max).then_inc(dve_step.sem, 1)
                dve.wait_ge(dve_step.sem, prog.step())
                dve.tensor_scalar(stat[:, st + 1:st + 2], stat[:, st:st + 1], -1.0, None,
                                  ALU.mult).then_inc(c_mx.sem, 1)

            scaled(0)
            split_branch(L, 1)
            for n in range(TT * H):
                t, h = divmod(n, H)
                st = 4 * (n % 2)
                if n + 1 < TT * H:
                    scaled(n + 1)
                dve.wait_ge(c_e.sem, c_e.at(L, n))
                dve.reciprocal(stat[:, st + 3:st + 4], stat[:, st + 2:st + 3]).then_inc(dve_step.sem, 1)
                dve.wait_ge(dve_step.sem, prog.step())
                if n % 2 == 0:
                    gated(L, n // 2, 3)
                    prep(1)
                dve.wait_ge(c_od.sem, c_od.at(L, n))
                dve.tensor_scalar(c_o[:, t, h * P:(h + 1) * P], PS[:, 2 + n % 2, 0:P],
                                  stat[:, st + 3:st + 4], None, ALU.mult).then_inc(c_oc.sem, 1)
                dve.wait_ge(c_oc.sem, c_oc.at(L, n))
            dve.wait_ge(o_hi_made.sem, o_hi_made.at(L, 2))
            tt(flat(o_lo[0]), bank(4, 5), flat(o_hi[0]).bitcast(F32), ALU.subtract).then_inc(o_lo_made.sem, 1)

        def split_branch(L, br):
            dve.wait_ge(o_hi_made.sem, o_hi_made.at(L, br))
            tt(flat(o_lo[br % 2]), oT[:, br, :, :].rearrange("p a b -> p (a b)"),
               flat(o_hi[br % 2]).bitcast(F32), ALU.subtract).then_inc(o_lo_made.sem, 1)

        def gated(L, k, pair):
            used(L, U_BR + k + 1)
            g = gates[k]
            dve.scalar_tensor_tensor(flat(g), flat(g), 1.0, bank(2 * pair, 2 * pair + 1), ALU.add,
                                     ALU.mult).then_inc(g_prod_made.sem, 1)
            dve.wait_ge(g_prod_made.sem, g_prod_made.at(L, k))
            if k >= 2:
                mix = gates[k % 2]
                tt(flat(mix), flat(mix), flat(g), ALU.add).then_inc(mix_made.sem, 1)
                dve.wait_ge(mix_made.sem, mix_made.at(L, k - 2))

        def dense():
            norm(0, 1)
            prep(1)
            turn_input(8, 0)

            def half_step(m, s, preps=(1, 2)):
                dve.wait_ge(f_silu.sem, m + 1)
                dve.wait_ge(f_lo.sem, f_lo.count(m - 1))
                dve.tensor_tensor(f_g[s][:, :].rearrange("p (j t) -> p j t", j=2),
                                  f_s[s][:, :].rearrange("p (j t) -> p j t", j=2),
                                  PS[:, 2 * s:2 * s + 2, T:2 * T], ALU.mult).then_inc(f_gm.sem, 1)
                prep(preps[0])
                dve.wait_ge(f_hi.sem, m + 1)
                dve.wait_ge(f_gm.sem, f_gm.count(m + 1))
                tt(flat(fT_lo[s]), f_g[s][:, :], flat(fT_hi[s]).bitcast(F32), ALU.subtract).then_inc(f_lo.sem, 1)
                prep(preps[1])

            half_step(0, 0)
            with prog.loop(dve, STEPS_DENSE // 2 - 1, 0) as i:
                half_step(2 * i + 1, 1)
                half_step(2 * i + 2, 0)
            half_step(STEPS_DENSE - 2, 1)
            half_step(STEPS_DENSE - 1, 0, (0, 0))
            dve.wait_ge(unit_used.sem, LAYER_U[1])
            tt(flat(x), flat(x), PS[:, 4:8, :].rearrange("p a b -> p (a b)"), ALU.add).then_inc(x_made.sem, 1)
            dve.wait_ge(x_made.sem, x_made.at(0, 2))
            prep(2)

        def choose(n, e, turn):
            dve.wait_ge(e_done.sem, e_done.count(2 * n))
            dve.wait_ge(pickT_done.sem, pickT_done.count(n))
            for t in range(TT):
                col = bass.ds(e + t * E, 1) if not isinstance(e, int) else slice(e + t * E, e + t * E + 1)
                dve.tensor_scalar(pick[:, t, :], slots[:, turn * P:(turn + 1) * P],
                                  r_t[:, 14, col], None, ALU.is_equal).then_inc(pick0.sem, 1)
            dve.wait_ge(pick0.sem, 2 * n + 2)
            dve.tensor_copy(flat(pick_r), flat(pick)).then_inc(pick_made.sem, 1)

        def tokens(n):
            for j in range(2):
                dve.wait_ge(e_hi_made.sem, 2 * n + j + 1)
                v = slice(4 * j, 4 * j + 4)
                tt(e_lo[:, v, :].rearrange("p a b -> p (a b)"), bank(6 + j),
                   e_hi[:, v, :].rearrange("p a b -> p (a b)").bitcast(F32), ALU.subtract).then_inc(e_lo_made.sem, 1)

        def add_to_x(n, e, t):
            dve.wait_ge(s_done.sem, 2 * n + t + 1)
            col = bass.ds(e + t * E, 1) if not isinstance(e, int) else slice(e + t * E, e + t * E + 1)
            dve.scalar_tensor_tensor(x[:, t, :], bank(4 + 2 * t, 5 + 2 * t), r_t[:, 15, col],
                                     x[:, t, :], ALU.mult, ALU.add).then_inc(s_read.sem, 1)

        def expert(n, e, turn, first, last):
            base = STEPS_DENSE + STEPS_EXPERT * n

            def multiply(m, s):
                dve.wait_ge(f_silu.sem, m + 1)
                dve.wait_ge(f_gT.sem, f_gT.count(m - STEPS_DENSE - 1))
                tt(f_g[s][:, 0:SUB], f_s[s][:, 0:SUB], PS[:, s, SUB:2 * SUB], ALU.mult).then_inc(f_gm.sem, 1)

            def low(m, s):
                dve.wait_ge(f_hi.sem, m + 1)
                tt(fT_lo[s][:, :, 0:P], PS[:, 2, s * SUB:(s + 1) * SUB].rearrange("p (j t) -> p j t", j=2),
                   fT_hi[s][:, :, 0:P].bitcast(F32),
                   ALU.subtract).then_inc(f_lo.sem, 1)

            multiply(base, 0)
            prep(1)
            if not first:
                add_to_x(n - 1, e - 1, 0)
            low(base, 0)
            prep(1)
            if not first:
                add_to_x(n - 1, e - 1, 1)
            prep(1)
            if not last:
                choose(n + 1, e + 1, turn)
            with prog.loop(dve, STEPS_EXPERT // 2 - 1, 0) as i:
                for d, s in ((1, 1), (2, 0)):
                    multiply(base + 2 * i + d, s)
                    prep(1)
                    low(base + 2 * i + d, s)
                    prep(2)
            multiply(base + STEPS_EXPERT - 1, 1)
            prep(0 if last else 1)
            low(base + STEPS_EXPERT - 1, 1)
            if not last:
                tokens(n + 1)
                prep(1)
            dve.wait_ge(y_hi_made.sem, n + 1)
            tt(y_lo[:, :], bank(4, 5), y_hi[:, :].bitcast(F32), ALU.subtract).then_inc(y_lo_made.sem, 1)
            prep(0 if last else 1)

        def experts(turn):
            n = E * turn
            if turn:
                choose(n, 0, turn)
            tokens(n)
            expert(n, 0, turn, True, False)
            with prog.loop(dve, E - 2, 0, rounds=EXPERT_R) as e:
                expert(n + 1 + e, e + 1, turn, False, False)
            expert(n + E - 1, E - 1, turn, False, True)
            for t in range(TT):
                add_to_x(n + E - 1, E - 1, t)
            dve.wait_ge(s_read.sem, s_read.count(2 * (n + E)))

        def moe():
            norm(1, 1)
            prep(1)
            turn_input(8, 1)
            dve.wait_ge(r_done.sem, 1)

            def r16(n):
                return r_t[:, n, :]

            def r8(n):
                return r_t[:, n, :].rearrange("p (t e) -> p t e", t=TT)

            dve.tensor_copy(r16(0), PS[:, 0, 0:TT * E]).then_inc(dve_step.sem, 1)
            dve.wait_ge(dve_step.sem, prog.step())
            for k in range(2):
                lg, eq, cs, first, v = 0 + k, 2, 3, 4 + k, r_t[:, 8, 2 * k:2 * k + 2]
                dve.tensor_reduce(v, r8(lg), AX.X, ALU.max).then_inc(dve_step.sem, 1)
                dve.wait_ge(dve_step.sem, prog.step())
                tt(r8(eq), r8(lg), wide(v, E), ALU.is_equal).then_inc(dve_step.sem, 1)
                dve.wait_ge(dve_step.sem, prog.step())
                for t in range(TT):
                    dve.tensor_tensor_scan(r_t[:, cs, t * E:(t + 1) * E], zero_t.broadcast_to([P, E]),
                                           r_t[:, eq, t * E:(t + 1) * E], 0.0, ALU.add, ALU.add).then_inc(dve_step.sem, 1)
                    dve.wait_ge(dve_step.sem, prog.step())
                dve.scalar_tensor_tensor(r16(first), r16(cs), 1.0, r16(eq), ALU.is_equal, ALU.mult).then_inc(dve_step.sem, 1)
                dve.wait_ge(dve_step.sem, prog.step())
                if k == 0:
                    dve.scalar_tensor_tensor(r16(1), r16(first), NEG, r16(0), ALU.mult, ALU.add).then_inc(dve_step.sem, 1)
                    dve.wait_ge(dve_step.sem, prog.step())
            tt(r_t[:, 9, 0:2], r_t[:, 8, 2:4], r_t[:, 8, 0:2], ALU.subtract).then_inc(r_read.sem, 1)
            dve.wait_ge(r_read.sem, 1)
            tt(r16(12), r16(4), r16(5), ALU.add).then_inc(r_sel.sem, 1)
            dve.wait_ge(r_sel.sem, 1)
            dve.wait_ge(fn_hi_made.sem, 1)
            tt(flat(fn_lo), flat(fn), flat(fn_hi).bitcast(F32), ALU.subtract).then_inc(fn_lo_made.sem, 1)
            dve.wait_ge(r_cnt.sem, 1)
            tt(r16(14), PS[:, 1, 0:2 * E], r16(12), ALU.mult).then_inc(dve_step.sem, 1)
            dve.wait_ge(dve_step.sem, prog.step())
            dve.tensor_scalar(r16(14), r16(14), -1.0, None, ALU.add).then_inc(dve_step.sem, 1)
            dve.wait_ge(dve_step.sem, prog.step())
            dve.tensor_reduce(r_t[:, 13, 0:1], PS[:, 1, 2 * E:3 * E], AX.X, ALU.max).then_inc(dve_step.sem, 1)
            dve.wait_ge(dve_step.sem, prog.step())
            dve.tensor_scalar(r_flag[:, 0:1], r_t[:, 13, 0:1], float(P), None, ALU.is_gt).then_inc(r_flag_made.sem, 1)
            dve.wait_ge(r_flag_made.sem, 1)
            dve.wait_ge(slots_here.sem, 2)
            choose(0, 0, 0)
            dve.wait_ge(r_e.sem, 1)
            dve.tensor_scalar(r_t[:, 9, 2:4], r_t[:, 10, 0:2], 1.0, None, ALU.add).then_inc(dve_step.sem, 1)
            dve.wait_ge(dve_step.sem, prog.step())
            dve.reciprocal(r_t[:, 11, 0:2], r_t[:, 9, 2:4]).then_inc(dve_step.sem, 1)
            dve.wait_ge(dve_step.sem, prog.step())
            tt(r_t[:, 11, 2:4], r_t[:, 11, 0:2], r_t[:, 10, 0:2], ALU.mult).then_inc(dve_step.sem, 1)
            dve.wait_ge(dve_step.sem, prog.step())
            tt(r8(6), r8(4), wide(r_t[:, 11, 0:2], E), ALU.mult).then_inc(dve_step.sem, 1)
            dve.wait_ge(dve_step.sem, prog.step())
            tt(r8(7), r8(5), wide(r_t[:, 11, 2:4], E), ALU.mult).then_inc(dve_step.sem, 1)
            dve.wait_ge(dve_step.sem, prog.step())
            tt(r16(15), r16(6), r16(7), ALU.add).then_inc(dve_step.sem, 1)
            dve.wait_ge(dve_step.sem, prog.step())
            experts(0)
            more = second_turn(dve, prog)
            with dve.If(more > 0):
                prep(3)
                experts(1)
            dve.memset(stat[:, 8:9], 0.0).then_inc(x_last.sem, 1)

        mixer(0)
        dense()
        mixer(1)
        moe()

    @block.gpsimd
    def _(pool):
        pool.dma_start(gain[:, :], dram["norm_mix"][0:1, :].partition_broadcast(P)
                       .rearrange("q o d -> q (o d)")).then_inc(gain_here.sem, 16)
        pool.wait_ge(by_dist_kept.sem, 1)
        pool.dma_start(hankel_dram.rearrange("(g h) z -> h g z", g=GROUPS), by_dist[:, :, :])\
            .then_inc(by_dist_out.sem, 16)
        pool.wait_ge(by_dist_out.sem, 16)
        pool.dma_start(hankel[:, :, :], bass.AP(hankel_dram.tensor, 0, [[1, P], [DIST, GROUPS * H], [1, T]]))\
            .then_inc(hankel_here.sem, 16)
        for L in range(DEPTH):
            if L:
                pool.wait_ge(x_made.sem, x_made.at(L - 1, 2))
                pool.dma_start(gain[:, :], dram["norm_mix"][L:L + 1, :].partition_broadcast(P)
                               .rearrange("q o d -> q (o d)")).then_inc(gain_here.sem, 16)
            pool.wait_ge(o_lo_made.sem, o_lo_made.at(L, 2))
            pool.wait_ge(gain_here.sem, 16 * (2 * L + 1))
            pool.dma_start(f_gain[:, :], dram["norm_ffn"][L:L + 1, :].partition_broadcast(P)
                           .rearrange("q o d -> q (o d)")).then_inc(gain_here.sem, 16)
        pool.wait_ge(x_made.sem, x_made.at(1, 1))
        pool.iota(slots_i[:, :], pattern=[[1, 2 * P]], base=0, channel_multiplier=0).then_inc(slots_here.sem, 1)
        pool.wait_ge(slots_here.sem, 1)
        pool.tensor_copy(slots[:, :], slots_i[:, :]).then_inc(slots_here.sem, 1)

    @block.sync
    def _(sp):
        prog = Program(None)

        def load(dst, src, sig):
            sp.dma_start(dst, src).then_inc(sig.sem, 16)

        def unit(src, k):
            slot = prog.u % RAW
            if prog.u >= RAW:
                sp.wait_ge(unit_used.sem, prog.unit(1 - RAW))
            load(unit_view(raw[slot], k), src, raw_full[slot])
            prog.u += 1

        def rows_of(ap):
            return ap.rearrange("(k p) n -> p k n", p=P)

        def cols(L, c):
            for half in range(2):
                sl = bass.ds(c, 512) if not isinstance(c, int) else slice(c, c + 512)
                unit(rows_of(dram["w_in"][L, half * 512:(half + 1) * 512, sl]), 4)

        xr = dram["x"][0].rearrange("(t p) d -> t p d", p=P)
        for t in range(TT):
            load(x[:, t, :], xr[t], x_here)
        load(consts[:, :, :], dram["masks"], consts_here)
        load(picks[:, :, :], dram["buckets"], consts_here)
        rows_of_small = (
            (R_CONV, dram["conv_a"].rearrange("l t (c p) -> (l t c) p", p=P)),
            (R_LB, dram["lb_logits"].rearrange("l (h p) -> (l h) p", p=P)),
            (R_GA, dram["gnorm_a"]), (R_GB, dram["gnorm_b"]),
            (R_QN, dram["qnorm_c"].rearrange("l g p -> (l g) p")),
            (R_KN, dram["knorm_c"].rearrange("l g p -> (l g) p")))
        assert len(rows_of_small) == N_ROW_LOADS
        for r, src in rows_of_small:
            load(rows[r:r + src.shape[0], :], src, rows_here)
        load(table[0:BUCKETS, :], dram["rel_bias"], table_here)
        for n in range(DEPTH):
            load(ab[:, n, :, :], rows_of(dram["w_in"][n, :, C_AB:C_AB + 2 * H]), ab_here)
        load(ab[:, 2, :, :], rows_of(dram["router"][0]), ab_here)
        for n, name in enumerate(("a_log", "dt_bias")):
            load(a_par[:, n, :, :], dram[name].rearrange("(o l) h -> o l h", o=1).partition_broadcast(P)
                 .rearrange("q o l h -> q (o l) h"), par_here)

        def mixer(L):
            for g in range(3):
                cols(L, C_QKV + g * W)
            cols(L, C_AGATE)
            for g in range(4):
                cols(L, C_BQ + g * W)
            with prog.loop(sp, 2, 0) as i:
                for k in range(3):
                    cols(L, i * (3 * 512) + (C_BR + k * 512))
            with prog.loop(sp, GROUPS, 0) as g:
                for j in range(3):
                    cols(L, g * W + (C_CQKV + j * GROUPS * W))
            for k in range(6):
                half = slice(k % 2 * 512, (k % 2 + 1) * 512)
                unit(rows_of(dram["w_br"][k // 2, L, :, half]), 4)
            for half in range(2):
                for k in range(2):
                    unit(rows_of(dram["w_out"][L, k * 512:(k + 1) * 512, half * 512:(half + 1) * 512]), 4)

        def up(w1, w3, c):
            for w in (w1, w3):
                sl = bass.ds(c, SUB) if not isinstance(c, int) else slice(c, c + SUB)
                unit(rows_of(w[:, sl]), 8)

        def dense():
            w1, w3, w2 = (dram[n][0] for n in ("ffn_w1", "ffn_w3", "ffn_w2"))

            def down(c):
                rows = bass.ds(c, SUB) if not isinstance(c, int) else slice(c, c + SUB)
                unit(rows_of(w2[rows, :]), 2)

            up(w1, w3, 0)
            up(w1, w3, SUB)
            down(0)
            with prog.loop(sp, STEPS_DENSE // 2 - 1, 0) as i:
                for m in (2, 3):
                    up(w1, w3, i * (2 * SUB) + m * SUB)
                    down(i * (2 * SUB) + (m - 1) * SUB)
            up(w1, w3, (STEPS_DENSE - 1) * SUB)
            down((STEPS_DENSE - 2) * SUB)
            down((STEPS_DENSE - 1) * SUB)

        def experts():
            with prog.loop(sp, E, 0, rounds=EXPERT_R) as e:
                w1, w3, w2 = (dram[n][0, bass.ds(e, 1), :, :].rearrange("o r n -> (o r) n")
                              for n in ("moe_w1", "moe_w3", "moe_w2"))

                def down(c):
                    rows = bass.ds(c, SUB) if not isinstance(c, int) else slice(c, c + SUB)
                    unit(rows_of(dram["moe_w2"][0, bass.ds(e, 1), rows, :].rearrange("o r n -> (o r) n")), 2)

                up(w1, w3, 0)
                up(w1, w3, SUB)
                down(0)
                with prog.loop(sp, STEPS_EXPERT // 2 - 1, 0) as c:
                    for m in (2, 3):
                        up(w1, w3, c * (2 * SUB) + m * SUB)
                        down(c * (2 * SUB) + (m - 1) * SUB)
                down((STEPS_EXPERT - 1) * SUB)

        mixer(0)
        dense()
        mixer(1)
        experts()
        more = second_turn(sp, prog)
        with sp.If(more > 0):
            experts()
        sp.wait_ge(x_last.sem, 1)
        out = dram["out"][0].rearrange("(t p) d -> t p d", p=P)
        for t in range(TT):
            load(out[t], x[:, t, :], out_here)
        sp.wait_ge(out_here.sem, 32)


_NAMES = ["x", "w_in", "norm_mix", "conv_a", "a_log", "dt_bias", "gnorm_a", "lb_logits", "gnorm_b", "qnorm_c",
          "knorm_c", "rel_bias", "w_out", "norm_ffn", "ffn_w1", "ffn_w3", "ffn_w2", "router", "moe_w1",
          "moe_w3", "moe_w2"]


def kernel(**inputs):
    import concourse.bacc as _bacc
    from concourse.bass_utils import run_bass_kernel_spmd as _run

    nc = _bacc.Bacc("TRN2", target_bir_lowering=False, num_devices=1)
    masks, buckets = shape_constants()
    given = {name: np.ascontiguousarray(inputs[name]) for name in _NAMES}
    given["w_br"] = np.stack([np.asarray(inputs[n]) for n in ("w_br_a", "w_br_b", "w_br_c")])
    given["masks"], given["buckets"] = masks, buckets
    dram, arrays = {}, {}
    for name, a in given.items():
        arrays[f"in_{name}"] = a
        dram[name] = nc.dram_tensor(f"in_{name}", a.shape, mybir.dt.from_np(a.dtype), kind="ExternalInput").ap()
    dram["out"] = nc.dram_tensor("out_x", (1, T, D), F32, kind="ExternalOutput").ap()
    with ExitStack() as ctx:
        build(ctx, nc, dram)
    return _run(nc, [arrays], core_ids=[0]).results[0]["out_x"]
```
